# Optimizing a Trainium2 kernel written in Bass

```python
import jax, jax.numpy as jnp
from jax import lax
import numpy as np

D_MODEL = 1024
BATCH = 1
SEQ = 256
DEPTH = 2

GRID_W = 64
QBLOCK = 128
NORM_EPS = 1e-6
ROPE_THETA = 10000.0
NEG_INF = -1e30

MLA_HEADS = 8
MLA_Q_RANK = 384
MLA_KV_RANK = 256
MLA_NOPE = 64
MLA_ROPE = 32
MLA_V = 64

DIL_PAIRS = ((128, 1), (512, 4), (2048, 16))
DIL_HALF = 64
DIL_SLOTS = 4
DIL_GROUPS = len(DIL_PAIRS)
DIL_HEADS = DIL_SLOTS * DIL_GROUPS
DIL_HEAD_DIM = 64

GQA_HEADS = 16
GQA_KV_HEADS = 4
GQA_HEAD_DIM = 64

FFN_HIDDEN = -(-8 * D_MODEL // (3 * 256)) * 256

IN_A = MLA_Q_RANK + MLA_KV_RANK + MLA_ROPE
IN_B = 3 * DIL_HEADS * DIL_HEAD_DIM
MIX_IN = IN_A + IN_B
MIX_OUT = MLA_HEADS * MLA_V + DIL_SLOTS * DIL_HEAD_DIM
N_EVEN = (DEPTH + 1) // 2
N_ODD = DEPTH // 2


def rmsnorm(x, g):
    xf = x.astype(jnp.float32)
    y = xf * lax.rsqrt(jnp.mean(xf * xf, axis=-1, keepdims=True) + NORM_EPS)
    return (y * g.astype(jnp.float32)).astype(x.dtype)

def rope_angles(pos, dim):
    freqs = ROPE_THETA ** (-jnp.arange(0, dim, 2, dtype=jnp.float32) / dim)
    ang = pos.astype(jnp.float32)[:, None] * freqs[None, :]
    return jnp.cos(ang), jnp.sin(ang)

def apply_rope(x, cos, sin):
    xf = x.astype(jnp.float32)
    x1, x2 = jnp.split(xf, 2, axis=-1)
    return jnp.concatenate([x1 * cos - x2 * sin, x1 * sin + x2 * cos], axis=-1).astype(x.dtype)

def blocked_attention(q, k, v, scale):
    b, h, s, dk = q.shape
    g = k.shape[1]
    r = h // g
    nq = s // QBLOCK
    qb = q.reshape(b, g, r, nq, QBLOCK, dk).transpose(3, 0, 1, 2, 4, 5)

    def one_block(qblk):
        sc = jnp.einsum('bgrqd,bgkd->bgrqk', qblk, k, preferred_element_type=jnp.float32) * scale
        p = jax.nn.softmax(sc, axis=-1)
        return jnp.einsum('bgrqk,bgkd->bgrqd', p.astype(v.dtype), v)

    out = lax.map(one_block, qb)
    return out.transpose(1, 2, 3, 0, 4, 5).reshape(b, h, s, -1)

def mla_mixer(h_a, q_norm_g, kv_norm_g, w_uq, w_ukv, cos, sin):
    b, s, _ = h_a.shape
    cq, ckv, k_rope = jnp.split(h_a, [MLA_Q_RANK, MLA_Q_RANK + MLA_KV_RANK], axis=-1)
    cq = rmsnorm(cq, q_norm_g)
    ckv = rmsnorm(ckv, kv_norm_g)
    q = jnp.einsum('bsr,rhd->bhsd', cq, w_uq)
    kv = jnp.einsum('bsr,rhd->bhsd', ckv, w_ukv)
    q_nope, q_rope = q[..., :MLA_NOPE], q[..., MLA_NOPE:]
    k_nope, v = kv[..., :MLA_NOPE], kv[..., MLA_NOPE:]
    q_rope = apply_rope(q_rope, cos, sin)
    k_rope = apply_rope(k_rope, cos, sin)[:, None]
    k_rope = jnp.broadcast_to(k_rope, (b, MLA_HEADS, s, MLA_ROPE))
    qh = jnp.concatenate([q_nope, q_rope], axis=-1)
    kh = jnp.concatenate([k_nope, k_rope], axis=-1)
    o = blocked_attention(qh, kh, v, (MLA_NOPE + MLA_ROPE) ** -0.5)
    return o.transpose(0, 2, 1, 3).reshape(b, s, MLA_HEADS * MLA_V)

def dilated_group_attention(q, k, v, dilation, slopes):
    b, hg, s, dh = q.shape
    P = DIL_HALF
    L = s // dilation
    nb = -(-L // P)
    Lp = nb * P

    def to_residue(t):
        return t.reshape(b, hg, L, dilation, dh).transpose(0, 1, 3, 2, 4)

    qr, kr, vr = to_residue(q), to_residue(k), to_residue(v)
    qb = jnp.pad(qr, ((0, 0), (0, 0), (0, 0), (0, Lp - L), (0, 0))).reshape(b, hg, dilation, nb, P, dh)

    def band(t):
        tb = jnp.pad(t, ((0, 0), (0, 0), (0, 0), (P, Lp - L + P), (0, 0))).reshape(b, hg, dilation, nb + 2, P, dh)
        return jnp.concatenate([tb[:, :, :, :-2], tb[:, :, :, 1:-1], tb[:, :, :, 2:]], axis=4)

    kb, vb = band(kr), band(vr)
    sc = jnp.einsum('bhrnqd,bhrnkd->bhrnqk', qb, kb, preferred_element_type=jnp.float32) * dh ** -0.5

    i = jnp.arange(P)[:, None]
    c = jnp.arange(3 * P)[None, :]
    rel = c - P - i
    uk = jnp.arange(nb)[:, None, None] * P + c - P
    valid = (jnp.abs(rel) <= DIL_HALF)[None] & (uk >= 0) & (uk < L)
    dist = (dilation * jnp.abs(rel)).astype(jnp.float32)
    bias = -slopes.astype(jnp.float32)[:, None, None, None, None] * dist

    sc = jnp.where(valid, sc + bias, NEG_INF)
    m = jnp.max(sc, axis=-1, keepdims=True)
    e = jnp.exp(sc - m)
    den = jnp.sum(e, axis=-1, keepdims=True)
    o = jnp.einsum('bhrnqk,bhrnkd->bhrnqd', (e / den).astype(v.dtype), vb)
    lse = (m + jnp.log(den))[..., 0]

    o = o.reshape(b, hg, dilation, Lp, dh)[:, :, :, :L].transpose(0, 1, 3, 2, 4).reshape(b, hg, s, dh)
    lse = lse.reshape(b, hg, dilation, Lp)[:, :, :, :L].transpose(0, 1, 3, 2).reshape(b, hg, s)
    return o, lse

def dilated_mixer(h_b, slopes):
    b, s, _ = h_b.shape

    def heads(t):
        return t.reshape(b, s, DIL_GROUPS, DIL_SLOTS, DIL_HEAD_DIM).transpose(2, 0, 3, 1, 4)

    q, k, v = (heads(t) for t in jnp.split(h_b, 3, axis=-1))
    outs, lses = [], []
    for g, (_, dil) in enumerate(DIL_PAIRS):
        o, lse = dilated_group_attention(q[g], k[g], v[g], dil, slopes[g * DIL_SLOTS:(g + 1) * DIL_SLOTS])
        outs.append(o)
        lses.append(lse)
    outs = jnp.stack(outs, axis=0)
    wts = jax.nn.softmax(jnp.stack(lses, axis=0), axis=0)
    comb = jnp.sum(wts[..., None] * outs.astype(jnp.float32), axis=0).astype(h_b.dtype)
    return comb.transpose(0, 2, 1, 3).reshape(b, s, DIL_SLOTS * DIL_HEAD_DIM)

def gqa_axial_mixer(hn, w_q, w_kv, q_gain, k_gain, w_o, cos_r, sin_r, cos_c, sin_c):
    b, s, _ = hn.shape
    q = (hn @ w_q).reshape(b, s, GQA_HEADS, GQA_HEAD_DIM).transpose(0, 2, 1, 3)
    kv = (hn @ w_kv).reshape(b, s, 2, GQA_KV_HEADS, GQA_HEAD_DIM)
    k = kv[:, :, 0].transpose(0, 2, 1, 3)
    v = kv[:, :, 1].transpose(0, 2, 1, 3)
    q = rmsnorm(q, q_gain)
    k = rmsnorm(k, k_gain)
    half = GQA_HEAD_DIM // 2

    def axial(t):
        return jnp.concatenate([apply_rope(t[..., :half], cos_r, sin_r),
                                apply_rope(t[..., half:], cos_c, sin_c)], axis=-1)

    o = blocked_attention(axial(q), axial(k), v, GQA_HEAD_DIM ** -0.5)
    return o.transpose(0, 2, 1, 3).reshape(b, s, GQA_HEADS * GQA_HEAD_DIM) @ w_o

def swiglu(hn, w_in, w_out):
    gate, up = jnp.split(hn @ w_in, 2, axis=-1)
    return (jax.nn.silu(gate) * up) @ w_out

def first_inputs(seed: int = 0) -> dict:
    key = jax.random.key(seed)
    ks = jax.random.split(key, 18)
    f32 = jnp.float32

    def w(k, shape, fan_in):
        return jax.random.normal(k, shape, f32) * fan_in ** -0.5

    def gain(k, shape):
        return 1.0 + 0.02 * jax.random.normal(k, shape, f32)

    ne, no = N_EVEN, N_ODD
    return {
        "x": jax.random.normal(ks[0], (BATCH, SEQ, D_MODEL), f32),
        "mix_norm_ab": gain(ks[1], (ne, D_MODEL)),
        "w_in_ab": w(ks[2], (ne, D_MODEL, MIX_IN), D_MODEL),
        "mla_q_norm": gain(ks[3], (ne, MLA_Q_RANK)),
        "mla_kv_norm": gain(ks[4], (ne, MLA_KV_RANK)),
        "mla_w_uq": w(ks[5], (ne, MLA_Q_RANK, MLA_HEADS, MLA_NOPE + MLA_ROPE), MLA_Q_RANK),
        "mla_w_ukv": w(ks[6], (ne, MLA_KV_RANK, MLA_HEADS, MLA_NOPE + MLA_V), MLA_KV_RANK),
        "w_out_ab": w(ks[7], (ne, MIX_OUT, D_MODEL), MIX_OUT),
        "mix_norm_c": gain(ks[8], (no, D_MODEL)),
        "gqa_w_q": w(ks[9], (no, D_MODEL, GQA_HEADS * GQA_HEAD_DIM), D_MODEL),
        "gqa_w_kv": w(ks[10], (no, D_MODEL, 2 * GQA_KV_HEADS * GQA_HEAD_DIM), D_MODEL),
        "gqa_q_norm": gain(ks[11], (no, GQA_HEAD_DIM)),
        "gqa_k_norm": gain(ks[12], (no, GQA_HEAD_DIM)),
        "gqa_w_o": w(ks[13], (no, GQA_HEADS * GQA_HEAD_DIM, D_MODEL), GQA_HEADS * GQA_HEAD_DIM),
        "ffn_norm": gain(ks[14], (DEPTH, D_MODEL)),
        "ffn_w_in": w(ks[15], (DEPTH, D_MODEL, 2 * FFN_HIDDEN), D_MODEL),
        "ffn_w_out": w(ks[16], (DEPTH, FFN_HIDDEN, D_MODEL), FFN_HIDDEN),
        "final_norm": gain(ks[17], (D_MODEL,)),
    }

def first_block(x, mix_norm_ab, w_in_ab, mla_q_norm, mla_kv_norm, mla_w_uq, mla_w_ukv, w_out_ab,
              mix_norm_c, gqa_w_q, gqa_w_kv, gqa_q_norm, gqa_k_norm, gqa_w_o,
              ffn_norm, ffn_w_in, ffn_w_out, final_norm):
    s = x.shape[1]
    rows = s // GRID_W
    pos = jnp.arange(s)
    cos_t, sin_t = rope_angles(pos, MLA_ROPE)
    row_idx = jnp.broadcast_to(jnp.arange(rows)[:, None], (rows, GRID_W)).reshape(-1)
    col_idx = jnp.broadcast_to(jnp.arange(GRID_W)[None, :], (rows, GRID_W)).reshape(-1)
    cos_r, sin_r = rope_angles(row_idx, GQA_HEAD_DIM // 2)
    cos_c, sin_c = rope_angles(col_idx, GQA_HEAD_DIM // 2)
    slopes = jnp.exp2(-8.0 * jnp.arange(1, DIL_HEADS + 1, dtype=jnp.float32) / DIL_HEADS)

    for layer in range(DEPTH):
        i = layer // 2
        if layer % 2 == 0:
            z = rmsnorm(x, mix_norm_ab[i]) @ w_in_ab[i]
            o_a = mla_mixer(z[..., :IN_A], mla_q_norm[i], mla_kv_norm[i], mla_w_uq[i], mla_w_ukv[i],
                            cos_t, sin_t)
            o_b = dilated_mixer(z[..., IN_A:], slopes)
            x = x + jnp.concatenate([o_a, o_b], axis=-1) @ w_out_ab[i]
        else:
            x = x + gqa_axial_mixer(rmsnorm(x, mix_norm_c[i]), gqa_w_q[i], gqa_w_kv[i], gqa_q_norm[i],
                                    gqa_k_norm[i], gqa_w_o[i], cos_r, sin_r, cos_c, sin_c)
        x = x + swiglu(rmsnorm(x, ffn_norm[layer]), ffn_w_in[layer], ffn_w_out[layer])
    return rmsnorm(x, final_norm)


D_FF = 2816
FFN_RES_WEIGHT = 0.5
GM_WIDTH = 512
GM_GROUPS = 4
GM_CHUNK = 128
RET_HEADS = 4
RET_DK = 64
RET_DV = 128
RET_CHUNK = 128
NSA_HEADS = 8
NSA_KV = 2
NSA_REP = NSA_HEADS // NSA_KV
NSA_DH = 64
CMP_LEN = 32
CMP_STRIDE = 16
CMP_HIDDEN = 128
SLC_BLOCK = 64
N_SELECT = 16
WINDOW = 512
Q_BLOCK = 128
N_NSA_BRANCH = 3
N_MIXERS = 3
MIX_WIDTH = 512
IN_SPLITS = (GM_WIDTH, GM_WIDTH, RET_HEADS * RET_DK, RET_HEADS * RET_DK, RET_HEADS * RET_DV, RET_HEADS * RET_DV, NSA_HEADS * NSA_DH, 6 * NSA_KV * NSA_DH, N_NSA_BRANCH * NSA_HEADS)
D_IN = sum(IN_SPLITS)
BIG = 1e9
NEG = -1e30


def rms_norm(x, g):
    xf = x.astype(jnp.float32)
    y = xf * lax.rsqrt(jnp.mean(xf * xf, axis=-1, keepdims=True) + NORM_EPS)
    return (y * g.astype(jnp.float32)).astype(x.dtype)

def layer_norm(x, g, b):
    xf = x.astype(jnp.float32)
    mu = jnp.mean(xf, axis=-1, keepdims=True)
    xc = xf - mu
    var = jnp.mean(xc * xc, axis=-1, keepdims=True)
    y = xc * lax.rsqrt(var + NORM_EPS) * g.astype(jnp.float32) + b.astype(jnp.float32)
    return y.astype(x.dtype)

def swiglu_ffn(x, w1, w2):
    a, b = jnp.split(x @ w1, 2, axis=-1)
    return (jax.nn.silu(a) * b) @ w2

def masked_softmax(s, mask):
    s = jnp.where(mask, s.astype(jnp.float32), NEG)
    m = jnp.max(s, axis=-1, keepdims=True)
    e = jnp.where(mask, jnp.exp(s - m), 0.0)
    return e / jnp.maximum(jnp.sum(e, axis=-1, keepdims=True), 1e-30)

def alibi_slopes():
    h = jnp.arange(1, NSA_HEADS + 1, dtype=jnp.float32)
    return (2.0 ** (-8.0 * h / NSA_HEADS)).reshape(NSA_KV, NSA_REP)

def gmlp_mixer(u, v, ln_g, ln_b, ws, bs):
    bsz, s, _ = u.shape
    nc = s // GM_CHUNK
    cg = GM_WIDTH // GM_GROUPS
    v = layer_norm(v, ln_g, ln_b).reshape(bsz, nc, GM_CHUNK, GM_GROUPS, cg)
    causal = jnp.tril(jnp.ones((GM_CHUNK, GM_CHUNK), dtype=bool))
    w = jnp.where(causal[None], ws, 0.0)
    sv = jnp.einsum('gts,bnsgc->bntgc', w, v) + jnp.transpose(bs)[None, None, :, :, None]
    return u * sv.reshape(bsz, s, GM_WIDTH)

def retention_mixer(q, k, v, g, gn_g, gn_b):
    f32 = jnp.float32
    bsz, s, _ = q.shape
    nc = s // RET_CHUNK
    q = q.reshape(bsz, nc, RET_CHUNK, RET_HEADS, RET_DK).astype(f32)
    k = (k.reshape(bsz, nc, RET_CHUNK, RET_HEADS, RET_DK) * RET_DK ** -0.5).astype(f32)
    v = v.reshape(bsz, nc, RET_CHUNK, RET_HEADS, RET_DV).astype(f32)
    log_gamma = jnp.log(1.0 - 2.0 ** (-5.0 - jnp.arange(RET_HEADS, dtype=f32)))
    pos = jnp.arange(RET_CHUNK, dtype=f32)
    diff = pos[:, None] - pos[None, :]
    intra_decay = jnp.where(diff >= 0, jnp.exp(log_gamma[:, None, None] * jnp.maximum(diff, 0.0)), 0.0)
    scores = jnp.einsum('bnihd,bnjhd->bnhij', q, k) * intra_decay
    intra = jnp.einsum('bnhij,bnjhe->bnihe', scores, v)
    k_decay = jnp.exp(log_gamma[None, :] * (RET_CHUNK - 1.0 - pos)[:, None])
    kv = jnp.einsum('bnjhd,jh,bnjhe->nbhde', k, k_decay, v)
    chunk_decay = jnp.exp(log_gamma * RET_CHUNK)[None, :, None, None]

    def step(state, kv_c):
        return state * chunk_decay + kv_c, state

    _, prev = lax.scan(step, jnp.zeros((bsz, RET_HEADS, RET_DK, RET_DV), f32), kv)
    q_decay = jnp.exp(log_gamma[None, :] * (pos + 1.0)[:, None])
    cross = jnp.einsum('bnihd,nbhde->bnihe', q, prev) * q_decay[None, None, :, :, None]
    y = layer_norm(intra + cross, gn_g.reshape(RET_HEADS, RET_DV), gn_b.reshape(RET_HEADS, RET_DV))
    return jax.nn.silu(g.astype(f32)) * y.reshape(bsz, s, RET_HEADS * RET_DV)

def nsa_mixer(q, kv, gate_logits, cmp_pos, cmp_w1, cmp_w2):
    f32 = jnp.float32
    bsz, s, _ = q.shape
    n_cmp = s // CMP_STRIDE - 1
    n_slc = s // SLC_BLOCK
    n_sel = min(N_SELECT, n_slc)
    q = q.reshape(bsz, s, NSA_KV, NSA_REP, NSA_DH) * NSA_DH ** -0.5
    k_c, v_c, k_s, v_s, k_w, v_w = [t.reshape(bsz, s, NSA_KV, NSA_DH) for t in jnp.split(kv, 6, axis=-1)]

    def compress(t, pos, w1, w2):
        seg = t.reshape(bsz, s // CMP_STRIDE, CMP_STRIDE, NSA_KV, NSA_DH)
        blocks = jnp.concatenate([seg[:, :-1], seg[:, 1:]], axis=2) + pos[None, None, :, None, :]
        flat = jnp.transpose(blocks, (0, 1, 3, 2, 4)).reshape(bsz, n_cmp, NSA_KV, CMP_LEN * NSA_DH)
        return jax.nn.gelu(flat @ w1) @ w2

    kc = compress(k_c, cmp_pos[0], cmp_w1[0], cmp_w2[0])
    vc = compress(v_c, cmp_pos[1], cmp_w1[1], cmp_w2[1])
    cmp_end = jnp.arange(n_cmp) * CMP_STRIDE + CMP_LEN - 1
    ci = jnp.arange(n_cmp)
    sj = jnp.arange(n_slc)
    overlap = ((ci[:, None] * CMP_STRIDE < (sj[None, :] + 1) * SLC_BLOCK) & (ci[:, None] * CMP_STRIDE + CMP_LEN > sj[None, :] * SLC_BLOCK)).astype(f32)
    ks_blocks = jnp.transpose(k_s.reshape(bsz, n_slc, SLC_BLOCK, NSA_KV, NSA_DH), (0, 3, 1, 2, 4))
    vs_blocks = jnp.transpose(v_s.reshape(bsz, n_slc, SLC_BLOCK, NSA_KV, NSA_DH), (0, 3, 1, 2, 4))
    kw_pad = jnp.pad(k_w, ((0, 0), (WINDOW, 0), (0, 0), (0, 0)))
    vw_pad = jnp.pad(v_w, ((0, 0), (WINDOW, 0), (0, 0), (0, 0)))
    gates = jax.nn.sigmoid(gate_logits.astype(f32)).reshape(bsz, s, NSA_KV, NSA_REP, N_NSA_BRANCH)
    slopes = alibi_slopes()
    bi = jnp.arange(bsz)[:, None, None, None]
    gi = jnp.arange(NSA_KV)[None, :, None, None]

    def block_fn(qb):
        t0 = qb * Q_BLOCK
        qblk = lax.dynamic_slice_in_dim(q, t0, Q_BLOCK, axis=1)
        tpos = t0 + jnp.arange(Q_BLOCK)
        s_c = jnp.einsum('bqgrd,bngd->bgrqn', qblk, kc)
        dist_c = tpos[:, None] - cmp_end[None, :]
        s_c = s_c - slopes[None, :, :, None, None] * dist_c.astype(f32)
        p_c = masked_softmax(s_c, dist_c >= 0)
        o_c = jnp.einsum('bgrqn,bngd->bqgrd', p_c, vc)
        imp = jnp.einsum('bgrqn,nj->bgqj', p_c, overlap)
        cur = tpos // SLC_BLOCK
        jj = sj[None, :]
        forced = (jj == 0) | (jj == cur[:, None]) | (jj == cur[:, None] - 1)
        imp = jnp.where(forced, BIG, imp)
        imp = jnp.where(jj > cur[:, None], -BIG, imp)
        _, sel = lax.top_k(imp, n_sel)
        ks = ks_blocks[bi, gi, sel]
        vs = vs_blocks[bi, gi, sel]
        s_s = jnp.einsum('bqgrd,bgqnkd->bgrqnk', qblk, ks)
        kpos = sel[..., None] * SLC_BLOCK + jnp.arange(SLC_BLOCK)
        dist_s = (tpos[None, None, :, None, None] - kpos)[:, :, None]
        s_s = s_s - slopes[None, :, :, None, None, None] * dist_s.astype(f32)
        m_tot = n_sel * SLC_BLOCK
        p_s = masked_softmax(s_s.reshape(bsz, NSA_KV, NSA_REP, Q_BLOCK, m_tot), (dist_s >= 0).reshape(bsz, NSA_KV, 1, Q_BLOCK, m_tot))
        o_s = jnp.einsum('bgrqm,bgqmd->bqgrd', p_s, vs.reshape(bsz, NSA_KV, Q_BLOCK, m_tot, NSA_DH))
        kw = lax.dynamic_slice_in_dim(kw_pad, t0, Q_BLOCK + WINDOW, axis=1)
        vw = lax.dynamic_slice_in_dim(vw_pad, t0, Q_BLOCK + WINDOW, axis=1)
        wpos = t0 - WINDOW + jnp.arange(Q_BLOCK + WINDOW)
        dist_w = tpos[:, None] - wpos[None, :]
        mask_w = (dist_w >= 0) & (dist_w < WINDOW) & (wpos[None, :] >= 0)
        s_w = jnp.einsum('bqgrd,bkgd->bgrqk', qblk, kw) - slopes[None, :, :, None, None] * dist_w.astype(f32)
        p_w = masked_softmax(s_w, mask_w)
        o_w = jnp.einsum('bgrqk,bkgd->bqgrd', p_w, vw)
        g = lax.dynamic_slice_in_dim(gates, t0, Q_BLOCK, axis=1)
        return g[..., 0:1] * o_c + g[..., 1:2] * o_s + g[..., 2:3] * o_w

    out = lax.map(block_fn, jnp.arange(s // Q_BLOCK))
    return jnp.transpose(out, (1, 0, 2, 3, 4, 5)).reshape(bsz, s, NSA_HEADS * NSA_DH)

def second_inputs(seed: int = 0) -> dict:
    key = jax.random.key(seed)
    ks = jax.random.split(key, 24)
    L = DEPTH
    f32 = jnp.float32

    def nrm(k, shape, scale):
        return jax.random.normal(k, shape, f32) * scale

    def gain(k, shape):
        return 1.0 + 0.02 * jax.random.normal(k, shape, f32)

    return {
        'x': nrm(ks[0], (BATCH, SEQ, D_MODEL), 1.0),
        'ffn1_norm': gain(ks[1], (L, D_MODEL)),
        'ffn1_w1': nrm(ks[2], (L, D_MODEL, 2 * D_FF), D_MODEL ** -0.5),
        'ffn1_w2': nrm(ks[3], (L, D_FF, D_MODEL), D_FF ** -0.5),
        'mix_norm': gain(ks[4], (L, D_MODEL)),
        'w_in': nrm(ks[5], (L, D_MODEL, D_IN), D_MODEL ** -0.5),
        'gm_ln_g': gain(ks[6], (L, GM_WIDTH)),
        'gm_ln_b': nrm(ks[7], (L, GM_WIDTH), 0.02),
        'gm_ws': nrm(ks[8], (L, GM_GROUPS, GM_CHUNK, GM_CHUNK), GM_CHUNK ** -0.5),
        'gm_bs': gain(ks[9], (L, GM_GROUPS, GM_CHUNK)),
        'ret_gn_g': gain(ks[10], (L, RET_HEADS * RET_DV)),
        'ret_gn_b': nrm(ks[11], (L, RET_HEADS * RET_DV), 0.02),
        'cmp_pos': nrm(ks[12], (L, 2, CMP_LEN, NSA_DH), 0.02),
        'cmp_w1': nrm(ks[13], (L, 2, CMP_LEN * NSA_DH, CMP_HIDDEN), (CMP_LEN * NSA_DH) ** -0.5),
        'cmp_w2': nrm(ks[14], (L, 2, CMP_HIDDEN, NSA_DH), CMP_HIDDEN ** -0.5),
        'w_branch_out': nrm(ks[15], (L, N_MIXERS, MIX_WIDTH, D_MODEL), MIX_WIDTH ** -0.5),
        'w_merge_gate': nrm(ks[16], (L, D_MODEL, N_MIXERS * D_MODEL), D_MODEL ** -0.5),
        'b_merge_gate': nrm(ks[17], (L, N_MIXERS * D_MODEL), 0.02),
        'w_o': nrm(ks[18], (L, D_MODEL, D_MODEL), D_MODEL ** -0.5),
        'ffn2_norm': gain(ks[19], (L, D_MODEL)),
        'ffn2_w1': nrm(ks[20], (L, D_MODEL, 2 * D_FF), D_MODEL ** -0.5),
        'ffn2_w2': nrm(ks[21], (L, D_FF, D_MODEL), D_FF ** -0.5),
        'final_norm': gain(ks[22], (D_MODEL,)),
    }

def second_block(x, ffn1_norm, ffn1_w1, ffn1_w2, mix_norm, w_in, gm_ln_g, gm_ln_b, gm_ws, gm_bs, ret_gn_g, ret_gn_b, cmp_pos, cmp_w1, cmp_w2, w_branch_out, w_merge_gate, b_merge_gate, w_o, ffn2_norm, ffn2_w1, ffn2_w2, final_norm):
    splits = np.cumsum(IN_SPLITS)[:-1].tolist()
    for l in range(DEPTH):
        x = x + FFN_RES_WEIGHT * swiglu_ffn(rms_norm(x, ffn1_norm[l]), ffn1_w1[l], ffn1_w2[l])
        h = rms_norm(x, mix_norm[l])
        proj = h @ w_in[l]
        gm_u, gm_v, r_q, r_k, r_v, r_g, n_q, n_kv, n_g = jnp.split(proj, splits, axis=-1)
        y_a = gmlp_mixer(jax.nn.gelu(gm_u), jax.nn.gelu(gm_v), gm_ln_g[l], gm_ln_b[l], gm_ws[l], gm_bs[l])
        y_b = retention_mixer(r_q, r_k, r_v, r_g, ret_gn_g[l], ret_gn_b[l])
        y_c = nsa_mixer(n_q, n_kv, n_g, cmp_pos[l], cmp_w1[l], cmp_w2[l])
        g_a, g_b, g_c = jnp.split(jax.nn.sigmoid(h @ w_merge_gate[l] + b_merge_gate[l]), N_MIXERS, axis=-1)
        mix = g_a * (y_a @ w_branch_out[l, 0]) + g_b * (y_b @ w_branch_out[l, 1]) + g_c * (y_c @ w_branch_out[l, 2])
        x = x + mix @ w_o[l]
        x = x + FFN_RES_WEIGHT * swiglu_ffn(rms_norm(x, ffn2_norm[l]), ffn2_w1[l], ffn2_w2[l])
    return rms_norm(x, final_norm)


_first_inputs = second_inputs


def second_inputs(seed=0):
    import zlib

    import numpy as np

    out = dict(_first_inputs(seed))
    spreads = {}
    factors = {'ffn1_norm': 3.956,
     'gm_ln_g': 8.0,
     'gm_ln_b': 8.0,
     'gm_bs': 6.486,
     'ret_gn_g': 7.105,
     'ret_gn_b': 7.002,
     'cmp_pos': 8.0,
     'b_merge_gate': 8.0,
     'ffn2_norm': 5.644,
     'final_norm': 2.827}
    for name, (base, spread) in spreads.items():
        noise = np.random.default_rng([zlib.crc32(name.encode()), seed]).standard_normal(out[name].shape)
        drawn = base * np.exp(spread * noise) if base else spread * noise
        out[name] = __import__('jax').numpy.asarray(drawn.astype(out[name].dtype))
    for name, factor in factors.items():
        out[name] = (out[name] * factor).astype(out[name].dtype)
    return out


_narrow_inputs = second_inputs


def second_inputs(seed=0):

    out = dict(_narrow_inputs(seed))
    wider = {'gm_ln_g': 5.86,
     'gm_ln_b': 5.87,
     'gm_bs': 5.08,
     'ret_gn_g': 5.19,
     'ret_gn_b': 5.14,
     'cmp_pos': 9.32,
     'final_norm': 3.18}
    for name, times in wider.items():
        mean = out[name].mean()
        out[name] = (mean + times * (out[name] - mean)).astype(out[name].dtype)
    return out


def setup_inputs(seed=0):
    out = dict(first_inputs(seed))
    for name, value in second_inputs(seed + 1).items():
        if name != "x":
            out[name + "_2"] = value
    return out


def reference(
    x, mix_norm_ab, w_in_ab, mla_q_norm, mla_kv_norm, mla_w_uq, mla_w_ukv, w_out_ab, mix_norm_c,
    gqa_w_q, gqa_w_kv, gqa_q_norm, gqa_k_norm, gqa_w_o, ffn_norm, ffn_w_in, ffn_w_out,
    final_norm, ffn1_norm_2, ffn1_w1_2, ffn1_w2_2, mix_norm_2, w_in_2, gm_ln_g_2, gm_ln_b_2,
    gm_ws_2, gm_bs_2, ret_gn_g_2, ret_gn_b_2, cmp_pos_2, cmp_w1_2, cmp_w2_2, w_branch_out_2,
    w_merge_gate_2, b_merge_gate_2, w_o_2, ffn2_norm_2, ffn2_w1_2, ffn2_w2_2, final_norm_2,
):
    x = first_block(
        x, mix_norm_ab, w_in_ab, mla_q_norm, mla_kv_norm, mla_w_uq, mla_w_ukv, w_out_ab,
        mix_norm_c, gqa_w_q, gqa_w_kv, gqa_q_norm, gqa_k_norm, gqa_w_o, ffn_norm, ffn_w_in,
        ffn_w_out, final_norm,
    )
    return second_block(
        x, ffn1_norm_2, ffn1_w1_2, ffn1_w2_2, mix_norm_2, w_in_2, gm_ln_g_2, gm_ln_b_2, gm_ws_2,
        gm_bs_2, ret_gn_g_2, ret_gn_b_2, cmp_pos_2, cmp_w1_2, cmp_w2_2, w_branch_out_2,
        w_merge_gate_2, b_merge_gate_2, w_o_2, ffn2_norm_2, ffn2_w1_2, ffn2_w2_2, final_norm_2,
    )


_drawn_inputs = setup_inputs


def setup_inputs(seed=0):
    import zlib

    import numpy as np

    out = dict(_drawn_inputs(seed))
    spreads = {}
    factors = {'mla_q_norm': 8.0,
     'mla_kv_norm': 5.252,
     'mix_norm_c': 5.724,
     'gqa_q_norm': 8.0,
     'gqa_k_norm': 8.0}
    for name, (base, spread) in spreads.items():
        noise = np.random.default_rng([zlib.crc32(name.encode()), seed]).standard_normal(out[name].shape)
        drawn = base * np.exp(spread * noise) if base else spread * noise
        out[name] = __import__('jax').numpy.asarray(drawn.astype(out[name].dtype))
    for name, factor in factors.items():
        out[name] = (out[name] * factor).astype(out[name].dtype)
    return out
```

```python
from contextlib import ExitStack

import concourse.bass as bass
import numpy as np
from concourse import mybir

F32 = mybir.dt.float32
F32R = mybir.dt.float32r
ALU = mybir.AluOpType
ACT = mybir.ActivationFunctionType
AX_X = mybir.AxisListType.X

P = 128
S = 256
D = 1024
M = S // P
KC = D // P
TILE = 2048
EPS = 1e-6
NEG = -1e30
H1, DK1, ROPE1 = 8, 96, 32
RQ, RKV = 384, 256
DG, DS = 3, 4
H2, G2 = 16, 4
FF = 2816
NF = FF // P
FFN_TILES = NF + NF // 2
SLOT_HEADS = (0, 2, 1, 3)
HN, NCMP = 8, 15
HR = 4
LAYERS = 2


class Plan:

    def __init__(self):
        self.tile, self.step, self.act, self.dve, self.tb = {}, {}, {}, {}, {}
        self.tiles = 0
        self.last_step = []
        self.drains = []
        self.copies = []

    def weights(self, name, drains, steps_per_tile=1):
        self.tile[name], self.step[name] = self.tiles, len(self.drains)
        for i, who in enumerate(drains):
            if i % steps_per_tile == 0:
                self.tiles += 1
                self.last_step.append(len(self.drains))
            self.last_step[-1] = len(self.drains)
            self.drains.append(who)

    def batches(self, name, who):
        self.tb[name] = len(self.copies)
        self.copies += who


def ffn_drains():
    return "DD" + "DD-" * (NF // 2 - 1) + "-"


PLAN1 = Plan()
PLAN1.batches("n0", "BBBB")
PLAN1.weights("z", "A" * 12)
PLAN1.batches("cq", "BBB")
PLAN1.weights("uq", "DDD", 2)
PLAN1.weights("ukv", "AAAA", 4)
PLAN1.batches("mqk", "ADADADAD")
PLAN1.batches("mla", "ADADADAD")
PLAN1.batches("dil", "ADADADADADAD")
PLAN1.batches("ocat", "BBB")
PLAN1.weights("wout", "DDDD")
PLAN1.batches("n1", "BBBB")
PLAN1.weights("f0", ffn_drains())
PLAN1.batches("n2", "BBBB")
PLAN1.weights("gqkv", "AAAAAA")
PLAN1.batches("gqk", "ADADA")
PLAN1.batches("gqa", "ADADADADADADADAD")
PLAN1.batches("go", "BBBB")
PLAN1.weights("gwo", "DDDD")
PLAN1.batches("n3", "BBBB")
PLAN1.weights("f1", ffn_drains())

PLAN2 = Plan()
PLAN2.batches("n4", "BBBB")
PLAN2.weights("fa", ffn_drains())
PLAN2.batches("n5", "BBBB")
WIN_DRAINS = "DDAAAADDAAAADDDDA"
PLAN2.weights("win", WIN_DRAINS)
PLAN2.batches("cmp", "AD")
PLAN2.weights("gates", "D" * 12)
PLAN2.batches("nsa", "ADADADADADAD")
PLAN2.batches("y", "BBBBBB")
PLAN2.weights("branch", "D" * 12, 2)
PLAN2.batches("mix", "BBBB")
PLAN2.weights("wo", "DDDD")
PLAN2.batches("n6", "BBBB")
PLAN2.weights("fb", ffn_drains())
TILES = PLAN1.tiles + LAYERS * PLAN2.tiles + 2
assert PLAN2.tiles % 3 == 0 and len(PLAN2.copies) % 2 == 0


class Numbers:

    def __init__(self, l=None):
        self.l = l
        self.plan = PLAN1 if l is None else PLAN2
        p1, p2 = PLAN1, PLAN2
        k = 0 if l is None else l

        def base(a, b):
            return 0 if l is None else a + b * k

        self.tile0_third = base(p1.tiles // 3, p2.tiles // 3)
        self.tile0_slot = 0 if l is None else p1.tiles % 3
        self.step0 = base(len(p1.drains), len(p2.drains))
        self.act0 = base(p1.drains.count("A"), p2.drains.count("A"))
        self.dve0 = base(p1.drains.count("D"), p2.drains.count("D"))
        self.tb0 = base(len(p1.copies), len(p2.copies))
        self.tb0_parity = 0 if l is None else len(p1.copies) % 2
        self.tb_act0 = base(len(p1.copies) - p1.copies.count("D"), len(p2.copies) - p2.copies.count("D"))
        self.tb_dve0 = base(len(p1.copies) - p1.copies.count("A"), len(p2.copies) - p2.copies.count("A"))

    def slot(self, tile):
        return (self.tile0_slot + tile) % 3

    def landed(self, tile, thirds=0):
        return 16 * (self.tile0_third + (self.tile0_slot + tile) // 3 + thirds + 1)

    def tile_no(self, tile, thirds=0):
        return 3 * (self.tile0_third + thirds) + self.tile0_slot + tile

    def last_step(self, tile):
        if tile < 0:
            return tile
        return self.plan.last_step[tile] if tile < self.plan.tiles else len(self.plan.drains) + tile - self.plan.tiles

    def drained(self, step, who):
        n = "".join(self.plan.drains)[:max(step, 0)].count(who)
        return (self.act0 if who == "A" else self.dve0) + n

    def copied(self, tb, who):
        other = "D" if who == "A" else "A"
        copies = self.plan.copies
        if tb < 0:
            return (self.tb_act0 if who == "A" else self.tb_dve0) + tb
        return (self.tb_act0 if who == "A" else self.tb_dve0) + sum(c != other for c in copies[:tb])

    def bank(self, tb):
        return 6 + (self.tb0_parity + tb) % 2


AG_MLA, AG_DIL, AG_GQA, AG_NSA = 0, 4, 10, 18



def tables():
    f32 = np.float32
    t = np.arange(S)

    def rope(pos, dim):
        freqs = (f32(10000.0) ** (-np.arange(0, dim, 2, dtype=f32) / f32(dim))).astype(f32)
        ang = (pos.astype(f32)[:, None] * freqs[None, :]).astype(f32)
        return np.cos(ang).astype(f32), np.sin(ang).astype(f32)

    def halves(a):
        return np.swapaxes(a.reshape(M, P, *a.shape[1:]), 0, 1)

    c, s = rope(t, ROPE1)
    cr, sr = rope(t // 64, 32)
    cc, sc = rope(t % 64, 32)
    gc, gs = np.stack([cr, cc], 1), np.stack([sr, sc], 1)
    misc = np.concatenate([np.eye(P, dtype=f32), halves(c).reshape(P, -1), halves(s).reshape(P, -1),
                           halves(gc).reshape(P, -1), halves(gs).reshape(P, -1)], 1)

    q = np.arange(P)[:, None]
    k = np.arange(3 * P)[None, :] - P
    slopes = np.exp2(f32(-8.0) * np.arange(1, 13, dtype=f32) / f32(12))
    dil = np.empty((P, 12, 3 * P), f32)
    for i in range(12):
        h = i // 4 * 4 + SLOT_HEADS[i % 4]
        d = (1, 4, 16)[h // 4]
        dist = np.abs(k - q)
        ok = (dist % d == 0) & (dist <= 64 * d)
        dil[:, i] = np.where(ok, -slopes[h] * dist.astype(f32), f32(NEG))

    sl = (f32(2.0) ** (f32(-8.0) * np.arange(1, 9, dtype=f32) / f32(8))).astype(f32)
    k = np.arange(2 * P)[None, :] - P
    nsa = np.empty((P, 8, 2 * P), f32)
    for h in range(8):
        dist = q - k
        nsa[:, h] = np.where(dist >= 0, -sl[h] * dist.astype(f32), f32(NEG))
    end = np.arange(NCMP) * 16 + 31
    dist = t[:, None, None] - end[None, None, :]
    cb = np.where(dist >= 0, -sl[None, :, None] * dist.astype(f32), f32(NEG)).astype(f32)
    cb = halves(cb).reshape(P, -1)
    log_gamma = np.log(1.0 - 2.0 ** (-5.0 - np.arange(HR)))
    j = np.arange(P)[:, None]
    i = np.arange(2 * P)[None, :]
    ret = np.stack([np.where(i >= j, np.exp(g * np.maximum(i - j, 0)), 0.0) for g in log_gamma], 1).astype(f32)
    block = np.zeros((P, HN), f32)
    for h in range(HN):
        block[h * NCMP:(h + 1) * NCMP, h] = 1.0
    tril_t = np.triu(np.ones((P, P), f32))
    second = np.concatenate([nsa.reshape(P, -1), ret.reshape(P, -1), cb, block, tril_t], 1)
    return misc, dil.reshape(P, -1), second


def build(nc, stream, xin, misc, dilb, second, gains, mlag, small, rows, out):
    ctx = ExitStack()
    with ctx:
        base = [16896]

        def at(name, off, cols, dt=F32, shape=None):
            t = nc.alloc_sbuf_tensor_at(name, [P, cols], dt, offset=base[0] + off)
            a = t[:, :]
            if shape:
                names = "abcdef"[:len(shape)]
                a = a.rearrange(f"p ({' '.join(names)}) -> p {' '.join(names)}", **dict(zip(names, shape)))
            return a

        K = 1024
        ctx.enter_context(nc.sbuf_tensor("fence", [P, 207 * 256], F32))
        raw = [at(f"raw{i}", 8 * K * i, TILE) for i in range(3)]
        whi = [at(f"whi{i}", 24 * K + 8 * K * i, TILE, F32R) for i in range(3)]
        wlo = [at(f"wlo{i}", 48 * K + 8 * K * i, TILE, F32R) for i in range(3)]
        x = at("x", 72 * K, M * D, shape=(M, D))
        y = at("y", 80 * K, M * D, shape=(M, D))
        yh = at("yh", 88 * K, KC * S, F32R, (KC, S))
        yl = at("yl", 96 * K, KC * S, F32R, (KC, S))
        gbc = at("gbc", 104 * K, D)
        CM = 108 * K
        misc_sb = at("misc", CM, 128 + 64 + 128)
        ident = misc_sb[:, 0:128]
        cos1 = misc_sb[:, 128:160].rearrange("p (m f) -> p m f", m=M)
        sin1 = misc_sb[:, 160:192].rearrange("p (m f) -> p m f", m=M)
        cos2 = misc_sb[:, 192:256].rearrange("p (m a f) -> p m a f", m=M, a=2)
        sin2 = misc_sb[:, 256:320].rearrange("p (m a f) -> p m a f", m=M, a=2)
        off = [CM + 1280]

        def little(name, cols, shape=None):
            a = at(name, off[0], cols, F32, shape)
            off[0] += -(-cols * 4 // 32) * 32
            assert off[0] <= 111 * K
            return a

        ss = little("ss", 2)
        ms = little("ms", 24)
        rstd = little("rstd", 24)
        half = little("half", 24)
        mx = little("mx", 8, (2, 4))
        nmx = little("nmx", 8, (2, 4))
        den = little("den", 16, (4, 4))
        rec = little("rec", 4)
        st = little("st", 8 * 6, (8, 6))
        mv = little("mv", 8 * 2, (8, 2))
        A = 111 * K
        dbias = at("dbias", A, 12 * 384, shape=(12, 384))
        zA = at("zA", A + 18 * K, M * 672, shape=(M, 672))
        dqk = at("dqk", A + 24 * K, 12 * S, shape=(12, S))
        dv = at("dv", A + 36 * K, M * 768, shape=(M, 768))
        kvTh = at("kvTh", A + 42 * K, 2 * S, F32R, (2, S))
        kvTl = at("kvTl", A + 44 * K, 2 * S, F32R, (2, S))
        cqTh = at("cqTh", 80 * K, 3 * S, F32R, (3, S))
        cqTl = at("cqTl", 83 * K, 3 * S, F32R, (3, S))
        mq = at("mq", A + 46 * K, M * 768, shape=(M, H1, DK1))
        mkv = at("mkv", A + 52 * K, M * 1024, shape=(M, H1, 128))
        kasm = at("kasm", A + 60 * K, M * 768, shape=(M, H1, DK1))
        mqT = at("mqT", A + 66 * K, H1 * S, shape=(H1, S))
        mkT = at("mkT", A + 74 * K, H1 * S, shape=(H1, S))
        kr = at("kr", A + 94 * K, M * 32, shape=(M, 32))
        rt = at("rt", A + 82 * K, 4 * 256, shape=(4, 256))
        mlagain = at("mlagain", A + 90 * K, 640)
        P0 = [at(f"p0_{i}", A + 82 * K + 4 * K * i, 1024, shape=(4, S)) for i in range(2)]
        PT0 = [at(f"pt0_{i}", A + 42 * K + 4 * K * i, 1024, shape=(4, M, P)) for i in range(2)]
        ocat = at("ocat", A + 60 * K, M * 768, shape=(M, 768))
        og = at("og", A + 18 * K, M * DG * 256, shape=(M, DG, 4, 64))
        mxd = at("mxd", A + 93 * K, M * DG * 4, shape=(M, DG, 4))
        dend = at("dend", A + 93 * K + 128, M * DG * 4, shape=(M, DG, 4))
        wd = at("wd", A + 93 * K + 256, M * DG * 4, shape=(M, DG, 4))
        bigm = at("bigm", A + 93 * K + 384, M * 4, shape=(M, 4))
        oTh = at("oTh", 88 * K, 6 * S, F32R, (6, S))
        oTl = at("oTl", 96 * K, 6 * S, F32R, (6, S))
        gqkv = at("gqkv", A, M * 1536, shape=(M, 1536))
        gsq = at("gsq", A + 12 * K, M * 1280, shape=(M, 1280))
        gr = at("gr", A + 22 * K, M * 1280, shape=(M, 1280))
        gqT = at("gqT", A + 32 * K, 8 * S, shape=(8, S))
        gkT = at("gkT", A + 40 * K, 2 * S, shape=(2, S))
        P1 = [at(f"p1_{i}", A + 42 * K + 4 * K * i, 1024, shape=(4, S)) for i in range(2)]
        PT1 = [at(f"pt1_{i}", A + 50 * K + 4 * K * i, 1024, shape=(4, M, P)) for i in range(2)]
        go = at("go", A + 58 * K, M * D, shape=(M, D))
        gt = at("gt", A + 66 * K, 2 * 640, shape=(2, 640))
        gms = at("gms", A + 72 * K, 40)
        grs = at("grs", A + 72 * K + 256, 40)
        ghalf = at("ghalf", A + 72 * K + 512, 40)
        ggain = at("ggain", A + 73 * K, 128)
        hh = [at(f"hh{i}", A + 80 * K + 2 * K * i, 2 * S, F32R, (2, S)) for i in range(2)]
        hl = [at(f"hl{i}", A + 84 * K + 2 * K * i, 2 * S, F32R, (2, S)) for i in range(2)]
        sg = [at(f"sg{i}", A + 88 * K + K * i, S) for i in range(2)]
        h32 = [at(f"h32{i}", A + 90 * K + K * i, S) for i in range(2)]
        NB2 = 2048 + 1024 + 240 + 8 + 128
        tab2 = at("tab2", A, NB2)
        nbias = tab2[:, 0:2048].rearrange("p (h k) -> p h k", h=8)
        rdec = tab2[:, 2048:3072].rearrange("p (h k) -> p h k", h=4)
        cbias = tab2[:, 3072:3312].rearrange("p (m h n) -> p m h n", m=M, h=HN)
        blockm = tab2[:, 3312:3320]
        trilT = tab2[:, 3320:3448]
        lng = at("lng", A + 14 * K, 2048)
        bm = [at(f"bm{i}", A + 22 * K + K * i, S) for i in range(2)]
        gmws = at("gmws", A + 24 * K, 512, shape=(4, P))
        bd = at("bd", A + 24 * K, 512, shape=(HN, 64))
        sm2 = at("sm2", A + 26 * K, 4 + 128 + 32)
        gmbs, cw2, cpos = sm2[:, 0:4], sm2[:, 4:132].rearrange("p (i d) -> p i d", i=2), sm2[:, 132:164].rearrange("p (i l) -> p i l", i=2)
        uA = at("uA", A + 27 * K, M * 512, shape=(M, 512))
        vA = at("vA", A + 31 * K, M * 512, shape=(M, 512))
        rqk = at("rqk", A + 35 * K, 4 * S, shape=(4, S))
        rv = at("rv", A + 39 * K, M * 512, shape=(M, 512))
        rg = at("rg", A + 43 * K, M * 512, shape=(M, 512))
        nq = at("nq", A + 47 * K, 4 * S, shape=(4, S))
        nk = at("nk", A + 51 * K, 2 * S, shape=(2, S))
        nv = at("nv", A + 53 * K, M * S, shape=(M, S))
        gates = at("gates", A + 55 * K, M * 3072, shape=(M, 3072))
        cw1 = at("cw1", A + 55 * K, 2 * TILE, shape=(2, 16, P))
        P2 = [at(f"p2_{i}", A + 79 * K + 4 * K * i, 1024, shape=(4, S)) for i in range(2)]
        PT2 = [at(f"pt2_{i}", A + 87 * K + 4 * K * i, 1024, shape=(4, M, P)) for i in range(2)]
        kvd = at("kvd", A + 87 * K, 4 * S, shape=(2, 2, S))
        blk = at("blk", A + 91 * K, 2 * 16 * 30, shape=(2, 16, 2, NCMP))
        rs = [at(f"rs{i}", A + 79 * K + 2 * K * i, 384) for i in range(2)]
        aTh = at("aTh", A + 79 * K, 4 * S, F32R, (4, S))
        aTl = at("aTl", A + 83 * K, 4 * S, F32R, (4, S))
        bTh = at("bTh", A + 87 * K, 4 * S, F32R, (4, S))
        bTl = at("bTl", A + 91 * K, 4 * S, F32R, (4, S))
        cTh = at("cTh", A + 35 * K, 4 * S, F32R, (4, S))
        cTl = at("cTl", A + 39 * K, 4 * S, F32R, (4, S))
        L2 = A + 95 * K
        hid = at("hid", L2, 60, shape=(2, 30))
        hidx = at("hidx", L2 + 256, 120, shape=(2, 4, NCMP))
        kcs = at("kcs", L2 + 736, NCMP)
        ng = at("ng", L2 + 800, M * 24, shape=(M, 2, 4, 3))
        bdrow = at("bdrow", A + 13 * K + 512, 64)[0:120, :]
        og2 = at("og2", A + 35 * K, 256, shape=(4, 64))
        pb = [ctx.enter_context(nc.psum_tensor(f"bank{i}", [P, 512], F32))[:, :] for i in range(8)]

        def sem(name):
            return ctx.enter_context(nc.semaphore(name))

        landed = [sem(f"landed{i}") for i in range(3)]
        hi_made = sem("hi_made")
        lo_made = sem("lo_made")
        step_done = sem("step_done")
        drain_act = sem("drain_act")
        drain_dve = sem("drain_dve")
        tb_done = sem("tb_done")
        tb_act = sem("tb_act")
        tb_dve = sem("tb_dve")
        x_ready = sem("x_ready")
        x_in = sem("x_in")
        tab_in = sem("tab_in")
        gg_in = sem("gg_in")
        tab2_in = sem("tab2_in")
        gain_in = sem("gain_in")
        lay_in = sem("lay_in")
        bm_in = [sem("bm_in0"), sem("bm_in1")]
        half_set = sem("half_set")
        ss_act = sem("ss_act")
        ms_ready = sem("ms_ready")
        rstd_ready = sem("rstd_ready")
        y_ready = sem("y_ready")
        src_ready = sem("src_ready")
        sc_done = sem("sc_done")
        mx_ready = sem("mx_ready")
        p_ready = sem("p_ready")
        o_done = sem("o_done")
        o_ready = sem("o_ready")
        h_ready = sem("h_ready")
        silu_done = sem("silu_done")
        acc_done = sem("acc_done")
        gsq_act = sem("gsq_act")
        wexp = sem("wexp")
        wmx = sem("wmx")
        blk_ready = sem("blk_ready")
        hid_done = sem("hid_done")
        hid_act = sem("hid_act")
        hidx_ready = sem("hidx_ready")
        kc_done = sem("kc_done")
        kc_ready = sem("kc_ready")
        gm_ready = sem("gm_ready")
        gm_done = sem("gm_done")
        ya_ready = sem("ya_ready")
        rs_done = sem("rs_done")
        rs_ready = sem("rs_ready")
        ro_done = sem("ro_done")
        yb_ready = sem("yb_ready")
        cs_done = sem("cs_done")
        cs_ready = sem("cs_ready")
        ce_ready = sem("ce_ready")
        co_done = sem("co_done")
        yc_ready = sem("yc_ready")
        sig_done = sem("sig_done")
        mix_ready = sem("mix_ready")
        layer_done = sem("layer_done")
        out_ready = sem("out_ready")
        out_done = sem("out_done")
        dve_link = sem("dve_link")

        N1 = Numbers()
        block = ctx.enter_context(nc.Block())

        def rows3(t, kc, w):
            return t[:, 0:kc * w].rearrange("p (k n) -> p k n", k=kc)

        def bank2(i):
            return pb[i].rearrange("p (a n) -> p a n", a=2)

        def pt_part(g, b):
            if g["nk"] == P:
                return g["pt"][:, :, 0, :]
            return g["pt"][:, 2 * b:2 * b + 2, :, :].rearrange("p h k q -> p (h k) q")

        def mla_groups():
            out = []
            for m in range(M):
                for q in range(2):
                    i = len(out)
                    hs = [4 * q + h for h in range(4)]
                    out.append(dict(
                        q=[mqT[0:DK1, h, m * P:m * P + P] for h in hs], k=[mkT[0:DK1, h, :] for h in hs],
                        v=lambda h, kt, q=q: mkv[:, kt, 4 * q + h, 64:128], nk=S, p=P0[i % 2], pt=PT0[i % 2],
                        scale=DK1 ** -0.5, bias=None, out=ocat[:, m, 256 * q:256 * q + 256].rearrange("p (h d) -> p h d", h=4)))
            return out

        def dil_groups():
            out = []
            for m in range(M):
                for g in range(DG):
                    i = len(out)
                    at_ = [(slice(64 * (s % 2), 64 * (s % 2) + 64), 2 * g + s // 2) for s in SLOT_HEADS]
                    out.append(dict(
                        q=[dqk[r, c, m * P:m * P + P] for r, c in at_],
                        k=[dqk[r, 6 + c, :] for r, c in at_],
                        v=lambda s, kt, g=g: dv[:, kt, 256 * g + 64 * SLOT_HEADS[s]:256 * g + 64 * SLOT_HEADS[s] + 64], nk=S, p=P0[i % 2], pt=PT0[i % 2],
                        scale=1.0, bias=dbias[:, 4 * g:4 * g + 4, P * (1 - m):P * (3 - m)], out=og[:, m, g, :, :],
                        mx=mxd[:, m, g, :], den=dend[:, m, g, :]))
            return out

        def gqa_groups():
            out = []
            for m in range(M):
                for g in range(G2):
                    i = len(out)
                    r = slice(64 * (g % 2), 64 * (g % 2) + 64)
                    c = 512 * (g // 2) + 64 * (g % 2)
                    o = go[:, m, 512 * (g // 2):512 * (g // 2) + 512].rearrange("p (h b d) -> p h b d", h=4, b=2)[:, :, g % 2, :]
                    out.append(dict(
                        q=[gqT[r, 4 * (g // 2) + h, m * P:m * P + P] for h in range(4)], k=[gkT[r, g // 2, :]] * 4,
                        v=lambda h, kt, g=g: gqkv[:, kt, 1280 + 64 * g:1344 + 64 * g], nk=S, p=P1[i % 2], pt=PT1[i % 2],
                        scale=0.125, bias=None, out=o))
            return out

        def nsa_groups():
            out = []
            for m in range(M):
                for br in range(2):
                    for g in range(2):
                        i = len(out)
                        r = slice(64 * g, 64 * g + 64)
                        nk_ = P * (m + 1)
                        out.append(dict(
                            q=[nq[r, h, m * P:m * P + P] for h in range(4)], k=[nk[r, br, 0:nk_]] * 4,
                            v=lambda h, kt, g=g, br=br: nv[:, kt, P * br + 64 * g:P * br + 64 * g + 64], nk=nk_,
                            p=P2[i % 2], pt=PT2[i % 2], scale=1.0, bias=nbias[:, 4 * g:4 * g + 4, P * (1 - m):2 * P],
                            gate=ng[:, m, g, :, 1 + br], out=vA[:, m, 256 * g:256 * g + 256].rearrange("p (h d) -> p h d", h=4)))
            return out

        @block.sync
        def _(sp):
            sp.dma_start(x, xin).then_inc(x_in, 16)
            for r in range(3):
                sp.dma_start(raw[r], stream[r]).then_inc(landed[r], 16)
            with nc.sync.Fori(1, TILES // 3) as third:
                for r in range(3):
                    sp.wait_ge(hi_made, 3 * third + r - 2)
                    sp.wait_ge(lo_made, 3 * third + r - 2)
                    sp.dma_start(raw[r], stream[bass.ds(3 * third + r, 1)].rearrange("a p n -> (a p) n")).then_inc(landed[r], 16)
            for t in range(3 * (TILES // 3), TILES):
                sp.wait_ge(hi_made, t - 2)
                sp.wait_ge(lo_made, t - 2)
                sp.dma_start(raw[t % 3], stream[t]).then_inc(landed[t % 3], 16)
            sp.wait_ge(out_ready, 1)
            sp.dma_start(out, y).then_inc(out_done, 16)
            sp.wait_ge(out_done, 16)

        @block.gpsimd
        def _(pool):
            pool.dma_start(misc_sb, misc).then_inc(tab_in, 16)
            pool.dma_start(gbc, gains[0]).then_inc(gain_in, 16)
            pool.dma_start(dbias.rearrange("p h k -> p (h k)"), dilb).then_inc(tab_in, 16)
            pool.dma_start(mlagain, mlag[:, 0:640]).then_inc(tab_in, 16)
            pool.memset(half, -0.5).then_inc(half_set, 1)
            pool.wait_ge(half_set, 1)
            powers = [0]

            def power(n, src=ms, dst=rstd, e=half, count=None):
                k = powers[0] if count is None else count
                pool.wait_ge(ms_ready, k + 1)
                pool.tensor_tensor(dst[:, 0:n], src[:, 0:n], e[:, 0:n], ALU.pow).then_inc(rstd_ready, 1)
                powers[0] += 1

            def next_gain(i):
                pool.wait_ge(y_ready, 2 * i)
                pool.dma_start(gbc, gains[i]).then_inc(gain_in, 16)

            power(2)
            next_gain(1)
            power(4)
            power(2)
            next_gain(2)
            power(2)
            next_gain(3)
            pool.wait_ge(x_ready, 2)
            pool.memset(ghalf, -0.5).then_inc(half_set, 1)
            pool.dma_start(ggain, mlag[:, 640:768]).then_inc(gg_in, 16)
            pool.wait_ge(half_set, 2)
            power(40, gms, grs, ghalf)
            power(2)
            next_gain(4)
            power(2)
            next_gain(5)
            pool.wait_ge(x_ready, 3)
            pool.dma_start(tab2, second).then_inc(tab2_in, 16)
            for l in range(LAYERS):
                n = 5 + 3 * l
                if l > 0:
                    pool.wait_ge(layer_done, l)
                pool.dma_start(lng, rows[l]).then_inc(lay_in, 16)
                pool.dma_start(gmws.rearrange("p g t -> p (g t)"), small[l][:, 0:512]).then_inc(lay_in, 16)
                pool.dma_start(sm2, small[l][:, 512:676]).then_inc(lay_in, 16)
                pool.dma_start(cw1.rearrange("p i l c -> p (i l c)"), small[l][:, 676:676 + 4096]).then_inc(lay_in, 16)
                power(2)
                next_gain(n + 1)
                power(2)
                next_gain(n + 2)
                pool.dma_start(bm[0], small[l][:, 4772:5028]).then_inc(bm_in[0], 16)
                pool.dma_start(bm[1], small[l][:, 5028:5284]).then_inc(bm_in[1], 16)
                power(2)
                power(8)
                B = Numbers(l)
                g0 = B.plan.step["gates"]
                for i in range(2, 12):
                    pool.wait_ge(drain_dve, B.drained(g0 + i - 1, "D"))
                    pool.dma_start(bm[i % 2], small[l][:, 4772 + 256 * i:5028 + 256 * i]).then_inc(bm_in[i % 2], 16)
                power(2)
                next_gain(n + 3)
            power(2)

        @block.tensor
        def _(pe):
            def three(o, a, b, first, last):
                pe.matmul(o, a[1], b[0], start=first, stop=False)
                pe.matmul(o, a[0], b[1], start=False, stop=False)
                return pe.matmul(o, a[0], b[0], start=False, stop=last)

            def tile_split(B, tile, thirds=0):
                n = B.tile_no(tile, thirds) + 1
                pe.wait_ge(hi_made, n)
                pe.wait_ge(lo_made, n)

            def bank_free(B, step, first):
                for s, who in ((drain_act, "A"), (drain_dve, "D")):
                    n = B.drained(step if first else step - 1, who)
                    if type(n) is not int or n > 0:
                        pe.wait_ge(s, n)

            def features(B, tile, kc, w, c0, act, o):
                s = B.slot(tile)
                hi, lo = rows3(whi[s], kc, w), rows3(wlo[s], kc, w)
                for c in range(2):
                    for k in range(kc):
                        cols = slice(c0 + c * P, c0 + c * P + P)
                        last = three(o[:, c, :], (hi[:, k, cols], lo[:, k, cols]), (act[0][:, k, :], act[1][:, k, :]),
                                     k == 0, k == kc - 1)
                return last

            def tokens(B, tile, kc, w, c0, n, act, o):
                s = B.slot(tile)
                hi, lo = rows3(whi[s], kc, w), rows3(wlo[s], kc, w)
                for m in range(M):
                    for k in range(kc):
                        t = slice(m * P, m * P + P)
                        last = three(o[:, m, 0:n], (act[0][:, k, t], act[1][:, k, t]), (hi[:, k, c0:c0 + n], lo[:, k, c0:c0 + n]),
                                     k == 0, k == kc - 1)
                return last

            def copied(B, n):
                for s, who in ((tb_act, "A"), (tb_dve, "D")):
                    pe.wait_ge(s, B.copied(n, who))

            def batch(B, tb, blocks, rows=P):
                n = B.tb0 + tb
                if type(n) is not int or n >= 2:
                    copied(B, tb - 1)
                o = pb[B.bank(tb)]
                for i, b in enumerate(blocks):
                    last = pe.transpose(o[0:rows, i * P:i * P + P], b, ident)
                last.then_inc(tb_done, 1)

            def norm_T(B, stage, n):
                for m in range(M):
                    pe.wait_ge(y_ready, 2 * n + m + 1)
                    for q in range(2):
                        batch(B, B.plan.tb[stage] + 2 * m + q, [y[:, m, (4 * q + k) * P:(4 * q + k + 1) * P] for k in range(4)])

            def dense(B, stage, i, kind, kc=8, w=256, c0=0, n=256, act=(yh, yl), per_tile=1, bank=None, alone=False):
                tile, step = B.plan.tile[stage] + i // per_tile, B.plan.step[stage] + i
                tile_split(B, tile)
                bank_free(B, step, i == 0 or alone)
                o = bank2(i % 2 if bank is None else bank)
                if kind == "F":
                    last = features(B, tile, kc, w, c0, act, o)
                else:
                    last = tokens(B, tile, kc, w, c0, n, act, o)
                last.then_inc(step_done, 1)

            def ffn(B, stage, f):
                t0, s0 = B.plan.tile[stage], B.plan.step[stage]

                def up(tile, j_bank, first=False):
                    tile_split(B, t0 + tile)
                    bank_free(B, s0 + tile, first)
                    features(B, t0 + tile, 8, 256, 0, (yh, yl), bank2(j_bank)).then_inc(step_done, 1)

                def down(i, tile):
                    tile_split(B, t0 + tile)
                    pe.wait_ge(h_ready, NF * f + 2 * i + 2)
                    s = B.slot(t0 + tile)
                    hi, lo = rows3(whi[s], 2, 1024), rows3(wlo[s], 2, 1024)
                    for k in range(2):
                        for m in range(M):
                            for n in range(2):
                                t, c = slice(m * P, m * P + P), slice(n * 512, n * 512 + 512)
                                last = three(pb[2 + 2 * m + n], (hh[i % 2][:, k, t], hl[i % 2][:, k, t]),
                                             (hi[:, k, c], lo[:, k, c]), i == 0 and k == 0, i == NF // 2 - 1 and k == 1)
                    last.then_inc(step_done, 1)

                up(0, 0, True)
                up(1, 1)
                for i in range(1, NF // 2):
                    up(3 * i - 1, 0)
                    up(3 * i, 1)
                    down(i - 1, 3 * i + 1)
                down(NF // 2 - 1, FFN_TILES - 1)

            def attention(B, stage, groups, ag0, extra=None):
                first_tb, t = [], B.plan.tb[stage]
                for g in groups:
                    first_tb.append(t)
                    t += g["nk"] // P
                n = len(groups)
                for i in range(n + 2):
                    if i < n:
                        g, a = groups[i], ag0 + i
                        if type(a) is not int or a >= 2:
                            pe.wait_ge(p_ready, a - 1)
                        for h in range(4):
                            o = pb[2 + 2 * (i % 2) + h // 2][:, (h % 2) * S:(h % 2) * S + g["nk"]]
                            last = pe.matmul(o, g["q"][h], g["k"][h], start=True, stop=True)
                        last.then_inc(sc_done, 1)
                    if extra:
                        extra(i)
                    if 1 <= i <= n:
                        g, a, tb = groups[i - 1], ag0 + i - 1, first_tb[i - 1]
                        pe.wait_ge(p_ready, a + 1)
                        nt = g["nk"] // P
                        for b in range(nt):
                            hs = range(4) if nt == 1 else (2 * b, 2 * b + 1)
                            batch(B, tb + b, [g["p"][:, h, kt * P:kt * P + P] for h in hs for kt in range(nt)])
                    if i >= 2:
                        g, a, tb = groups[i - 2], ag0 + i - 2, first_tb[i - 2]
                        nt = g["nk"] // P
                        copied(B, tb + nt)
                        if type(a) is not int or a >= 1:
                            pe.wait_ge(o_ready, a)
                        for h in range(4):
                            o = pb[1][:, h * 64:h * 64 + 64]
                            for kt in range(nt):
                                last = pe.matmul(o, g["pt"][:, h, kt, :], g["v"](h, kt), start=kt == 0, stop=kt == nt - 1)
                        last.then_inc(o_done, 1)

            def square(B, tb, src, kc, n_blocks):
                for b in range(n_blocks // 4):
                    batch(B, tb + b, [src(m, 2 * b + k) for k in range(2) for m in range(M)])

            B = N1
            pe.wait_ge(tab_in, 48)
            norm_T(B, "n0", 0)
            copied(B, 4)
            for i in range(12):
                if i < 3:
                    dense(B, "z", i, "T", n=256 if i < 2 else 160)
                else:
                    dense(B, "z", i, "F" if i < 9 else "T")
            pe.wait_ge(src_ready, 1)
            tb = B.plan.tb["cq"]
            batch(B, tb, [zA[:, 0, k * P:k * P + P] for k in range(3)])
            batch(B, tb + 1, [zA[:, 1, k * P:k * P + P] for k in range(3)])
            batch(B, tb + 2, [zA[:, m, RQ + k * P:RQ + k * P + P] for k in range(2) for m in range(M)])
            copied(B, tb + 3)
            for i in range(3):
                dense(B, "uq", i, "T", kc=3, w=512 if i < 2 else 256, c0=256 * (i % 2), act=(cqTh, cqTl), per_tile=2)
            for i in range(4):
                dense(B, "ukv", i, "T", kc=2, w=1024, c0=256 * i, act=(kvTh, kvTl), per_tile=4)
            pe.wait_ge(src_ready, 2)
            tb = B.plan.tb["mqk"]
            for b in range(4):
                batch(B, tb + b, [mq[:, m, 2 * b + k, :] for k in range(2) for m in range(M)], DK1)
            pe.wait_ge(src_ready, 3)
            for b in range(4):
                batch(B, tb + 4 + b, [kasm[:, m, 2 * b + k, :] for k in range(2) for m in range(M)], DK1)
            copied(B, tb + 8)
            attention(B, "mla", mla_groups(), AG_MLA)
            attention(B, "dil", dil_groups(), AG_DIL)
            pe.wait_ge(src_ready, 4)
            tb = B.plan.tb["ocat"]
            square(B, tb, lambda m, k: ocat[:, m, k * P:k * P + P], 6, 12)
            copied(B, tb + 3)
            for i in range(4):
                dense(B, "wout", i, "T", kc=6, act=(oTh, oTl))
            norm_T(B, "n1", 1)
            copied(B, B.plan.tb["n1"] + 4)
            ffn(B, "f0", 0)
            norm_T(B, "n2", 2)
            copied(B, B.plan.tb["n2"] + 4)
            for i in range(6):
                dense(B, "gqkv", i, "T")
            pe.wait_ge(src_ready, 5)
            tb = B.plan.tb["gqk"]
            square(B, tb, lambda m, k: gr[:, m, k * P:k * P + P], 10, 20)
            copied(B, tb + 5)
            attention(B, "gqa", gqa_groups(), AG_GQA)
            pe.wait_ge(o_ready, AG_GQA + 8)
            tb = B.plan.tb["go"]
            square(B, tb, lambda m, k: go[:, m, k * P:k * P + P], 8, 16)
            copied(B, tb + 4)
            for i in range(4):
                dense(B, "gwo", i, "T")
            norm_T(B, "n3", 3)
            copied(B, B.plan.tb["n3"] + 4)
            ffn(B, "f1", 1)

            def layer(l):
                B = Numbers(l)
                plan = B.plan
                norm_T(B, "n4", 5 + 3 * l)
                copied(B, plan.tb["n4"] + 4)
                ffn(B, "fa", 2 + 2 * l)
                norm_T(B, "n5", 6 + 3 * l)
                copied(B, plan.tb["n5"] + 4)
                kinds = "FFTTTTFFTTTTFFFTT"
                pe.wait_ge(lay_in, 64 * (l + 1))
                for i in range(17):
                    dense(B, "win", i, kinds[i], n=24 if i == 16 else 256)
                    if i == 3:
                        pe.wait_ge(blk_ready, l + 1)
                        for kv in range(2):
                            for lp in range(16):
                                last = pe.matmul(pb[2][:, kv * 30:kv * 30 + 30], cw1[:, kv, lp, :],
                                                 blk[:, kv, lp, :, :].rearrange("p g n -> p (g n)"), start=lp == 0, stop=lp == 15)
                        last.then_inc(hid_done, 1)
                    if i == 7:
                        pe.wait_ge(hidx_ready, l + 1)
                        for g in range(2):
                            pe.matmul(pb[3][64 * g:64 * g + 64, 0:NCMP], cw2[:, 0, :], hid[:, 0, g * NCMP:g * NCMP + NCMP], start=True, stop=True)
                        pe.matmul(pb[4][0:120, 0:64], hidx.rearrange("p g r n -> p (g r n)"), cw2[:, 1, :], start=True, stop=True).then_inc(kc_done, 1)
                pe.wait_ge(gm_ready, l + 1)
                pe.wait_ge(kc_ready, l + 1)
                for m in range(M):
                    for g in range(4):
                        last = pe.matmul(pb[4 + m][:, g * P:g * P + P], gmws[:, g, :], vA[:, m, g * P:g * P + P], start=True, stop=True)
                last.then_inc(gm_done, 1)
                pe.wait_ge(drain_dve, B.drained(plan.step["win"] + 8, "D"))
                pe.wait_ge(drain_act, B.drained(plan.step["win"] + 10, "A"))
                for h in range(HR + 1):
                    if h < HR:
                        r = slice(64 * (h % 2), 64 * (h % 2) + 64)
                        if h >= 2:
                            pe.wait_ge(rs_ready, HR * l + h - 1)
                        pe.matmul(pb[2 + h % 2][:, 0:S], rqk[r, 2 + h // 2, 0:P], rqk[r, h // 2, :], start=True, stop=True)
                        pe.matmul(pb[2 + h % 2][:, S:S + P], rqk[r, 2 + h // 2, P:S], rqk[r, h // 2, P:S], start=True, stop=True).then_inc(rs_done, 1)
                    if h >= 1:
                        g = h - 1
                        if g == 0:
                            pe.wait_ge(ya_ready, l + 1)
                        pe.wait_ge(rs_ready, HR * l + g + 1)
                        c = slice(g * P, g * P + P)
                        pe.matmul(pb[4][:, c], rs[g % 2][:, 0:P], rv[:, 0, c], start=True, stop=True)
                        pe.matmul(pb[5][:, c], rs[g % 2][:, P:S], rv[:, 0, c], start=True, stop=False)
                        pe.matmul(pb[5][:, c], rs[g % 2][:, S:S + P], rv[:, 1, c], start=False, stop=True).then_inc(ro_done, 1)
                for m in range(M):
                    for g in range(2):
                        for h in range(4 * g, 4 * g + 4):
                            r = slice(64 * g, 64 * g + 64)
                            last = pe.matmul(pb[2 + m][:, h * NCMP:h * NCMP + NCMP], nq[r, h % 4, m * P:m * P + P], kcs[r, :], start=True, stop=True)
                        last.then_inc(cs_done, 1)
                        if g == 0:
                            pe.wait_ge(cs_done, 4 * l + 2 * m + 1)
                dense(B, "gates", 0, "T", bank=0)
                tb = plan.tb["cmp"]
                for m in range(M):
                    pe.wait_ge(ce_ready, M * l + m + 1)
                    batch(B, tb + m, [P2[0][:, m, 0:120]], 120)
                dense(B, "gates", 1, "T", bank=0, alone=True)
                pe.wait_ge(yb_ready, l + 1)
                for m in range(M):
                    copied(B, tb + m + 1)
                    pe.matmul(pb[4 + m], PT2[0][0:120, m, 0, :], bd[0:120, :, :].rearrange("p h d -> p (h d)"), start=True, stop=True).then_inc(co_done, 1)
                pe.wait_ge(yc_ready, 3 * l + 2)
                attention(B, "nsa", nsa_groups(), AG_NSA + 8 * l,
                          lambda i: dense(B, "gates", 2 + i, "T", bank=0, alone=True))
                tb = plan.tb["y"]
                square(B, tb, lambda m, k: uA[:, m, k * P:k * P + P], 4, 8)
                square(B, tb + 2, lambda m, k: rg[:, m, k * P:k * P + P], 4, 8)
                pe.wait_ge(yc_ready, 3 * l + 3)
                square(B, tb + 4, lambda m, k: vA[:, m, k * P:k * P + P], 4, 8)
                for i in range(12):
                    if i % 4 == 0:
                        copied(B, tb + 2 * (i // 4) + 2)
                    dense(B, "branch", i, "T", kc=4, w=512, c0=256 * (i % 2), per_tile=2,
                          act=((aTh, aTl), (bTh, bTl), (cTh, cTl))[i // 4])
                pe.wait_ge(mix_ready, l + 1)
                tb = plan.tb["mix"]
                square(B, tb, lambda m, k: y[:, m, k * P:k * P + P], 8, 16)
                copied(B, tb + 4)
                for i in range(4):
                    dense(B, "wo", i, "T")
                norm_T(B, "n6", 7 + 3 * l)
                copied(B, plan.tb["n6"] + 4)
                ffn(B, "fb", 3 + 2 * l)

            for l in range(LAYERS):
                layer(l)

        @block.scalar
        def _(act):

            def split(B, tile, thirds=0):
                s = B.slot(tile)
                act.wait_ge(landed[s], B.landed(tile, thirds))
                if B.l is not None or tile >= 3:
                    act.wait_ge(step_done, B.step0 + B.last_step(tile - 3) + 1)
                act.activation(whi[s], raw[s], ACT.Copy).then_inc(hi_made, 1)

            def ahead(B, stage, i, per_tile=1):
                if i % per_tile == 0:
                    split(B, B.plan.tile[stage] + i // per_tile + 2)

            def stepped(B, stage, i):
                act.wait_ge(step_done, B.step0 + B.plan.step[stage] + i + 1)

            def hi_T(B, tb, dst, n=512):
                act.wait_ge(tb_done, B.tb0 + tb + 1)
                src = pb[B.bank(tb)][:, 0:n]
                if len(dst.shape) == 3:
                    src = src.rearrange("p (a n) -> p a n", a=dst.shape[1])
                act.activation(dst, src, ACT.Copy).then_inc(tb_act, 1)

            def plain_T(B, tb, dst, rows_=P):
                if B.plan.copies[tb] == "A":
                    act.wait_ge(tb_done, B.tb0 + tb + 1)
                    act.activation(dst, pb[B.bank(tb)][0:rows_].rearrange("p (a n) -> p a n", a=dst.shape[1]), ACT.Copy).then_inc(tb_act, 1)

            def sumsq(n):
                if n == 0:
                    act.wait_ge(x_in, 16)
                else:
                    act.wait_ge(x_ready, n)
                act.activation(y[:, 0, :], x[:, 0, :], ACT.Square, accum_out=ss[:, 0:1]).then_inc(ss_act, 1)

            def norm_T(B, stage):
                for m in range(M):
                    for q in range(2):
                        hi_T(B, B.plan.tb[stage] + 2 * m + q, yh[:, 4 * q:4 * q + 4, m * P:m * P + P])

            def square_T(B, tb, n, dst):
                for b in range(n):
                    hi_T(B, tb + b, dst[:, 2 * b:2 * b + 2, :])

            def ffn(B, stage, f):
                for i in range(NF // 2 + 1):
                    if i < NF // 2:
                        for j in (2 * i, 2 * i + 1):
                            t = j if i == 0 else 3 * i - 1 + j % 2
                            ahead(B, stage, t)
                            stepped(B, stage, t)
                            if 22 * f + j >= 2:
                                act.wait_ge(h_ready, NF * f + j - 1)
                            act.activation(sg[j % 2], bank2(j % 2)[:, 0, :], ACT.Silu).then_inc(silu_done, 1)
                    if i > 0:
                        ahead(B, stage, 3 * i + 1 if i < NF // 2 else FFN_TILES - 1)

            def attention(B, stage, groups, ag0, extra=None):
                t, first_tb = B.plan.tb[stage], []
                for g in groups:
                    first_tb.append(t)
                    t += g["nk"] // P
                n = len(groups)
                for i in range(n + 1):
                    if extra:
                        extra(i)
                    if i < n:
                        g, a = groups[i], ag0 + i
                        act.wait_ge(mx_ready, a + 1)
                        if i >= 2:
                            act.wait_ge(tb_done, B.tb0 + first_tb[i - 2] + groups[i - 2]["nk"] // P)
                        if i >= 4 or type(a) is not int or a >= 4:
                            act.wait_ge(o_ready, a - 3)
                        for h in range(4):
                            src = g["p"][:, h, 0:g["nk"]] if g["bias"] is not None else \
                                pb[2 + 2 * (i % 2) + h // 2][:, (h % 2) * S:(h % 2) * S + S]
                            d = g["den"][:, h:h + 1] if "den" in g else den[:, i % 4, h:h + 1]
                            last = act.activation(g["p"][:, h, 0:g["nk"]], src, ACT.Exp, bias=nmx[:, i % 2, h:h + 1],
                                                  scale=g["scale"], accum_out=d)
                        last.then_inc(p_ready, 1)
                    if i >= 1:
                        g, a, tb = groups[i - 1], ag0 + i - 1, first_tb[i - 1]
                        nt = g["nk"] // P
                        if i - 1 >= 2:
                            act.wait_ge(o_done, a - 1)
                        for b in range(nt):
                            plain_T(B, tb + b, pt_part(g, b))

            B = N1
            split(B, 0)
            split(B, 1)
            sumsq(0)
            norm_T(B, "n0")
            for i in range(12):
                ahead(B, "z", i)
                stepped(B, "z", i)
                if i < 3:
                    n = 256 if i < 2 else 160
                    ins = act.activation(zA[:, :, 256 * i:256 * i + n], bank2(i % 2)[:, :, 0:n], ACT.Copy)
                elif i < 9:
                    ins = act.activation(dqk[:, 2 * i - 6:2 * i - 4, :], bank2(i % 2), ACT.Copy, scale=0.125 if i < 6 else 1.0)
                else:
                    ins = act.activation(dv[:, :, 256 * (i - 9):256 * (i - 8)], bank2(i % 2), ACT.Copy)
                ins.then_inc(drain_act, 1)
            tb = B.plan.tb["cq"]
            hi_T(B, tb, cqTh[:, :, 0:P], 384)
            hi_T(B, tb + 1, cqTh[:, :, P:S], 384)
            hi_T(B, tb + 2, kvTh[:, :, :])
            for i in range(3):
                ahead(B, "uq", i, 2)
            for i in range(4):
                ahead(B, "ukv", i, 4)
                stepped(B, "ukv", i)
                act.activation(mkv[:, :, 2 * i:2 * i + 2, :].rearrange("p m h d -> p m (h d)"), bank2(i % 2), ACT.Copy).then_inc(drain_act, 1)
            tb = B.plan.tb["mqk"]
            for b in range(8):
                plain_T(B, tb + b, (mqT if b < 4 else mkT)[0:DK1, 2 * (b % 4):2 * (b % 4) + 2, :], DK1)
            attention(B, "mla", mla_groups(), AG_MLA)
            attention(B, "dil", dil_groups(), AG_DIL)
            act.wait_ge(wmx, 1)
            act.activation(wd.rearrange("p m g s -> p (m g s)"), wd.rearrange("p m g s -> p (m g s)"), ACT.Exp).then_inc(wexp, 1)
            square_T(B, B.plan.tb["ocat"], 3, oTh)
            for i in range(4):
                ahead(B, "wout", i)
            sumsq(1)
            norm_T(B, "n1")
            ffn(B, "f0", 0)
            sumsq(2)
            norm_T(B, "n2")
            for i in range(6):
                ahead(B, "gqkv", i)
                stepped(B, "gqkv", i)
                act.activation(gqkv[:, :, 256 * i:256 * i + 256], bank2(i % 2), ACT.Copy).then_inc(drain_act, 1)
            act.wait_ge(drain_act, B.drained(B.plan.step["gqkv"] + 6, "A"))
            act.activation(gsq, gqkv[:, :, 0:1280], ACT.Square).then_inc(gsq_act, 1)
            tb = B.plan.tb["gqk"]
            for b in range(5):
                plain_T(B, tb + b, gqT[:, 2 * b:2 * b + 2, :] if b < 4 else gkT)
            attention(B, "gqa", gqa_groups(), AG_GQA)
            square_T(B, B.plan.tb["go"], 4, yh)
            for i in range(4):
                ahead(B, "gwo", i)
            sumsq(3)
            norm_T(B, "n3")
            ffn(B, "f1", 1)
            sumsq(4)

            def layer(l):
                B = Numbers(l)
                plan = B.plan
                sumsq(5 + 3 * l)
                norm_T(B, "n4")
                ffn(B, "fa", 2 + 2 * l)
                sumsq(6 + 3 * l)
                norm_T(B, "n5")
                for i in range(17):
                    ahead(B, "win", i)
                    o = bank2(i % 2)
                    if WIN_DRAINS[i] == "A":
                        stepped(B, "win", i)
                        if i in (2, 3, 4, 5):
                            dst = (vA if i < 4 else uA)[:, :, 256 * (i % 2):256 * (i % 2) + 256]
                            ins = act.activation(dst, o, ACT.Gelu_apprx_tanh)
                        elif i in (8, 9):
                            ins = act.activation(rv[:, :, 256 * (i % 2):256 * (i % 2) + 256], o, ACT.Copy)
                        elif i in (10, 11):
                            ins = act.activation(rg[:, :, 256 * (i % 2):256 * (i % 2) + 256], o, ACT.Silu)
                        else:
                            ins = act.activation(ng.rearrange("p m g r b -> p m (g r b)"), o[:, :, 0:24], ACT.Exp, scale=-1.0)
                        ins.then_inc(drain_act, 1)
                    if i == 5:
                        act.wait_ge(hid_done, l + 1)
                        act.activation(hid.rearrange("p i n -> p (i n)"), pb[2][:, 0:60], ACT.Gelu_apprx_tanh).then_inc(hid_act, 1)
                for m in range(M):
                    act.wait_ge(cs_ready, M * l + m + 1)
                    act.activation(P2[0][:, m, 0:120], P2[0][:, m, 0:120], ACT.Exp).then_inc(ce_ready, 1)
                    if m == 0:
                        ahead(B, "gates", 0)
                ahead(B, "gates", 1)
                tb = plan.tb["cmp"]
                act.wait_ge(tb_done, B.tb0 + tb + 1)
                act.activation(PT2[0][0:120, 0, 0, :], pb[B.bank(tb)][0:120, 0:P], ACT.Copy).then_inc(tb_act, 1)
                act.wait_ge(co_done, M * l + 2)
                attention(B, "nsa", nsa_groups(), AG_NSA + 8 * l,
                          lambda i: ahead(B, "gates", 2 + i))
                ahead(B, "gates", 11)
                tb = plan.tb["y"]
                square_T(B, tb, 2, aTh)
                square_T(B, tb + 2, 2, bTh)
                square_T(B, tb + 4, 2, cTh)
                for i in range(3):
                    act.wait_ge(drain_dve, B.drained(plan.step["gates"] + 4 * i + 4, "D"))
                    act.activation(gates[:, :, 1024 * i:1024 * i + 1024], gates[:, :, 1024 * i:1024 * i + 1024], ACT.Sigmoid).then_inc(sig_done, 1)
                for i in range(12):
                    ahead(B, "branch", i, 2)
                square_T(B, plan.tb["mix"], 4, yh)
                for i in range(4):
                    ahead(B, "wo", i)
                sumsq(7 + 3 * l)
                norm_T(B, "n6")
                ffn(B, "fb", 3 + 2 * l)

            for l in range(LAYERS):
                layer(l)
            sumsq(11)

        @block.vector
        def _(dve):
            links = [0]
            powers = [0]

            def link(ins):
                links[0] += 1
                ins.then_inc(dve_link, 1)
                dve.wait_ge(dve_link, links[0])

            def split(B, tile, thirds=0):
                s = B.slot(tile)
                dve.wait_ge(hi_made, B.tile_no(tile, thirds) + 1)
                dve.tensor_tensor(wlo[s], raw[s], whi[s].bitcast(F32), ALU.subtract).then_inc(lo_made, 1)

            def ahead(B, stage, i, per_tile=1):
                if i % per_tile == 0:
                    split(B, B.plan.tile[stage] + i // per_tile + 2)

            def stepped(B, stage, i):
                dve.wait_ge(step_done, B.step0 + B.plan.step[stage] + i + 1)

            def lo_T(B, tb, dst, hi, n=512):
                dve.wait_ge(tb_act, B.copied(tb + 1, "A"))
                src = pb[B.bank(tb)][:, 0:n]
                if len(dst.shape) == 3:
                    src = src.rearrange("p (a n) -> p a n", a=dst.shape[1])
                dve.tensor_tensor(dst, src, hi.bitcast(F32), ALU.subtract).then_inc(tb_dve, 1)

            def plain_T(B, tb, dst, rows_=P):
                if B.plan.copies[tb] == "D":
                    dve.wait_ge(tb_done, B.tb0 + tb + 1)
                    dve.tensor_copy(dst, pb[B.bank(tb)][0:rows_].rearrange("p (a n) -> p a n", a=dst.shape[1])).then_inc(tb_dve, 1)

            def power(mean):
                mean.then_inc(ms_ready, 1)
                powers[0] += 1
                dve.wait_ge(rstd_ready, powers[0])

            def norm(n, dst=y):
                if n == 0:
                    dve.wait_ge(x_in, 16)
                else:
                    dve.wait_ge(x_ready, n)
                link(dve.tensor_tensor_reduce(out=y[:, 1, :], in0=x[:, 1, :], in1=x[:, 1, :], scale=1.0, scalar=0.0,
                                              op0=ALU.mult, op1=ALU.add, accum_out=ss[:, 1:2]))
                dve.wait_ge(ss_act, n + 1)
                power(dve.tensor_scalar(ms[:, 0:2], ss, 1.0 / D, EPS, ALU.mult, ALU.add))
                dve.wait_ge(gain_in, 16 * (n + 1))
                for m in range(M):
                    dve.scalar_tensor_tensor(out=dst[:, m, :], in0=x[:, m, :], scalar=rstd[:, m:m + 1], in1=gbc,
                                             op0=ALU.mult, op1=ALU.mult).then_inc(y_ready, 1)

            def norm_T(B, stage, n):
                norm(n)
                for m in range(M):
                    for q in range(2):
                        sl = (slice(None), slice(4 * q, 4 * q + 4), slice(m * P, m * P + P))
                        lo_T(B, B.plan.tb[stage] + 2 * m + q, yl[sl], yh[sl])

            def square_T(B, tb, n, lo, hi):
                for b in range(n):
                    lo_T(B, tb + b, lo[:, 2 * b:2 * b + 2, :], hi[:, 2 * b:2 * b + 2, :])

            def add_x(B, stage, bank_i, i):
                c = slice(256 * i, 256 * i + 256)
                dve.tensor_tensor(x[:, :, c], x[:, :, c], bank2(bank_i), ALU.add).then_inc(drain_dve, 1)

            def out_steps(B, stage, norm_no):
                for i in range(4):
                    ahead(B, stage, i)
                    stepped(B, stage, i)
                    add_x(B, stage, i % 2, i)
                dve.wait_ge(drain_dve, B.drained(B.plan.step[stage] + 4, "D"))
                dve.sem_inc(x_ready, 1)

            def ffn(B, stage, f, weight):
                for i in range(NF // 2 + 1):
                    if i < NF // 2:
                        for j in (2 * i, 2 * i + 1):
                            t = j if i == 0 else 3 * i - 1 + j % 2
                            ahead(B, stage, t)
                            dve.wait_ge(silu_done, NF * f + j + 1)
                            dve.tensor_tensor(h32[j % 2], sg[j % 2], bank2(j % 2)[:, 1, :], ALU.mult).then_inc(drain_dve, 1)
                            if i >= 2:
                                dve.wait_ge(step_done, B.step0 + B.plan.step[stage] + 3 * (i - 2) + 4 + 1)
                            dve.wait_ge(drain_dve, B.drained(B.plan.step[stage] + t + 1, "D"))
                            link(dve.tensor_copy(hh[i % 2][:, j % 2, :], h32[j % 2]))
                            dve.tensor_tensor(hl[i % 2][:, j % 2, :], h32[j % 2], hh[i % 2][:, j % 2, :].bitcast(F32), ALU.subtract).then_inc(h_ready, 1)
                    if i > 0:
                        ahead(B, stage, 3 * i + 1 if i < NF // 2 else FFN_TILES - 1)
                stepped(B, stage, FFN_TILES - 1)
                for m in range(M):
                    for n in range(2):
                        c = slice(512 * n, 512 * n + 512)
                        last = dve.scalar_tensor_tensor(out=x[:, m, c], in0=pb[2 + 2 * m + n], scalar=weight, in1=x[:, m, c],
                                                        op0=ALU.mult, op1=ALU.add)
                last.then_inc(x_ready, 1)

            def bc(a, n):
                return a.unsqueeze(len(a.shape)).broadcast_to(list(a.shape) + [n])

            def attention(B, stage, groups, ag0, drain, extra=None, after=None):
                t, first_tb = B.plan.tb[stage], []
                for g in groups:
                    first_tb.append(t)
                    t += g["nk"] // P
                n = len(groups)
                for i in range(n + 2):
                    if extra:
                        extra(i)
                    if i < n:
                        g, a = groups[i], ag0 + i
                        nk_ = g["nk"]
                        dve.wait_ge(sc_done, a + 1)
                        if type(a) is not int or a >= 2:
                            dve.wait_ge(p_ready, a - 1)
                        mxo = g["mx"] if "mx" in g else mx[:, i % 2, :]
                        if g["bias"] is not None:
                            if i >= 2:
                                dve.wait_ge(tb_done, B.tb0 + first_tb[i - 2] + groups[i - 2]["nk"] // P)
                            for h2 in range(2):
                                src = bank2(2 + 2 * (i % 2) + h2)[:, :, 0:nk_]
                                ins = dve.tensor_tensor(g["p"][:, 2 * h2:2 * h2 + 2, 0:nk_], src, g["bias"][:, 2 * h2:2 * h2 + 2, :], ALU.add)
                            link(ins)
                            link(dve.tensor_reduce(mxo, g["p"][:, :, 0:nk_], AX_X, ALU.max))
                        else:
                            for h2 in range(2):
                                ins = dve.tensor_reduce(mxo[:, 2 * h2:2 * h2 + 2], bank2(2 + 2 * (i % 2) + h2), AX_X, ALU.max)
                            link(ins)
                        dve.tensor_scalar(nmx[:, i % 2, :], mxo, -g["scale"], None, ALU.mult).then_inc(mx_ready, 1)
                    if 1 <= i <= n:
                        g, a, tb = groups[i - 1], ag0 + i - 1, first_tb[i - 1]
                        nt = g["nk"] // P
                        if i - 1 >= 2:
                            dve.wait_ge(o_done, a - 1)
                        for b in range(nt):
                            plain_T(B, tb + b, pt_part(g, b))
                    if i >= 2:
                        g, a = groups[i - 2], ag0 + i - 2
                        dve.wait_ge(o_done, a + 1)
                        drain(g, i - 2, pb[1][:, 0:S].rearrange("p (h d) -> p h d", h=4))
                    if after:
                        after(i)

            def normalize(g, i, o):
                link(dve.reciprocal(rec, den[:, i % 4, :]))
                dve.tensor_tensor(g["out"], o, bc(rec, 64), ALU.mult).then_inc(o_ready, 1)

            B = N1
            split(B, 0)
            split(B, 1)
            dve.wait_ge(tab_in, 48)
            norm_T(B, "n0", 0)
            for i in range(4):
                ahead(B, "z", i)
            dve.wait_ge(drain_act, 3)
            for j, (c0, n) in enumerate(((0, RQ), (RQ, RKV))):
                for m in range(M):
                    ins = dve.tensor_tensor_reduce(out=y[:, m, 0:n], in0=zA[:, m, c0:c0 + n], in1=zA[:, m, c0:c0 + n], scale=1.0,
                                                   scalar=0.0, op0=ALU.mult, op1=ALU.add, accum_out=ms[:, 4 + 2 * j + m:5 + 2 * j + m])
                    link(ins)
            link(dve.tensor_scalar(ms[:, 0:2], ms[:, 4:6], 1.0 / RQ, EPS, ALU.mult, ALU.add))
            power(dve.tensor_scalar(ms[:, 2:4], ms[:, 6:8], 1.0 / RKV, EPS, ALU.mult, ALU.add))
            for j, (c0, n) in enumerate(((0, RQ), (RQ, RKV))):
                for m in range(M):
                    ins = dve.scalar_tensor_tensor(out=zA[:, m, c0:c0 + n], in0=zA[:, m, c0:c0 + n], scalar=rstd[:, 2 * j + m:2 * j + m + 1],
                                                   in1=mlagain[:, c0:c0 + n], op0=ALU.mult, op1=ALU.mult)
            link(ins)
            dve.sem_inc(src_ready, 1)
            t1, t2 = (rt[:, i, 0:32].rearrange("p (m f) -> p m f", m=M) for i in range(2))
            ka, kb = zA[:, :, 640:656], zA[:, :, 656:672]
            dve.tensor_tensor(t1, ka, cos1, ALU.mult)
            link(dve.tensor_tensor(t2, kb, sin1, ALU.mult))
            link(dve.tensor_tensor(kr[:, :, 0:16], t1, t2, ALU.subtract))
            dve.tensor_tensor(t1, ka, sin1, ALU.mult)
            link(dve.tensor_tensor(t2, kb, cos1, ALU.mult))
            link(dve.tensor_tensor(kr[:, :, 16:32], t1, t2, ALU.add))
            for i in range(4, 12):
                ahead(B, "z", i)
            tb = B.plan.tb["cq"]
            for m in range(M):
                c = slice(m * P, m * P + P)
                lo_T(B, tb + m, cqTl[:, :, c], cqTh[:, :, c], 384)
            lo_T(B, tb + 2, kvTl, kvTh)
            for i in range(3):
                ahead(B, "uq", i, 2)
                stepped(B, "uq", i)
                dve.tensor_copy(mq.rearrange("p m h d -> p m (h d)")[:, :, 256 * i:256 * i + 256], bank2(i % 2)).then_inc(drain_dve, 1)
            ahead(B, "ukv", 0)
            dve.wait_ge(drain_dve, 3)
            qa, qb = mq[:, :, :, 64:80], mq[:, :, :, 80:96]
            t = [rt[:, i, :].rearrange("p (m h f) -> p m h f", m=M, h=H1) for i in range(4)]
            cb = cos1.unsqueeze(2).broadcast_to([P, M, H1, 16])
            sb_ = sin1.unsqueeze(2).broadcast_to([P, M, H1, 16])
            dve.tensor_tensor(t[0], qa, cb, ALU.mult)
            dve.tensor_tensor(t[1], qb, sb_, ALU.mult)
            dve.tensor_tensor(t[2], qa, sb_, ALU.mult)
            link(dve.tensor_tensor(t[3], qb, cb, ALU.mult))
            dve.tensor_tensor(qa, t[0], t[1], ALU.subtract)
            dve.tensor_tensor(qb, t[2], t[3], ALU.add).then_inc(src_ready, 1)
            dve.wait_ge(drain_act, B.drained(B.plan.step["ukv"] + 4, "A"))
            for m in range(M):
                dve.tensor_copy(kasm[:, m, :, 0:64], mkv[:, m, :, 0:64])
                ins = dve.tensor_copy(kasm[:, m, :, 64:96], kr[:, m, :].unsqueeze(1).broadcast_to([P, H1, 32]))
            ins.then_inc(src_ready, 1)
            tb = B.plan.tb["mqk"]
            for b in range(8):
                plain_T(B, tb + b, (mqT if b < 4 else mkT)[0:DK1, 2 * (b % 4):2 * (b % 4) + 2, :], DK1)
            attention(B, "mla", mla_groups(), AG_MLA, normalize)
            attention(B, "dil", dil_groups(), AG_DIL,
                      lambda g, i, o: dve.tensor_copy(g["out"], o).then_inc(o_ready, 1))
            dve.tensor_tensor(bigm, mxd[:, :, 0, :], mxd[:, :, 1, :], ALU.max).then_inc(dve_link, 1)
            links[0] += 1
            dve.wait_ge(dve_link, links[0])
            link(dve.tensor_tensor(bigm, bigm, mxd[:, :, 2, :], ALU.max))
            dve.tensor_tensor(wd, mxd, bigm.unsqueeze(2).broadcast_to([P, M, DG, 4]), ALU.subtract).then_inc(wmx, 1)
            dve.wait_ge(wexp, 1)
            link(dve.tensor_tensor(dend, dend, wd, ALU.mult))
            link(dve.tensor_tensor(bigm, dend[:, :, 0, :], dend[:, :, 1, :], ALU.add))
            link(dve.tensor_tensor(bigm, bigm, dend[:, :, 2, :], ALU.add))
            link(dve.reciprocal(bigm, bigm))
            link(dve.tensor_tensor(wd, wd, bigm.unsqueeze(2).broadcast_to([P, M, DG, 4]), ALU.mult))
            dve.wait_ge(o_ready, AG_GQA)
            for m in range(M):
                for g in range(DG):
                    ins = dve.tensor_tensor(og[:, m, g, :, :], og[:, m, g, :, :], bc(wd[:, m, g, :], 64), ALU.mult)
            link(ins)

            def og4(m, g):
                return og[:, m, g, :, :].rearrange("p (b a) d -> p b a d", b=2)

            for m in range(M):
                o = ocat[:, m, 512:768].rearrange("p (a b d) -> p b a d", a=2, b=2)
                ins = dve.tensor_tensor(o, og4(m, 0), og4(m, 1), ALU.add)
            link(ins)
            for m in range(M):
                o = ocat[:, m, 512:768].rearrange("p (a b d) -> p b a d", a=2, b=2)
                ins = dve.tensor_tensor(o, o, og4(m, 2), ALU.add)
            ins.then_inc(src_ready, 1)
            square_T(B, B.plan.tb["ocat"], 3, oTl, oTh)
            out_steps(B, "wout", 1)
            norm_T(B, "n1", 1)
            ffn(B, "f0", 0, 1.0)
            norm_T(B, "n2", 2)
            for i in range(6):
                ahead(B, "gqkv", i)
            dve.wait_ge(gsq_act, 1)
            dve.wait_ge(gg_in, 16)
            link(dve.tensor_reduce(gms, gsq.rearrange("p m (h d) -> p (m h) d", d=64), AX_X, ALU.add))
            link(dve.tensor_scalar(gms, gms, 1.0 / 64, EPS, ALU.mult, ALU.add))
            dve.sem_inc(ms_ready, 1)
            powers[0] += 1
            dve.wait_ge(rstd_ready, powers[0])
            qk = gqkv[:, :, 0:1280].rearrange("p m (h d) -> p m h d", d=64)
            sq = gsq.rearrange("p m (h d) -> p m h d", d=64)
            gro = gr.rearrange("p m (h a d) -> p m h a d", h=20, a=2)
            for m in range(M):
                ins = dve.tensor_tensor(sq[:, m], qk[:, m], bc(grs.rearrange("p (m h) -> p m h", m=M)[:, m], 64), ALU.mult)
            link(ins)
            for m in range(M):
                for h0, n, gi in ((0, 16, 0), (16, 4, 1)):
                    gg = ggain[:, 64 * gi:64 * gi + 64].unsqueeze(1).broadcast_to([P, n, 64])
                    ins = dve.tensor_tensor(sq[:, m, h0:h0 + n], sq[:, m, h0:h0 + n], gg, ALU.mult)
            link(ins)
            for m in range(M):
                s5 = sq[:, m].rearrange("p h (a x f) -> p h a x f", a=2, x=2)
                o5 = gr[:, m, :].rearrange("p (h a x f) -> p h a x f", h=20, a=2, x=2)
                c2 = cos2[:, m].unsqueeze(1).broadcast_to([P, 20, 2, 16])
                n2 = sin2[:, m].unsqueeze(1).broadcast_to([P, 20, 2, 16])
                t1, t2 = (gt[:, i, :].rearrange("p (h a f) -> p h a f", h=20, a=2) for i in range(2))
                xa, xb = s5[:, :, :, 0, :], s5[:, :, :, 1, :]
                dve.tensor_tensor(t1, xa, c2, ALU.mult)
                link(dve.tensor_tensor(t2, xb, n2, ALU.mult))
                link(dve.tensor_tensor(o5[:, :, :, 0, :], t1, t2, ALU.subtract))
                dve.tensor_tensor(t1, xa, n2, ALU.mult)
                link(dve.tensor_tensor(t2, xb, c2, ALU.mult))
                link(dve.tensor_tensor(o5[:, :, :, 1, :], t1, t2, ALU.add))
            dve.sem_inc(src_ready, 1)
            tb = B.plan.tb["gqk"]
            for b in range(5):
                plain_T(B, tb + b, gqT[:, 2 * b:2 * b + 2, :] if b < 4 else gkT)
            attention(B, "gqa", gqa_groups(), AG_GQA, normalize)
            square_T(B, B.plan.tb["go"], 4, yl, yh)
            out_steps(B, "gwo", 3)
            norm_T(B, "n3", 3)
            ffn(B, "f1", 1, 1.0)

            def layer(l):
                B = Numbers(l)
                plan = B.plan
                norm_T(B, "n4", 5 + 3 * l)
                ffn(B, "fa", 2 + 2 * l, 0.5)
                norm_T(B, "n5", 6 + 3 * l)
                dve.wait_ge(lay_in, 64 * (l + 1))
                dve.wait_ge(tab2_in, 16)
                w0 = plan.step["win"]
                for i in range(17):
                    ahead(B, "win", i)
                    o = bank2(i % 2)
                    if WIN_DRAINS[i] == "D":
                        stepped(B, "win", i)
                        if i in (0, 1):
                            ins = dve.tensor_copy(kvd[:, i], o)
                        elif i == 6:
                            ins = dve.tensor_copy(rqk[:, 0:2, :], o)
                        elif i == 7:
                            ins = dve.tensor_scalar(rqk[:, 2:4, :], o, 0.125, None, ALU.mult)
                        elif i in (12, 13):
                            ins = dve.tensor_scalar(nq[:, 2 * i - 24:2 * i - 22, :], o, 0.125, None, ALU.mult)
                        elif i == 14:
                            ins = dve.tensor_copy(nk, o)
                        else:
                            ins = dve.tensor_copy(nv, o)
                        ins.then_inc(drain_dve, 1)
                    if i == 1:
                        dve.wait_ge(drain_dve, B.drained(w0 + 2, "D"))
                        for kv in range(2):
                            for g in range(2):
                                for par in range(2):
                                    r = slice(64 * par, 64 * par + 64)
                                    k3 = kvd[r, kv, g, :].rearrange("p (n l b) -> p l n b", l=8, b=2)[:, :, :, par]
                                    for hf in range(2):
                                        ins = dve.tensor_tensor(blk[r, kv, 8 * hf:8 * hf + 8, g, :], k3[:, :, hf:hf + NCMP],
                                                                bc(cpos[r, kv, 8 * hf:8 * hf + 8], NCMP), ALU.add)
                        ins.then_inc(blk_ready, 1)
                    if i == 5:
                        dve.wait_ge(hid_act, l + 1)
                        dve.tensor_copy(hidx, hid[:, 1, :].rearrange("p (g n) -> p g n", g=2).unsqueeze(2).broadcast_to([P, 2, 4, NCMP])).then_inc(hidx_ready, 1)
                        dve.wait_ge(drain_act, B.drained(w0 + 4, "A"))
                        for m in range(M):
                            ins = dve.bn_stats(st[:, m, :], vA[:, m, :])
                        link(ins)
                        for m in range(M):
                            ins = dve.bn_aggr(mv[:, m, :], st[:, m, :])
                        link(ins)
                        power(dve.tensor_scalar(ms[:, 0:2], mv[:, 0:2, 1], EPS, None, ALU.add))
                        for m in range(M):
                            ins = dve.tensor_scalar(vA[:, m, :], vA[:, m, :], mv[:, m, 0:1], rstd[:, m:m + 1], ALU.subtract, ALU.mult)
                        link(ins)
                        for c0, op in ((0, ALU.mult), (512, ALU.add)):
                            for m in range(M):
                                ins = dve.tensor_tensor(vA[:, m, :], vA[:, m, :], lng[:, c0:c0 + 512], op)
                            link(ins)
                        dve.tensor_tensor(gmws, gmws, trilT.unsqueeze(1).broadcast_to([P, 4, P]), ALU.mult).then_inc(gm_ready, 1)
                    if i == 8:
                        dve.wait_ge(kc_done, l + 1)
                        dve.tensor_copy(kcs, pb[3][:, 0:NCMP])
                        dve.tensor_copy(bdrow, pb[4][0:120, 0:64]).then_inc(kc_ready, 1)
                dve.wait_ge(gm_done, l + 1)
                dve.wait_ge(drain_act, B.drained(w0 + 6, "A"))
                for m in range(M):
                    for g in range(4):
                        c = slice(g * P, g * P + P)
                        ins = dve.scalar_tensor_tensor(out=uA[:, m, c], in0=pb[4 + m][:, c], scalar=gmbs[:, g:g + 1], in1=uA[:, m, c],
                                                       op0=ALU.add, op1=ALU.mult)
                ins.then_inc(ya_ready, 1)
                dve.wait_ge(kc_ready, l + 1)
                dve.tensor_tensor(bd[0:120], bdrow.unsqueeze(1).broadcast_to([120, HN, 64]), bc(blockm[0:120, :], 64), ALU.mult)
                for h in range(HR):
                    dve.wait_ge(rs_done, HR * l + h + 1)
                    if h >= 2:
                        dve.wait_ge(ro_done, HR * l + h - 1)
                    dve.tensor_tensor(rs[h % 2][:, 0:S], pb[2 + h % 2][:, 0:S], rdec[:, h, :], ALU.mult)
                    dve.tensor_tensor(rs[h % 2][:, S:S + P], pb[2 + h % 2][:, S:S + P], rdec[:, h, 0:P], ALU.mult).then_inc(rs_ready, 1)
                dve.wait_ge(ro_done, HR * l + HR)
                for m in range(M):
                    for h in range(HR):
                        ins = dve.bn_stats(st[:, 4 * m + h, :], pb[4 + m][:, h * P:h * P + P])
                link(ins)
                for j in range(8):
                    ins = dve.bn_aggr(mv[:, j, :], st[:, j, :])
                link(ins)
                power(dve.tensor_scalar(ms[:, 0:8], mv[:, :, 1], EPS, None, ALU.add))
                r0 = P2[1]
                r1 = r0.rearrange("p a n -> p (a n)").rearrange("p (m n) -> p m n", m=M)
                for m in range(M):
                    for h in range(HR):
                        j = 4 * m + h
                        ins = dve.tensor_scalar(r1[:, m, h * P:h * P + P], pb[4 + m][:, h * P:h * P + P], mv[:, j, 0:1], rstd[:, j:j + 1],
                                                ALU.subtract, ALU.mult)
                link(ins)
                for c0, op in ((1024, ALU.mult), (1536, ALU.add)):
                    for m in range(M):
                        ins = dve.tensor_tensor(r1[:, m, :], r1[:, m, :], lng[:, c0:c0 + 512], op)
                    link(ins)
                dve.wait_ge(drain_act, B.drained(w0 + 12, "A"))
                dve.tensor_tensor(rg, rg, r1, ALU.mult).then_inc(yb_ready, 1)
                dve.wait_ge(drain_act, B.drained(w0 + 17, "A"))
                ngf = ng.rearrange("p m g r b -> p (m g r b)")
                link(dve.tensor_scalar(ngf, ngf, 1.0, None, ALU.add))
                link(dve.reciprocal(ngf, ngf))
                cden = st.rearrange("p a b -> p (a b)")[:, 0:16].rearrange("p (m h) -> p m h", m=M)
                cmx = st.rearrange("p a b -> p (a b)")[:, 16:32].rearrange("p (m h) -> p m h", m=M)
                cp = [P2[0][:, m, 0:120].rearrange("p (h n) -> p h n", h=HN) for m in range(M)]
                for m in range(M):
                    dve.wait_ge(cs_done, 4 * l + 2 * m + 2)
                    link(dve.tensor_tensor(cp[m], pb[2 + m][:, 0:120].rearrange("p (h n) -> p h n", h=HN), cbias[:, m], ALU.add))
                    link(dve.tensor_reduce(cmx[:, m, :], cp[m], AX_X, ALU.max))
                    link(dve.tensor_scalar(cmx[:, m, :], cmx[:, m, :], -1e29, None, ALU.max))
                    dve.tensor_tensor(cp[m], cp[m], bc(cmx[:, m, :], NCMP), ALU.subtract).then_inc(cs_ready, 1)
                    if m == 0:
                        ahead(B, "gates", 0)

                def gate_drain(i):
                    stepped(B, "gates", i)
                    dve.wait_ge(bm_in[i % 2], 16 * (6 * l + i // 2 + 1))
                    dve.tensor_tensor(gates[:, :, 256 * i:256 * i + 256], bank2(0), bm[i % 2].unsqueeze(1).broadcast_to([P, M, 256]), ALU.add).then_inc(drain_dve, 1)

                gate_drain(0)
                ahead(B, "gates", 1)
                tb = plan.tb["cmp"]
                dve.wait_ge(tb_done, B.tb0 + tb + 2)
                dve.tensor_copy(PT2[0][0:120, 1, 0, :], pb[B.bank(tb + 1)][0:120, 0:P]).then_inc(tb_dve, 1)
                for m in range(M):
                    dve.wait_ge(ce_ready, M * l + m + 1)
                    link(dve.tensor_reduce(cden[:, m, :], cp[m], AX_X, ALU.add))
                    link(dve.tensor_scalar(cden[:, m, :], cden[:, m, :], 1e-30, None, ALU.max))
                    link(dve.reciprocal(cden[:, m, :], cden[:, m, :]))
                    link(dve.tensor_tensor(cden[:, m, :].rearrange("p (g r) -> p g r", g=2), cden[:, m, :].rearrange("p (g r) -> p g r", g=2),
                                           ng[:, m, :, :, 0], ALU.mult))
                gate_drain(1)
                for m in range(M):
                    dve.wait_ge(co_done, M * l + m + 1)
                    dve.tensor_tensor(vA[:, m, :].rearrange("p (h d) -> p h d", h=HN), pb[4 + m].rearrange("p (h d) -> p h d", h=HN),
                                      bc(cden[:, m, :], 64), ALU.mult).then_inc(yc_ready, 1)
                dve.wait_ge(yc_ready, 3 * l + 2)

                def gated(g, i, o):
                    link(dve.reciprocal(rec, den[:, i % 4, :]))
                    link(dve.tensor_tensor(rec, rec, g["gate"], ALU.mult))
                    link(dve.tensor_tensor(og2, o, bc(rec, 64), ALU.mult))
                    link(dve.tensor_tensor(g["out"], g["out"], og2, ALU.add))
                    dve.sem_inc(o_ready, 1)

                attention(B, "nsa", nsa_groups(), AG_NSA + 8 * l, gated,
                          lambda i: ahead(B, "gates", 2 + i), lambda i: gate_drain(2 + i))
                dve.sem_inc(yc_ready, 1)
                tb = plan.tb["y"]
                square_T(B, tb, 2, aTl, aTh)
                square_T(B, tb + 2, 2, bTl, bTh)
                square_T(B, tb + 4, 2, cTl, cTh)
                b0 = plan.step["branch"]
                for i in range(12):
                    ahead(B, "branch", i, 2)
                    stepped(B, "branch", i)
                    dve.wait_ge(sig_done, 3 * l + i // 4 + 1)
                    c = slice(256 * (i % 4), 256 * (i % 4) + 256)
                    gs = gates[:, :, 256 * i:256 * i + 256]
                    if i < 4:
                        dve.tensor_tensor(y[:, :, c], bank2(i % 2), gs, ALU.mult).then_inc(drain_dve, 1)
                    else:
                        dve.tensor_tensor(gs, bank2(i % 2), gs, ALU.mult).then_inc(drain_dve, 1)
                        dve.wait_ge(drain_dve, B.drained(b0 + i + 1, "D"))
                        link(dve.tensor_tensor(y[:, :, c], y[:, :, c], gs, ALU.add))
                dve.sem_inc(mix_ready, 1)
                dve.sem_inc(layer_done, 1)
                square_T(B, plan.tb["mix"], 4, yl, yh)
                out_steps(B, "wo", 7 + 3 * l)
                norm_T(B, "n6", 7 + 3 * l)
                ffn(B, "fb", 3 + 2 * l, 0.5)

            norm(4, x)
            dve.wait_ge(y_ready, 10)
            dve.sem_inc(x_ready, 1)
            for l in range(LAYERS):
                layer(l)
            norm(11)
            dve.wait_ge(y_ready, 24)
            dve.sem_inc(out_ready, 1)
    return nc


def weight_tile(parts, k_rows):
    w = np.concatenate(parts, 1)
    kc = k_rows // P
    t = w.reshape(kc, P, -1).transpose(1, 0, 2).reshape(P, -1)
    out = np.zeros((P, TILE), w.dtype)
    out[:, :t.shape[1]] = t
    return out


def weight_stream(a):
    tiles = []

    def cols(w, starts, n=256):
        for c in starts:
            tiles.append(weight_tile([w[:, c:c + n]], w.shape[0]))

    def ffn(w1, w2):
        def up(j):
            tiles.append(weight_tile([w1[:, P * j:P * j + P], w1[:, FF + P * j:FF + P * j + P]], D))

        def down(i):
            tiles.append(weight_tile([w2[2 * P * i:2 * P * i + 2 * P]], 2 * P))
        up(0)
        up(1)
        for i in range(1, NF // 2):
            up(2 * i)
            up(2 * i + 1)
            down(i - 1)
        down(NF // 2 - 1)

    w = a["w_in_ab"][0]
    cols(w, (0, 256))
    cols(w, (512,))
    cols(w, range(672, 2976, 256))
    w = a["mla_w_uq"][0].reshape(RQ, -1)
    cols(w, (0, 512), 512)
    cols(a["mla_w_ukv"][0].reshape(RKV, -1), (0,), 1024)
    cols(a["w_out_ab"][0], range(0, D, 256))
    ffn(a["ffn_w_in"][0], a["ffn_w_out"][0])
    order = [4 * (2 * (c // 4) + b) + c % 4 for c in range(8) for b in range(2)]
    wq = a["gqa_w_q"][0].reshape(D, H2, 64)[:, order].reshape(D, D)
    cols(wq, range(0, D, 256))
    cols(a["gqa_w_kv"][0], (0, 256))
    cols(a["gqa_w_o"][0].reshape(H2, 64, D)[order].reshape(D, D), range(0, D, 256))
    ffn(a["ffn_w_in"][1], a["ffn_w_out"][1])
    for l in range(LAYERS):
        ffn(a["ffn1_w1_2"][l], a["ffn1_w2_2"][l])
        w = a["w_in_2"][l]

        def part(c, n=64):
            return w[:, c:c + n]
        for c in (3072, 3200):
            tiles.append(weight_tile([part(c), part(c), part(c + 64), part(c + 64)], D))
        cols(w, (512, 768, 0, 256, 1024, 1280, 1536, 1792, 2048, 2304))
        for j in (0, 2):
            tiles.append(weight_tile([part(2560 + 64 * h) for h in (j, j + 4, j + 1, j + 5)], D))
        tiles.append(weight_tile([part(3328, P), part(3584, P)], D))
        tiles.append(weight_tile([part(3456, P), part(3712, P)], D))
        gl = np.zeros((D, 256), w.dtype)
        gl[:, :24] = w[:, 3840:3864]
        tiles.append(weight_tile([gl], D))
        cols(a["w_merge_gate_2"][l], range(0, 3 * D, 256))
        for i in range(3):
            cols(a["w_branch_out_2"][l, i], (0, 512), 512)
        cols(a["w_o_2"][l], range(0, D, 256))
        ffn(a["ffn2_w1_2"][l], a["ffn2_w2_2"][l])
    tiles += [np.zeros((P, TILE), np.float32)] * 2
    assert len(tiles) == TILES
    return np.stack(tiles)


def everywhere(v):
    return np.ascontiguousarray(np.broadcast_to(v.reshape(1, -1), (P, v.size)))


def layer_small(a, l):
    ws = a["gm_ws_2"][l].transpose(2, 0, 1).reshape(P, -1)
    bs = a["gm_bs_2"][l].T
    w2 = a["cmp_w2_2"][l].transpose(1, 0, 2).reshape(P, -1)
    pos = a["cmp_pos_2"][l].reshape(2, 16, P).transpose(2, 0, 1).reshape(P, -1)
    w1 = a["cmp_w1_2"][l].reshape(2, 16, P, P).transpose(2, 0, 1, 3).reshape(P, -1)
    return np.concatenate([ws, bs, w2, pos, w1, everywhere(a["b_merge_gate_2"][l])], 1)


def kernel(**inputs):
    import concourse.bacc as _bacc
    from concourse.bass_utils import run_bass_kernel_spmd as _run

    a = {k: np.asarray(v) for k, v in inputs.items()}
    misc, dil, second = tables()
    norms = [a["mix_norm_ab"][0], a["ffn_norm"][0], a["mix_norm_c"][0], a["ffn_norm"][1], a["final_norm"]]
    for l in range(LAYERS):
        norms += [a["ffn1_norm_2"][l], a["mix_norm_2"][l], a["ffn2_norm_2"][l]]
    norms.append(a["final_norm_2"])
    arrays = {
        "stream": weight_stream(a),
        "xin": np.ascontiguousarray(a["x"].reshape(M, P, D).transpose(1, 0, 2)),
        "misc": misc, "dilb": dil, "second": second,
        "gains": np.stack([everywhere(g) for g in norms]),
        "mlag": everywhere(np.concatenate([a["mla_q_norm"][0], a["mla_kv_norm"][0], a["gqa_q_norm"][0], a["gqa_k_norm"][0]])),
        "small": np.stack([layer_small(a, l) for l in range(LAYERS)]),
        "rows": np.stack([everywhere(np.concatenate([a[k][l] for k in ("gm_ln_g_2", "gm_ln_b_2", "ret_gn_g_2", "ret_gn_b_2")]))
                          for l in range(LAYERS)]),
    }
    nc = _bacc.Bacc("TRN2", target_bir_lowering=False, num_devices=1)
    d = {k: nc.dram_tensor(k, v.shape, F32, kind="ExternalInput").ap() for k, v in arrays.items()}
    out = nc.dram_tensor("out", (P, M, D), F32, kind="ExternalOutput").ap()
    build(nc, d["stream"], d["xin"], d["misc"], d["dilb"], d["second"], d["gains"], d["mlag"], d["small"], d["rows"], out)
    r = _run(nc, [arrays], core_ids=[0])
    return np.ascontiguousarray(r.results[0]["out"].transpose(1, 0, 2).reshape(1, S, D))
```

```python
from contextlib import ExitStack

import concourse.bass as bass
import numpy as np
from concourse import mybir

F32 = mybir.dt.float32
F32R = mybir.dt.float32r
ALU = mybir.AluOpType
ACT = mybir.ActivationFunctionType
AX_X = mybir.AxisListType.X

P = 128
S = 256
D = 1024
M = S // P
KC = D // P
TILE = 2048
EPS = 1e-6
NEG = -1e30
H1, DK1, ROPE1 = 8, 96, 32
RQ, RKV = 384, 256
DG, DS = 3, 4
H2, G2 = 16, 4
FF = 2816
NF = FF // P
FFN_TILES = NF + NF // 2
FFN_ROUNDS = (NF // 2 - 3) // 2
LINKS = 73
POWERS_GQA = 6
POWERS = 7
SLOT_HEADS = (0, 2, 1, 3)
HN, NCMP = 8, 15
HR = 4
LAYERS = 2


class Plan:

    def __init__(self):
        self.tile, self.step, self.act, self.dve, self.tb = {}, {}, {}, {}, {}
        self.tiles = 0
        self.last_step = []
        self.drains = []
        self.copies = []

    def weights(self, name, drains, steps_per_tile=1):
        self.tile[name], self.step[name] = self.tiles, len(self.drains)
        for i, who in enumerate(drains):
            if i % steps_per_tile == 0:
                self.tiles += 1
                self.last_step.append(len(self.drains))
            self.last_step[-1] = len(self.drains)
            self.drains.append(who)

    def batches(self, name, who):
        self.tb[name] = len(self.copies)
        self.copies += who


def ffn_drains():
    return "DD" + "DD-" * (NF // 2 - 1) + "-"


PLAN1 = Plan()
PLAN1.batches("n0", "BBBB")
PLAN1.weights("z", "A" * 12)
PLAN1.batches("cq", "BBB")
PLAN1.weights("uq", "DDD", 2)
PLAN1.weights("ukv", "AAAA", 4)
PLAN1.batches("mqk", "ADADADAD")
PLAN1.batches("mla", "ADADADAD")
PLAN1.batches("dil", "ADADADADADAD")
PLAN1.batches("ocat", "BBB")
PLAN1.weights("wout", "DDDD")
PLAN1.batches("n1", "BBBB")
PLAN1.weights("f0", ffn_drains())
PLAN1.batches("n2", "BBBB")
PLAN1.weights("gqkv", "AAAAAA")
PLAN1.batches("gqk", "ADADA")
PLAN1.batches("gqa", "ADADADADADADADAD")
PLAN1.batches("go", "BBBB")
PLAN1.weights("gwo", "DDDD")
PLAN1.batches("n3", "BBBB")
PLAN1.weights("f1", ffn_drains())

PLAN2 = Plan()
PLAN2.batches("n4", "BBBB")
PLAN2.weights("fa", ffn_drains())
PLAN2.batches("n5", "BBBB")
WIN_DRAINS = "DDAAAADDAAAADDDDA"
PLAN2.weights("win", WIN_DRAINS)
PLAN2.batches("cmp", "AD")
PLAN2.weights("gates", "A" * 12)
PLAN2.batches("ya", "BB")
PLAN2.batches("nsa", "ADADADADADAD")
PLAN2.batches("y", "BBBB")
PLAN2.weights("branch", "D" * 12, 2)
PLAN2.weights("wo", "DDDD")
PLAN2.batches("n6", "BBBB")
PLAN2.weights("fb", ffn_drains())
TILES = PLAN1.tiles + LAYERS * PLAN2.tiles + 2
assert PLAN2.tiles % 3 == 0 and len(PLAN2.copies) % 2 == 0


class Numbers:

    def __init__(self, l=None):
        self.l = l
        self.plan = PLAN1 if l is None else PLAN2
        p1, p2 = PLAN1, PLAN2
        k = 0 if l is None else l

        def base(a, b):
            return 0 if l is None else a + b * k

        self.tile0_third = base(p1.tiles // 3, p2.tiles // 3)
        self.tile0_slot = 0 if l is None else p1.tiles % 3
        self.step0 = base(len(p1.drains), len(p2.drains))
        self.act0 = base(p1.drains.count("A"), p2.drains.count("A"))
        self.dve0 = base(p1.drains.count("D"), p2.drains.count("D"))
        self.tb0 = base(len(p1.copies), len(p2.copies))
        self.tb0_parity = 0 if l is None else len(p1.copies) % 2
        self.tb_act0 = base(len(p1.copies) - p1.copies.count("D"), len(p2.copies) - p2.copies.count("D"))
        self.tb_dve0 = base(len(p1.copies) - p1.copies.count("A"), len(p2.copies) - p2.copies.count("A"))

    def later(self, pairs):
        out = Numbers(self.l)
        out.tile0_third = self.tile0_third + 2 * pairs
        out.step0 = self.step0 + 6 * pairs
        out.dve0 = self.dve0 + 4 * pairs
        return out

    def slot(self, tile):
        return (self.tile0_slot + tile) % 3

    def landed(self, tile):
        return 16 * (self.tile0_third + (self.tile0_slot + tile) // 3 + 1)

    def tile_no(self, tile):
        return 3 * self.tile0_third + self.tile0_slot + tile

    def last_step(self, tile):
        if tile < 0:
            return tile
        return self.plan.last_step[tile] if tile < self.plan.tiles else len(self.plan.drains) + tile - self.plan.tiles

    def drained(self, step, who):
        n = "".join(self.plan.drains)[:max(step, 0)].count(who)
        return (self.act0 if who == "A" else self.dve0) + n

    def copied(self, tb, who):
        other = "D" if who == "A" else "A"
        copies = self.plan.copies
        if tb < 0:
            return (self.tb_act0 if who == "A" else self.tb_dve0) + tb
        return (self.tb_act0 if who == "A" else self.tb_dve0) + sum(c != other for c in copies[:tb])

    def bank(self, tb):
        return 6 + (self.tb0_parity + tb) % 2

    def quarters(self, stage):
        order = ((0, 0), (0, 1), (1, 0), (1, 1)) if stage in ("n0", "n2") else ((0, 0), (1, 0), (0, 1), (1, 1))
        tb = self.plan.tb[stage]
        return [(tb + j, m, q, self.bank(tb + q) if m == 0 else 2 + q) for j, (m, q) in enumerate(order)]


AG_MLA, AG_DIL, AG_GQA, AG_NSA = 0, 4, 10, 18



def tables():
    f32 = np.float32
    t = np.arange(S)

    def rope(pos, dim):
        freqs = (f32(10000.0) ** (-np.arange(0, dim, 2, dtype=f32) / f32(dim))).astype(f32)
        ang = (pos.astype(f32)[:, None] * freqs[None, :]).astype(f32)
        return np.cos(ang).astype(f32), np.sin(ang).astype(f32)

    def halves(a):
        return np.swapaxes(a.reshape(M, P, *a.shape[1:]), 0, 1)

    c, s = rope(t, ROPE1)
    cr, sr = rope(t // 64, 32)
    cc, sc = rope(t % 64, 32)
    gc, gs = np.stack([cr, cc], 1), np.stack([sr, sc], 1)
    misc = np.concatenate([np.eye(P, dtype=f32), halves(c).reshape(P, -1), halves(s).reshape(P, -1),
                           halves(gc).reshape(P, -1), halves(gs).reshape(P, -1)], 1)

    q = np.arange(P)[:, None]
    k = np.arange(3 * P)[None, :] - P
    slopes = np.exp2(f32(-8.0) * np.arange(1, 13, dtype=f32) / f32(12))
    dil = np.empty((P, 12, 3 * P), f32)
    for i in range(12):
        h = i // 4 * 4 + SLOT_HEADS[i % 4]
        d = (1, 4, 16)[h // 4]
        dist = np.abs(k - q)
        ok = (dist % d == 0) & (dist <= 64 * d)
        dil[:, i] = np.where(ok, -slopes[h] * dist.astype(f32), f32(NEG))

    sl = (f32(2.0) ** (f32(-8.0) * np.arange(1, 9, dtype=f32) / f32(8))).astype(f32)
    k = np.arange(2 * P)[None, :] - P
    nsa = np.empty((P, 8, 2 * P), f32)
    for h in range(8):
        dist = q - k
        nsa[:, h] = np.where(dist >= 0, -sl[h] * dist.astype(f32), f32(NEG))
    end = np.arange(NCMP) * 16 + 31
    dist = t[:, None, None] - end[None, None, :]
    cb = np.where(dist >= 0, -sl[None, :, None] * dist.astype(f32), f32(NEG)).astype(f32)
    cb = halves(cb).reshape(P, -1)
    log_gamma = np.log(1.0 - 2.0 ** (-5.0 - np.arange(HR)))
    j = np.arange(P)[:, None]
    i = np.arange(2 * P)[None, :]
    ret = np.stack([np.where(i >= j, np.exp(g * np.maximum(i - j, 0)), 0.0) for g in log_gamma], 1).astype(f32)
    block = np.zeros((P, HN), f32)
    for h in range(HN):
        block[h * NCMP:(h + 1) * NCMP, h] = 1.0
    tril_t = np.triu(np.ones((P, P), f32))
    second = np.concatenate([nsa.reshape(P, -1), ret.reshape(P, -1), cb, block, tril_t], 1)
    return misc, dil.reshape(P, -1), second


def build(nc, stream, xin, misc, dilb, second, gains, mlag, small, rows, out):
    ctx = ExitStack()
    with ctx:
        base = [16896]

        def gain_no(n):
            return n if type(n) is int and n < 5 else n - 1

        def at(name, off, cols, dt=F32, shape=None):
            t = nc.alloc_sbuf_tensor_at(name, [P, cols], dt, offset=base[0] + off)
            a = t[:, :]
            if shape:
                names = "abcdef"[:len(shape)]
                a = a.rearrange(f"p ({' '.join(names)}) -> p {' '.join(names)}", **dict(zip(names, shape)))
            return a

        K = 1024
        ctx.enter_context(nc.sbuf_tensor("fence", [P, 207 * 256], F32))
        raw = [at(f"raw{i}", 8 * K * i, TILE) for i in range(3)]
        whi = [at(f"whi{i}", 24 * K + 8 * K * i, TILE, F32R) for i in range(3)]
        wlo = [at(f"wlo{i}", 48 * K + 8 * K * i, TILE, F32R) for i in range(3)]
        x = at("x", 72 * K, M * D, shape=(M, D))
        y = at("y", 80 * K, M * D, shape=(M, D))
        yh = at("yh", 88 * K, KC * S, F32R, (KC, S))
        yl = at("yl", 96 * K, KC * S, F32R, (KC, S))
        gbc = at("gbc", 104 * K, D)
        CM = 108 * K
        misc_sb = at("misc", CM, 128 + 64 + 128)
        ident = misc_sb[:, 0:128]
        cos1 = misc_sb[:, 128:160].rearrange("p (m f) -> p m f", m=M)
        sin1 = misc_sb[:, 160:192].rearrange("p (m f) -> p m f", m=M)
        cos2 = misc_sb[:, 192:256].rearrange("p (m a f) -> p m a f", m=M, a=2)
        sin2 = misc_sb[:, 256:320].rearrange("p (m a f) -> p m a f", m=M, a=2)
        off = [CM + 1280]

        def little(name, cols, shape=None):
            a = at(name, off[0], cols, F32, shape)
            off[0] += -(-cols * 4 // 32) * 32
            assert off[0] <= 111 * K
            return a

        ss = little("ss", 8, (2, 4))
        ms = little("ms", 24)
        rstd = little("rstd", 24)
        half = little("half", 24)
        mx = little("mx", 8, (2, 4))
        nmx = little("nmx", 8, (2, 4))
        den = little("den", 16, (4, 4))
        rec = little("rec", 4)
        idle = little("idle", 1)
        warm = little("warm", 1)
        st = little("st", 8 * 6, (8, 6))
        mv = little("mv", 8 * 2, (8, 2))
        A = 111 * K
        dbias = at("dbias", A, 12 * 384, shape=(12, 384))
        zA = at("zA", A + 18 * K, M * 672, shape=(M, 672))
        dqk = at("dqk", A + 24 * K, 12 * S, shape=(12, S))
        dv = at("dv", A + 36 * K, M * 768, shape=(M, 768))
        kvTh = at("kvTh", A + 42 * K, 2 * S, F32R, (2, S))
        kvTl = at("kvTl", A + 44 * K, 2 * S, F32R, (2, S))
        cqTh = at("cqTh", 80 * K, 3 * S, F32R, (3, S))
        cqTl = at("cqTl", 83 * K, 3 * S, F32R, (3, S))
        mq = at("mq", A + 46 * K, M * 768, shape=(M, H1, DK1))
        mkv = at("mkv", A + 52 * K, M * 1024, shape=(M, H1, 128))
        kasm = at("kasm", A + 60 * K, M * 768, shape=(M, H1, DK1))
        mqT = at("mqT", A + 66 * K, H1 * S, shape=(H1, S))
        mkT = at("mkT", A + 74 * K, H1 * S, shape=(H1, S))
        kr = at("kr", A + 94 * K, M * 32, shape=(M, 32))
        rt = at("rt", A + 82 * K, 4 * 256, shape=(4, 256))
        mlagain = at("mlagain", A + 90 * K, 640)
        P0 = [at(f"p0_{i}", A + 82 * K + 4 * K * i, 1024, shape=(4, S)) for i in range(2)]
        PT0 = [at(f"pt0_{i}", A + 42 * K + 4 * K * i, 1024, shape=(4, M, P)) for i in range(2)]
        ocat = at("ocat", A + 60 * K, M * 768, shape=(M, 768))
        og = at("og", A + 18 * K, M * DG * 256, shape=(M, DG, 4, 64))
        mxd = at("mxd", A + 93 * K, M * DG * 4, shape=(M, DG, 4))
        dend = at("dend", A + 93 * K + 128, M * DG * 4, shape=(M, DG, 4))
        wd = at("wd", A + 93 * K + 256, M * DG * 4, shape=(M, DG, 4))
        bigm = at("bigm", A + 93 * K + 384, M * 4, shape=(M, 4))
        oTh = at("oTh", 88 * K, 6 * S, F32R, (6, S))
        oTl = at("oTl", 96 * K, 6 * S, F32R, (6, S))
        gqkv = at("gqkv", A, M * 1536, shape=(M, 1536))
        gsq = [at(f"gsq{i}", A + 12 * K + 2 * K * i, M * S, shape=(M, S)) for i in range(2)]
        gr = at("gr", A + 22 * K, M * 1280, shape=(M, 1280))
        gqT = at("gqT", A + 32 * K, 8 * S, shape=(8, S))
        gkT = at("gkT", A + 40 * K, 2 * S, shape=(2, S))
        P1 = [at(f"p1_{i}", A + 42 * K + 4 * K * i, 1024, shape=(4, S)) for i in range(2)]
        PT1 = [at(f"pt1_{i}", A + 50 * K + 4 * K * i, 1024, shape=(4, M, P)) for i in range(2)]
        go = at("go", A + 58 * K, M * D, shape=(M, D))
        gn = [at(f"gn{i}", A + 66 * K + 2 * K * i, M * S, shape=(M, S)) for i in range(2)]
        gtv = at("gtv", A + 70 * K, 2 * S, shape=(2, M, 8, 16))
        gtp = at("gtp", A + 78 * K, 2 * S, shape=(2, M, 8, 16))
        gtab = [at(f"gtab{i}", A + o * K, 4 * S, shape=(4, M, 8, 16)) for i, o in ((0, 16), (1, 74))]
        gms = at("gms", A + 72 * K, 40)
        grs = at("grs", A + 72 * K + 256, 40)
        ghalf = at("ghalf", A + 72 * K + 512, 40)
        ggain = at("ggain", A + 73 * K, 128)
        hh = [at(f"hh{i}", A + 80 * K + 2 * K * i, 2 * S, F32R, (2, S)) for i in range(2)]
        hl = [at(f"hl{i}", A + 84 * K + 2 * K * i, 2 * S, F32R, (2, S)) for i in range(2)]
        sg = [at(f"sg{i}", A + 88 * K + K * i, S) for i in range(2)]
        h32 = [at(f"h32{i}", A + 90 * K + K * i, S) for i in range(2)]
        NB2 = 2048 + 1024 + 240 + 8 + 128
        tab2 = at("tab2", A, NB2)
        nbias = tab2[:, 0:2048].rearrange("p (h k) -> p h k", h=8)
        rdec = tab2[:, 2048:3072].rearrange("p (h k) -> p h k", h=4)
        cbias = tab2[:, 3072:3312].rearrange("p (m h n) -> p m h n", m=M, h=HN)
        blockm = tab2[:, 3312:3320]
        trilT = tab2[:, 3320:3448]
        lng = at("lng", A + 14 * K, 2048)
        hmb = at("hmb", A + 22 * K, 24)
        gbc5 = at("gbc5", A + 14 * K, D)
        gmws = at("gmws", A + 24 * K, 512, shape=(4, P))
        bd = at("bd", A + 24 * K, 512, shape=(HN, 64))
        sm2 = at("sm2", A + 26 * K, 4 + 128 + 32 + 24)
        gmbs, cw2, cpos = sm2[:, 0:4], sm2[:, 4:132].rearrange("p (i d) -> p i d", i=2), sm2[:, 132:164].rearrange("p (i l) -> p i l", i=2)
        mb = sm2[:, 164:188]
        uA = at("uA", A + 27 * K, M * 512, shape=(M, 512))
        vA = at("vA", A + 31 * K, M * 512, shape=(M, 512))
        rqk = at("rqk", A + 35 * K, 4 * S, shape=(4, S))
        rv = at("rv", A + 39 * K, M * 512, shape=(M, 512))
        rg = at("rg", A + 43 * K, M * 512, shape=(M, 512))
        nq = at("nq", A + 47 * K, 4 * S, shape=(4, S))
        nk = at("nk", A + 51 * K, 2 * S, shape=(2, S))
        nv = at("nv", A + 53 * K, M * S, shape=(M, S))
        gates = at("gates", A + 55 * K, 24 * S, shape=(24, S))
        mix = at("mix", 80 * K, KC * S, shape=(KC, S))
        cw1 = at("cw1", A + 55 * K, 2 * TILE, shape=(2, 16, P))
        P2 = [at(f"p2_{i}", A + 79 * K + 4 * K * i, 1024, shape=(4, S)) for i in range(2)]
        PT2 = [at(f"pt2_{i}", A + 87 * K + 4 * K * i, 1024, shape=(4, M, P)) for i in range(2)]
        kvd = at("kvd", A + 87 * K, 4 * S, shape=(2, 2, S))
        blk = at("blk", A + 91 * K, 2 * 16 * 30, shape=(2, 16, 2, NCMP))
        rnorm = at("rnorm", 80 * K, M * 512, shape=(M, 512))
        rs = [at(f"rs{i}", A + 79 * K + 2 * K * i, 384) for i in range(2)]
        aTh = at("aTh", A + 35 * K, 4 * S, F32R, (4, S))
        aTl = at("aTl", A + 39 * K, 4 * S, F32R, (4, S))
        bTh = at("bTh", A + 87 * K, 4 * S, F32R, (4, S))
        bTl = at("bTl", A + 91 * K, 4 * S, F32R, (4, S))
        cTh = at("cTh", A + 79 * K, 4 * S, F32R, (4, S))
        cTl = at("cTl", A + 83 * K, 4 * S, F32R, (4, S))
        L2 = A + 95 * K
        hidT = at("hidT", A + 23 * K, 2 * P, shape=(2, P))
        hid = at("hid", L2, 60, shape=(2, 30))
        hidx = at("hidx", L2 + 256, 120, shape=(2, 4, NCMP))
        kcs = at("kcs", L2 + 736, NCMP)
        ng = at("ng", L2 + 800, M * 24, shape=(M, 2, 4, 3))
        bdrow = at("bdrow", A + 13 * K + 512, 64)[0:120, :]
        og2 = at("og2", A + 23 * K, 256, shape=(4, 64))
        pb = [ctx.enter_context(nc.psum_tensor(f"bank{i}", [P, 512], F32))[:, :] for i in range(8)]

        def sem(name):
            return ctx.enter_context(nc.semaphore(name))

        landed = [sem(f"landed{i}") for i in range(3)]
        hi_made = sem("hi_made")
        lo_made = sem("lo_made")
        step_done = sem("step_done")
        drain_act = sem("drain_act")
        drain_dve = sem("drain_dve")
        tb_done = sem("tb_done")
        tb_act = sem("tb_act")
        tb_dve = sem("tb_dve")
        x_ready = sem("x_ready")
        x_in = [sem("x_in0"), sem("x_in1")]
        tab_in = sem("tab_in")
        mlag_in = sem("mlag_in")
        dilb_in = sem("dilb_in")
        gg_in = sem("gg_in")
        tab2_in = sem("tab2_in")
        gain_in = sem("gain_in")
        gain0_in = sem("gain0_in")
        gain5_in = sem("gain5_in")
        lay_in = sem("lay_in")
        half_set = sem("half_set")
        ss_act = sem("ss_act")
        ms_ready = sem("ms_ready")
        rstd_ready = sem("rstd_ready")
        y_ready = sem("y_ready")
        src_ready = sem("src_ready")
        sc_done = sem("sc_done")
        mx_ready = sem("mx_ready")
        p_ready = sem("p_ready")
        o_done = sem("o_done")
        o_ready = sem("o_ready")
        h_ready = sem("h_ready")
        silu_done = sem("silu_done")
        hh_made = sem("hh_made")
        acc_done = sem("acc_done")
        gtab_ready = sem("gtab_ready")
        gn_ready = sem("gn_ready")
        gtp_ready = sem("gtp_ready")
        gr_pool = sem("gr_pool")
        gr_dve = sem("gr_dve")
        wexp = sem("wexp")
        wmx = sem("wmx")
        blk_ready = sem("blk_ready")
        hid_done = sem("hid_done")
        hid_act = sem("hid_act")
        hidt_done = sem("hidt_done")
        hidx_ready = sem("hidx_ready")
        kc_done = sem("kc_done")
        kc_ready = sem("kc_ready")
        gm_ready = sem("gm_ready")
        gm_done = sem("gm_done")
        ya_ready = sem("ya_ready")
        rs_done = sem("rs_done")
        rs_ready = sem("rs_ready")
        ro_done = sem("ro_done")
        ro_used = sem("ro_used")
        yb_ready = sem("yb_ready")
        cs_done = sem("cs_done")
        cs_ready = sem("cs_ready")
        ce_ready = sem("ce_ready")
        co_done = sem("co_done")
        yc_ready = sem("yc_ready")
        mix_pool = sem("mix_pool")
        mix_sum = sem("mix_sum")
        mixh_made = sem("mixh_made")
        mix_ready = sem("mix_ready")
        pool_link = sem("pool_link")
        layer_done = sem("layer_done")
        out_ready = sem("out_ready")
        out_done = sem("out_done")
        dve_link = [sem("dve_link0"), sem("dve_link1")]

        N1 = Numbers()
        block = ctx.enter_context(nc.Block())

        def rows3(t, kc, w):
            return t[:, 0:kc * w].rearrange("p (k n) -> p k n", k=kc)

        def bank2(i):
            return pb[i].rearrange("p (a n) -> p a n", a=2)

        def pt_part(g, b):
            if g["nk"] == P:
                return g["pt"][:, :, 0, :]
            return g["pt"][:, 2 * b:2 * b + 2, :, :].rearrange("p h k q -> p (h k) q")

        def mla_groups():
            out = []
            for m in range(M):
                for q in range(2):
                    i = len(out)
                    hs = [4 * q + h for h in range(4)]
                    out.append(dict(
                        q=[mqT[0:DK1, h, m * P:m * P + P] for h in hs], k=[mkT[0:DK1, h, :] for h in hs],
                        v=lambda h, kt, q=q: mkv[:, kt, 4 * q + h, 64:128], nk=S, p=P0[i % 2], pt=PT0[i % 2],
                        scale=DK1 ** -0.5, bias=None, out=ocat[:, m, 256 * q:256 * q + 256].rearrange("p (h d) -> p h d", h=4)))
            return out

        def dil_groups():
            out = []
            for m in range(M):
                for g in range(DG):
                    i = len(out)
                    at_ = [(slice(64 * (s % 2), 64 * (s % 2) + 64), 2 * g + s // 2) for s in SLOT_HEADS]
                    out.append(dict(
                        q=[dqk[r, c, m * P:m * P + P] for r, c in at_],
                        k=[dqk[r, 6 + c, :] for r, c in at_],
                        v=lambda s, kt, g=g: dv[:, kt, 256 * g + 64 * SLOT_HEADS[s]:256 * g + 64 * SLOT_HEADS[s] + 64], nk=S, p=P0[i % 2], pt=PT0[i % 2],
                        scale=1.0, bias=dbias[:, 4 * g:4 * g + 4, P * (1 - m):P * (3 - m)], out=og[:, m, g, :, :],
                        mx=mxd[:, m, g, :], den=dend[:, m, g, :]))
            return out

        def gqa_groups():
            out = []
            for m in range(M):
                for g in range(G2):
                    i = len(out)
                    r = slice(64 * (g % 2), 64 * (g % 2) + 64)
                    c = 512 * (g // 2) + 64 * (g % 2)
                    o = go[:, m, 512 * (g // 2):512 * (g // 2) + 512].rearrange("p (h b d) -> p h b d", h=4, b=2)[:, :, g % 2, :]
                    out.append(dict(
                        q=[gqT[r, 4 * (g // 2) + h, m * P:m * P + P] for h in range(4)], k=[gkT[r, g // 2, :]] * 4,
                        v=lambda h, kt, g=g: gqkv[:, kt, 1280 + 64 * g:1344 + 64 * g], nk=S, p=P1[i % 2], pt=PT1[i % 2],
                        scale=0.125, bias=None, out=o))
            return out

        def nsa_groups():
            out = []
            for m in range(M):
                for br in range(2):
                    for g in range(2):
                        i = len(out)
                        r = slice(64 * g, 64 * g + 64)
                        nk_ = P * (m + 1)
                        out.append(dict(
                            q=[nq[r, h, m * P:m * P + P] for h in range(4)], k=[nk[r, br, 0:nk_]] * 4,
                            v=lambda h, kt, g=g, br=br: nv[:, kt, P * br + 64 * g:P * br + 64 * g + 64], nk=nk_,
                            p=P2[i % 2], pt=PT2[i % 2], scale=1.0, bias=nbias[:, 4 * g:4 * g + 4, P * (1 - m):2 * P],
                            gate=ng[:, m, g, :, 1 + br], out=vA[:, m, 256 * g:256 * g + 256].rearrange("p (h d) -> p h d", h=4)))
            return out

        @block.sync
        def _(sp):
            sp.dma_start(x[:, 0, :], xin[:, 0, :]).then_inc(x_in[0], 16)
            sp.dma_start(gbc, gains[0]).then_inc(gain0_in, 16)
            sp.dma_start(raw[0], stream[0]).then_inc(landed[0], 16)
            sp.dma_start(x[:, 1, :], xin[:, 1, :]).then_inc(x_in[1], 16)
            for r in range(1, 3):
                sp.dma_start(raw[r], stream[r]).then_inc(landed[r], 16)
            with nc.sync.Fori(1, TILES // 3) as third:
                for r in range(3):
                    sp.wait_ge(hi_made, 3 * third + r - 2)
                    sp.wait_ge(lo_made, 3 * third + r - 2)
                    sp.dma_start(raw[r], stream[bass.ds(3 * third + r, 1)].rearrange("a p n -> (a p) n")).then_inc(landed[r], 16)
            for t in range(3 * (TILES // 3), TILES):
                sp.wait_ge(hi_made, t - 2)
                sp.wait_ge(lo_made, t - 2)
                sp.dma_start(raw[t % 3], stream[t]).then_inc(landed[t % 3], 16)
            sp.wait_ge(out_ready, 1)
            sp.dma_start(out, y).then_inc(out_done, 16)
            sp.wait_ge(out_done, 16)

        @block.gpsimd
        def _(pool):
            pool.dma_start(misc_sb, misc).then_inc(tab_in, 16)
            pool.memset(half, -0.5).then_inc(half_set, 1)
            pool.wait_ge(half_set, 1)
            powers = [0]

            def power(n, src=ms, dst=rstd, e=half, at_=0):
                pool.wait_ge(ms_ready, powers[0] + 1)
                c = slice(at_, at_ + n)
                pool.tensor_tensor(dst[:, c], src[:, c], e[:, c], ALU.pow).then_inc(rstd_ready, 1)
                powers[0] = powers[0] + 1

            def halves_power():
                power(1)
                power(1, at_=1)

            def one(a, i):
                return a[bass.ds(i, 1)].rearrange("a p n -> (a p) n")

            def next_gain(i):
                pool.wait_ge(y_ready, 4 * i)
                pool.dma_start(gbc, one(gains, i)).then_inc(gain_in, 16)

            halves_power()
            pool.dma_start(mlagain, mlag[:, 0:640]).then_inc(mlag_in, 16)
            pool.dma_start(dbias.rearrange("p h k -> p (h k)"), dilb).then_inc(dilb_in, 16)
            next_gain(1)
            power(4)
            power(2)
            next_gain(2)
            pool.wait_ge(x_ready, 4)
            pool.memset(ghalf, -0.5).then_inc(half_set, 1)
            pool.dma_start(ggain, mlag[:, 640:768]).then_inc(gg_in, 16)
            pool.wait_ge(gg_in, 16)
            pool.wait_ge(tab_in, 16)
            for s in range(2):
                g4 = ggain[:, 64 * s:64 * s + 64].rearrange("p (a x f) -> p a x f", a=2, x=2)
                for j, angle in enumerate((cos2, sin2, sin2, cos2)):
                    gx = g4[:, :, j % 2, :].unsqueeze(1).broadcast_to([P, M, 2, 16])
                    for h in range(4):
                        ins = pool.tensor_tensor(gtab[s][:, j, :, 2 * h:2 * h + 2, :], angle, gx, ALU.mult)
            ins.then_inc(gtab_ready, 1)
            halves_power()
            next_gain(3)
            pool.wait_ge(half_set, 2)
            pool.wait_ge(gtab_ready, 1)
            for u in range(5):
                power(8, gms, grs, ghalf, 8 * u)
                pool.wait_ge(rstd_ready, powers[0])
                if u >= 2:
                    pool.wait_ge(gr_dve, u - 1)
                c = 1024 if u == 0 else 256 * (u - 1)
                pool.tensor_tensor(gn[u % 2].rearrange("p m (h d) -> p m h d", h=4), gqkv[:, :, c:c + 256].rearrange("p m (h d) -> p m h d", h=4),
                                   grs[:, 8 * u:8 * u + 8].rearrange("p (m h) -> p m h", m=M).unsqueeze(3).broadcast_to([P, M, 4, 64]),
                                   ALU.mult).then_inc(gn_ready, 1)
                pool.wait_ge(gn_ready, u + 1)
                xab = gn[u % 2].rearrange("p m (g x f) -> p m g x f", g=8, x=2)
                for x_ in range(2):
                    if u and x_ == 0:
                        pool.wait_ge(gr_pool, u)
                    pool.tensor_tensor(gtp[:, x_], xab[:, :, :, x_, :], gtab[u == 0][:, 2 + x_], ALU.mult).then_inc(gtp_ready, 1)
                pool.wait_ge(gtp_ready, 2 * u + 2)
                pool.tensor_tensor(gr[:, :, c:c + 256].rearrange("p m (g x f) -> p m g x f", g=8, x=2)[:, :, :, 1, :],
                                   gtp[:, 0], gtp[:, 1], ALU.add).then_inc(gr_pool, 1)
            power(2)
            next_gain(4)
            pool.wait_ge(x_ready, 12)
            pool.dma_start(gbc5, gains[5]).then_inc(gain5_in, 16)
            pool.dma_start(tab2, second).then_inc(tab2_in, 16)
            halves_power()
            halves_power()
            before = powers[0]
            with nc.gpsimd.Fori(0, LAYERS) as l:
                powers[0] = before + POWERS * l
                n = 5 + 3 * l
                pool.wait_ge(layer_done, l + 1)
                pool.dma_start(lng, one(rows, l)).then_inc(lay_in, 16)
                pool.dma_start(gmws.rearrange("p g t -> p (g t)"), one(small, l)[:, 0:512]).then_inc(lay_in, 16)
                pool.dma_start(sm2, one(small, l)[:, 512:700]).then_inc(lay_in, 16)
                pool.dma_start(cw1.rearrange("p i l c -> p (i l c)"), one(small, l)[:, 700:4796]).then_inc(lay_in, 16)
                next_gain(n + 1)
                halves_power()
                next_gain(n + 2)
                power(2)
                power(8)
                B = Numbers(l)
                pool.wait_ge(lay_in, 64 * (l + 1))
                pool.wait_ge(ro_used, l + 1)
                for j, op in enumerate((ALU.mult, ALU.add)):
                    for m in range(M):
                        c = slice(1024 + 512 * j, 1536 + 512 * j)
                        pool.tensor_tensor(rnorm[:, m, :], rnorm[:, m, :], lng[:, c], op).then_inc(pool_link, 1)
                    pool.wait_ge(pool_link, 4 * l + 2 * j + 2)
                pool.wait_ge(drain_act, B.drained(B.plan.step["win"] + 12, "A"))
                pool.tensor_tensor(rg, rg, rnorm, ALU.mult).then_inc(yb_ready, 1)
                for j in range(4):
                    pool.wait_ge(drain_dve, B.drained(B.plan.step["branch"] + 4 + j + 1, "D"))
                    c = slice(2 * j, 2 * j + 2)
                    pool.tensor_tensor(mix[:, c, :], mix[:, c, :], gates[:, 8 + 2 * j:10 + 2 * j, :], ALU.add).then_inc(mix_pool, 1)
                power(2)
                next_gain(n + 3)
                halves_power()

        @block.tensor
        def _(pe):
            def three(o, a, b, first, last):
                pe.matmul(o, a[1], b[0], start=first, stop=False)
                pe.matmul(o, a[0], b[1], start=False, stop=False)
                return pe.matmul(o, a[0], b[0], start=False, stop=last)

            def tile_split(B, tile):
                n = B.tile_no(tile) + 1
                pe.wait_ge(hi_made, n)
                pe.wait_ge(lo_made, n)

            def bank_free(B, step, first):
                for s, who in ((drain_act, "A"), (drain_dve, "D")):
                    n = B.drained(step if first else step - 1, who)
                    if type(n) is not int or n > 0:
                        pe.wait_ge(s, n)

            def features(B, tile, kc, w, c0, act, o, late=None):
                s = B.slot(tile)
                hi, lo = rows3(whi[s], kc, w), rows3(wlo[s], kc, w)
                for c in range(2):
                    for k in range(kc):
                        if late and c == 0 and k == kc // 2:
                            late()
                        cols = slice(c0 + c * P, c0 + c * P + P)
                        last = three(o[:, c, :], (hi[:, k, cols], lo[:, k, cols]), (act[0][:, k, :], act[1][:, k, :]),
                                     k == 0, k == kc - 1)
                return last

            def tokens(B, tile, kc, w, c0, n, act, o, late=None):
                s = B.slot(tile)
                hi, lo = rows3(whi[s], kc, w), rows3(wlo[s], kc, w)
                for m in range(M):
                    for k in range(kc):
                        if late and (m, k) == late[0]:
                            late[1]()
                        t = slice(m * P, m * P + P)
                        last = three(o[:, m, 0:n], (act[0][:, k, t], act[1][:, k, t]), (hi[:, k, c0:c0 + n], lo[:, k, c0:c0 + n]),
                                     k == 0, k == kc - 1)
                return last

            def copied(B, n):
                for s, who in ((tb_act, "A"), (tb_dve, "D")):
                    pe.wait_ge(s, B.copied(n, who))

            def bank_used(B, tb):
                n = B.tb0 + tb
                if type(n) is not int or n >= 2:
                    copied(B, tb - 1)

            def batch(B, tb, blocks, rows=P, bank=None):
                if bank is None:
                    bank_used(B, tb)
                o = pb[B.bank(tb) if bank is None else bank]
                for i, b in enumerate(blocks):
                    last = pe.transpose(o[0:rows, i * P:i * P + P], b, ident)
                last.then_inc(tb_done, 1)

            def keep_warm(n, bank):
                for _ in range(n):
                    pe.matmul(pb[bank][:, 0:P], ident, ident, start=True, stop=True)

            def norm_T(B, stage, n, halves=range(M)):
                for tb, m, q, bank in B.quarters(stage):
                    if m not in halves:
                        continue
                    after_mixer = stage in ("n1", "n3", "n6")
                    j = 2 * q + m if after_mixer else 2 * m + q
                    if after_mixer and (m, q) == (0, 0):
                        keep_warm(14, 4)
                    if not after_mixer and (m, q) == (1, 0) and stage != "n0":
                        keep_warm(8, 0)
                    pe.wait_ge(y_ready, 4 * n + j + 1)
                    if m == 0:
                        bank_used(B, B.plan.tb[stage] + q)
                    batch(B, tb, [y[:, m, (4 * q + k) * P:(4 * q + k + 1) * P] for k in range(4)], bank=bank)

            def dense(B, stage, i, kind, kc=8, w=256, c0=0, n=256, act=(yh, yl), per_tile=1, bank=None, alone=False, late=None, follows=False):
                tile, step = B.plan.tile[stage] + i // per_tile, B.plan.step[stage] + i
                tile_split(B, tile)
                bank_free(B, step, (i == 0 and not follows) or alone)
                o = bank2(i % 2 if bank is None else bank)
                if kind == "F":
                    last = features(B, tile, kc, w, c0, act, o, late)
                else:
                    last = tokens(B, tile, kc, w, c0, n, act, o, late)
                last.then_inc(step_done, 1)

            def ffn(B, stage, f, norm_stage):
                t0 = B.plan.tile[stage]
                t0_batches = B.plan.tb[norm_stage]

                def up(B, tile, bank, first=False, late=None):
                    tile_split(B, t0 + tile)
                    bank_free(B, B.plan.step[stage] + tile, first)
                    features(B, t0 + tile, 8, 256, 0, (yh, yl), bank2(bank), late).then_inc(step_done, 1)

                def down(B, chunks, i, tile):
                    tile_split(B, t0 + tile)
                    pe.wait_ge(h_ready, chunks + 2 * i + 2)
                    s = B.slot(t0 + tile)
                    hi, lo = rows3(whi[s], 2, 1024), rows3(wlo[s], 2, 1024)
                    ends = i == NF // 2 - 1
                    for j in range(4):
                        m, n = j // 2, j % 2
                        t, c = slice(m * P, m * P + P), slice(n * 512, n * 512 + 512)
                        for k in range(2):
                            last = three(pb[2 + j], (hh[i % 2][:, k, t], hl[i % 2][:, k, t]), (hi[:, k, c], lo[:, k, c]),
                                         i == 0 and k == 0, ends and k == 1)
                        if ends and j < 3:
                            last.then_inc(acc_done, 1)
                    last.then_inc(step_done, 1)

                def pair(B, chunks, i):
                    up(B, 3 * i - 1, 0)
                    up(B, 3 * i, 1)
                    down(B, chunks, i - 1, 3 * i + 1)

                copied(B, t0_batches + 2)
                up(B, 0, 0, True, lambda: copied(B, t0_batches + 4))
                up(B, 1, 1)
                pair(B, NF * f, 1)
                with nc.tensor.Fori(0, FFN_ROUNDS) as r:
                    for i in (2, 3):
                        pair(B.later(r), NF * f + 4 * r, i)
                pair(B, NF * f, NF // 2 - 1)
                down(B, NF * f, NF // 2 - 1, FFN_TILES - 1)

            def attention(B, stage, groups, ag0, extra=None):
                first_tb, t = [], B.plan.tb[stage]
                for g in groups:
                    first_tb.append(t)
                    t += g["nk"] // P
                n = len(groups)
                for i in range(n + 2):
                    if i < n:
                        g, a = groups[i], ag0 + i
                        if type(a) is not int or a >= 2:
                            pe.wait_ge(p_ready, a - 1)
                        for h in range(4):
                            o = pb[2 + 2 * (i % 2) + h // 2][:, (h % 2) * S:(h % 2) * S + g["nk"]]
                            last = pe.matmul(o, g["q"][h], g["k"][h], start=True, stop=True)
                        last.then_inc(sc_done, 1)
                    if extra:
                        extra(i)
                    elif i == 1:
                        keep_warm(7, 1)
                    if 1 <= i <= n:
                        g, a, tb = groups[i - 1], ag0 + i - 1, first_tb[i - 1]
                        pe.wait_ge(p_ready, a + 1)
                        nt = g["nk"] // P
                        for b in range(nt):
                            hs = range(4) if nt == 1 else (2 * b, 2 * b + 1)
                            batch(B, tb + b, [g["p"][:, h, kt * P:kt * P + P] for h in hs for kt in range(nt)])
                    if i >= 2:
                        g, a, tb = groups[i - 2], ag0 + i - 2, first_tb[i - 2]
                        nt = g["nk"] // P
                        if i > n and not extra:
                            keep_warm(4, 0)
                        copied(B, tb + nt)
                        if type(a) is not int or a >= 1:
                            pe.wait_ge(o_ready, a)
                        for h in range(4):
                            o = pb[1][:, h * 64:h * 64 + 64]
                            for kt in range(nt):
                                last = pe.matmul(o, g["pt"][:, h, kt, :], g["v"](h, kt), start=kt == 0, stop=kt == nt - 1)
                        last.then_inc(o_done, 1)

            def square(B, tb, src, kc, n_blocks):
                for b in range(n_blocks // 4):
                    batch(B, tb + b, [src(m, 2 * b + k) for k in range(2) for m in range(M)])

            B = N1
            pe.wait_ge(tab_in, 16)
            norm_T(B, "n0", 0, (0,))
            keep_warm(12, 0)
            copied(B, 2)
            tb = B.plan.tb["cq"]

            def second_half():
                norm_T(B, "n0", 0, (1,))
                copied(B, 4)

            def latents_T():
                pe.wait_ge(src_ready, 1)
                batch(B, tb, [zA[:, 0, k * P:k * P + P] for k in range(3)])
                batch(B, tb + 1, [zA[:, 1, k * P:k * P + P] for k in range(3)])
                batch(B, tb + 2, [zA[:, m, RQ + k * P:RQ + k * P + P] for k in range(2) for m in range(M)])

            for i in range(12):
                if i < 3:
                    dense(B, "z", i, "T", n=256 if i < 2 else 160, late=((1, 0), second_half) if i == 0 else None)
                else:
                    if i == 11:
                        latents_T()
                    dense(B, "z", i, "F" if i < 9 else "T")
            copied(B, tb + 3)
            for i in range(3):
                dense(B, "uq", i, "T", kc=3, w=512 if i < 2 else 256, c0=256 * (i % 2), act=(cqTh, cqTl), per_tile=2)
            for i in range(4):
                dense(B, "ukv", i, "T", kc=2, w=1024, c0=256 * i, act=(kvTh, kvTl), per_tile=4)
            pe.wait_ge(src_ready, 2)
            tb = B.plan.tb["mqk"]
            for b in range(4):
                batch(B, tb + b, [mq[:, m, 2 * b + k, :] for k in range(2) for m in range(M)], DK1)
            pe.wait_ge(src_ready, 3)
            for b in range(4):
                batch(B, tb + 4 + b, [kasm[:, m, 2 * b + k, :] for k in range(2) for m in range(M)], DK1)
            copied(B, tb + 8)
            attention(B, "mla", mla_groups() + dil_groups(), AG_MLA)
            tb = B.plan.tb["ocat"]
            pe.wait_ge(o_ready, AG_DIL)
            square(B, tb, lambda m, k: ocat[:, m, k * P:k * P + P], 4, 8)
            pe.wait_ge(src_ready, 4)
            square(B, tb + 2, lambda m, k: ocat[:, m, 512 + k * P:512 + k * P + P], 2, 4)
            copied(B, tb + 2)
            for i in range(4):
                dense(B, "wout", i, "T", kc=6, act=(oTh, oTl), late=((0, 4), lambda: copied(B, tb + 3)) if i == 0 else None)
            norm_T(B, "n1", 1)
            ffn(B, "f0", 0, "n1")
            norm_T(B, "n2", 2)
            copied(B, B.plan.tb["n2"] + 2)
            tb = B.plan.tb["gqk"]

            def turned_T(u):
                pe.wait_ge(gr_dve, u + 1)
                pe.wait_ge(gr_pool, u + 1)
                c = 8 if u == 0 else 2 * (u - 1)
                batch(B, tb + u, [gr[:, m, (c + k) * P:(c + k) * P + P] for k in range(2) for m in range(M)])

            for i in range(6):
                if i == 5:
                    for u in range(3):
                        turned_T(u)
                dense(B, "gqkv", i, "T", late=((1, 0), lambda: copied(B, B.plan.tb["n2"] + 4)) if i == 0 else None)
            turned_T(3)
            turned_T(4)
            copied(B, tb + 5)
            pe.wait_ge(drain_act, B.drained(B.plan.step["gqkv"] + 6, "A"))
            attention(B, "gqa", gqa_groups(), AG_GQA)
            tb = B.plan.tb["go"]
            pe.wait_ge(o_ready, AG_GQA + 6)
            square(B, tb, lambda m, k: go[:, m, k * P:k * P + P], 4, 8)
            pe.wait_ge(o_ready, AG_GQA + 8)
            square(B, tb + 2, lambda m, k: go[:, m, 512 + k * P:512 + k * P + P], 4, 8)
            copied(B, tb + 3)
            for i in range(4):
                dense(B, "gwo", i, "T", late=((0, 6), lambda: copied(B, tb + 4)) if i == 0 else None)
            norm_T(B, "n3", 3)
            ffn(B, "f1", 1, "n3")

            def layer(l):
                B = Numbers(l)
                plan = B.plan
                norm_T(B, "n4", 5 + 3 * l)
                ffn(B, "fa", 2 + 2 * l, "n4")
                norm_T(B, "n5", 6 + 3 * l)
                copied(B, plan.tb["n5"] + 2)
                kinds = "FFTTTTFFTTTTFFFTT"
                pe.wait_ge(lay_in, 64 * (l + 1))
                for i in range(17):
                    dense(B, "win", i, kinds[i], n=24 if i == 16 else 256, late=(lambda: copied(B, plan.tb["n5"] + 4)) if i == 0 else None)
                    if i == 3:
                        pe.wait_ge(blk_ready, l + 1)
                        keep_warm(1, 2)
                        for kv in range(2):
                            for lp in range(16):
                                last = pe.matmul(pb[2][0:30, kv * P:kv * P + P], blk[:, kv, lp, :, :].rearrange("p g n -> p (g n)"),
                                                 cw1[:, kv, lp, :], start=lp == 0, stop=lp == 15)
                        last.then_inc(hid_done, 1)
                    if i == 5:
                        pe.wait_ge(hid_act, l + 1)
                        keep_warm(1, 5)
                        for kv in range(2):
                            last = pe.transpose(pb[5][:, kv * 30:kv * 30 + 30], hidT[0:30, kv, :], ident[0:30, 0:30])
                        last.then_inc(hidt_done, 1)
                    if i == 7:
                        pe.wait_ge(hidx_ready, l + 1)
                        for g in range(2):
                            pe.matmul(pb[3][64 * g:64 * g + 64, 0:NCMP], cw2[:, 0, :], hid[:, 0, g * NCMP:g * NCMP + NCMP], start=True, stop=True)
                        pe.matmul(pb[4][0:120, 0:64], hidx.rearrange("p g r n -> p (g r n)"), cw2[:, 1, :], start=True, stop=True).then_inc(kc_done, 1)
                pe.wait_ge(gm_ready, l + 1)
                pe.wait_ge(kc_ready, l + 1)
                for m in range(M):
                    for g in range(4):
                        last = pe.matmul(pb[4 + m][:, g * P:g * P + P], gmws[:, g, :], vA[:, m, g * P:g * P + P], start=True, stop=True)
                last.then_inc(gm_done, 1)
                pe.wait_ge(drain_dve, B.drained(plan.step["win"] + 8, "D"))
                pe.wait_ge(drain_act, B.drained(plan.step["win"] + 10, "A"))
                for h in range(HR + 1):
                    if h < HR:
                        r = slice(64 * (h % 2), 64 * (h % 2) + 64)
                        if h >= 2:
                            pe.wait_ge(rs_ready, HR * l + h - 1)
                        pe.matmul(pb[2 + h % 2][:, 0:S], rqk[r, 2 + h // 2, 0:P], rqk[r, h // 2, :], start=True, stop=True)
                        pe.matmul(pb[2 + h % 2][:, S:S + P], rqk[r, 2 + h // 2, P:S], rqk[r, h // 2, P:S], start=True, stop=True).then_inc(rs_done, 1)
                    if h >= 1:
                        g = h - 1
                        if g == 0:
                            pe.wait_ge(ya_ready, l + 1)
                        pe.wait_ge(rs_ready, HR * l + g + 1)
                        c = slice(g * P, g * P + P)
                        pe.matmul(pb[4][:, c], rs[g % 2][:, 0:P], rv[:, 0, c], start=True, stop=True)
                        pe.matmul(pb[5][:, c], rs[g % 2][:, P:S], rv[:, 0, c], start=True, stop=False)
                        pe.matmul(pb[5][:, c], rs[g % 2][:, S:S + P], rv[:, 1, c], start=False, stop=True).then_inc(ro_done, 1)
                for m in range(M):
                    for g in range(2):
                        for h in range(4 * g, 4 * g + 4):
                            r = slice(64 * g, 64 * g + 64)
                            last = pe.matmul(pb[2 + m][:, h * NCMP:h * NCMP + NCMP], nq[r, h % 4, m * P:m * P + P], kcs[r, :], start=True, stop=True)
                        last.then_inc(cs_done, 1)
                        if g == 0:
                            pe.wait_ge(cs_done, 4 * l + 2 * m + 1)
                dense(B, "gates", 0, "F", bank=0)
                tb = plan.tb["cmp"]
                for m in range(M):
                    pe.wait_ge(ce_ready, M * l + m + 1)
                    batch(B, tb + m, [P2[0][:, m, 0:120]], 120)
                dense(B, "gates", 1, "F", bank=0, alone=True)
                square(B, plan.tb["ya"], lambda m, k: uA[:, m, k * P:k * P + P], 4, 8)
                pe.wait_ge(ro_used, l + 1)
                for m in range(M):
                    copied(B, tb + m + 1)
                    pe.matmul(pb[4 + m], PT2[0][0:120, m, 0, :], bd[0:120, :, :].rearrange("p h d -> p (h d)"), start=True, stop=True).then_inc(co_done, 1)

                def gate_step(i):
                    dense(B, "gates", 2 + i, "F", bank=0, alone=True)
                    if i == 0:
                        pe.wait_ge(yc_ready, 3 * l + 2)

                attention(B, "nsa", nsa_groups(), AG_NSA + 8 * l, gate_step)
                tb = plan.tb["y"]
                pe.wait_ge(yb_ready, l + 1)
                square(B, tb, lambda m, k: rg[:, m, k * P:k * P + P], 4, 8)
                for i in range(12):
                    if i == 1:
                        pe.wait_ge(yc_ready, 3 * l + 3)
                        square(B, tb + 2, lambda m, k: vA[:, m, k * P:k * P + P], 4, 8)
                    if i in (4, 8):
                        copied(B, tb + i // 2)
                    dense(B, "branch", i, "F", kc=4, w=512, c0=256 * (i % 2), per_tile=2,
                          act=((aTh, aTl), (bTh, bTl), (cTh, cTl))[i // 4])
                pe.wait_ge(mix_ready, 4 * l + 3)
                for i in range(4):
                    dense(B, "wo", i, "T", follows=True,
                          late=((0, 6), lambda: pe.wait_ge(mix_ready, 4 * l + 4)) if i == 0 else None)
                norm_T(B, "n6", 7 + 3 * l)
                ffn(B, "fb", 3 + 2 * l, "n6")

            keep_warm(24, 0)
            with nc.tensor.Fori(0, LAYERS) as l:
                layer(l)

        @block.scalar
        def _(act):

            def split(B, tile):
                s = B.slot(tile)
                act.wait_ge(landed[s], B.landed(tile))
                if B.l is not None or tile >= 3:
                    act.wait_ge(step_done, B.step0 + B.last_step(tile - 3) + 1)
                act.activation(whi[s], raw[s], ACT.Copy).then_inc(hi_made, 1)

            def ahead(B, stage, i, per_tile=1):
                if i % per_tile == 0:
                    split(B, B.plan.tile[stage] + i // per_tile + 2)

            def load_table(func):
                act.activation(warm, half[:, 0:1], func)

            def stepped(B, stage, i):
                act.wait_ge(step_done, B.step0 + B.plan.step[stage] + i + 1)

            def hi_T(B, tb, dst, n=512, bank=None):
                act.wait_ge(tb_done, B.tb0 + tb + 1)
                src = pb[B.bank(tb) if bank is None else bank][:, 0:n]
                if len(dst.shape) == 3:
                    src = src.rearrange("p (a n) -> p a n", a=dst.shape[1])
                act.activation(dst, src, ACT.Copy).then_inc(tb_act, 1)

            def plain_T(B, tb, dst, rows_=P):
                if B.plan.copies[tb] == "A":
                    act.wait_ge(tb_done, B.tb0 + tb + 1)
                    act.activation(dst, pb[B.bank(tb)][0:rows_].rearrange("p (a n) -> p a n", a=dst.shape[1]), ACT.Copy).then_inc(tb_act, 1)

            def sumsq(n, of_norm=False, parts=range(4)):
                for j in parts:
                    if of_norm:
                        act.wait_ge(y_ready, 4 * n - 3 + j)
                    elif type(n) is int and n == 0:
                        act.wait_ge(x_in[j // 2], 16)
                    else:
                        act.wait_ge(x_ready, 4 * n - 3 + j)
                    c = slice(512 * (j % 2), 512 * (j % 2) + 512)
                    act.activation(y[:, j // 2, c], x[:, j // 2, c], ACT.Square, scale=D ** -0.5,
                                   accum_out=ss[:, j // 2, j % 2:j % 2 + 1]).then_inc(ss_act, 1)

            def out_steps(B, stage):
                ahead(B, stage, 0)
                for i in range(4):
                    if i < 3:
                        ahead(B, stage, i + 1)
                    act.wait_ge(drain_dve, B.drained(B.plan.step[stage] + i + 1, "D"))
                    c = slice(256 * i, 256 * i + 256)
                    act.activation(y[:, 0, c], x[:, 0, c], ACT.Square, scale=D ** -0.5, accum_out=ss[:, 0, i:i + 1]).then_inc(ss_act, 1)

            def norm_T(B, stage, halves=range(M)):
                for tb, m, q, bank in B.quarters(stage):
                    if m in halves:
                        hi_T(B, tb, yh[:, 4 * q:4 * q + 4, m * P:m * P + P], bank=bank)

            def square_T(B, tb, n, dst):
                for b in range(n):
                    hi_T(B, tb + b, dst[:, 2 * b:2 * b + 2, :])

            def ffn(B, stage, f):
                def silu(B, chunks, j, tile):
                    ahead(B, stage, tile)
                    if type(tile) is int and tile == 0:
                        load_table(ACT.Silu)
                    stepped(B, stage, tile)
                    if j >= 2:
                        act.wait_ge(h_ready, chunks + j - 1)
                    act.activation(sg[j % 2], bank2(j % 2)[:, 0, :], ACT.Silu).then_inc(silu_done, 1)

                def pair(B, chunks, i):
                    silu(B, chunks, 2 * i, 3 * i - 1)
                    silu(B, chunks, 2 * i + 1, 3 * i)
                    ahead(B, stage, 3 * i + 1)

                silu(B, NF * f, 0, 0)
                silu(B, NF * f, 1, 1)
                pair(B, NF * f, 1)
                with nc.scalar.Fori(0, FFN_ROUNDS) as r:
                    for i in (2, 3):
                        pair(B.later(r), NF * f + 4 * r, i)
                pair(B, NF * f, NF // 2 - 1)
                ahead(B, stage, FFN_TILES - 1)

            def attention(B, stage, groups, ag0, extra=None, after=None):
                t, first_tb = B.plan.tb[stage], []
                for g in groups:
                    first_tb.append(t)
                    t += g["nk"] // P
                n = len(groups)
                for i in range(n + 1):
                    if extra:
                        extra(i)
                    if i < n:
                        g, a = groups[i], ag0 + i
                        act.wait_ge(mx_ready, a + 1)
                        if i >= 2:
                            act.wait_ge(tb_done, B.tb0 + first_tb[i - 2] + groups[i - 2]["nk"] // P)
                        if i >= 4 or type(a) is not int or a >= 4:
                            act.wait_ge(o_ready, a - 3)
                        for h in range(4):
                            src = g["p"][:, h, 0:g["nk"]] if g["bias"] is not None else \
                                pb[2 + 2 * (i % 2) + h // 2][:, (h % 2) * S:(h % 2) * S + S]
                            d = g["den"][:, h:h + 1] if "den" in g else den[:, i % 4, h:h + 1]
                            last = act.activation(g["p"][:, h, 0:g["nk"]], src, ACT.Exp, bias=nmx[:, i % 2, h:h + 1],
                                                  scale=g["scale"], accum_out=d)
                        last.then_inc(p_ready, 1)
                    if after:
                        after(i)
                    if i >= 1:
                        g, a, tb = groups[i - 1], ag0 + i - 1, first_tb[i - 1]
                        nt = g["nk"] // P
                        if i - 1 >= 2:
                            act.wait_ge(o_done, a - 1)
                        for b in range(nt):
                            plain_T(B, tb + b, pt_part(g, b))

            B = N1
            sumsq(0, parts=(0, 1))
            norm_T(B, "n0", (0,))
            split(B, 0)
            sumsq(0, parts=(2, 3))
            split(B, 1)
            norm_T(B, "n0", (1,))
            for i in range(12):
                if i == 11:
                    tb = B.plan.tb["cq"]
                    hi_T(B, tb, cqTh[:, :, 0:P], 384)
                    hi_T(B, tb + 1, cqTh[:, :, P:S], 384)
                    hi_T(B, tb + 2, kvTh[:, :, :])
                ahead(B, "z", i)
                stepped(B, "z", i)
                if i < 3:
                    n = 256 if i < 2 else 160
                    ins = act.activation(zA[:, :, 256 * i:256 * i + n], bank2(i % 2)[:, :, 0:n], ACT.Copy)
                elif i < 9:
                    ins = act.activation(dqk[:, 2 * i - 6:2 * i - 4, :], bank2(i % 2), ACT.Copy, scale=0.125 if i < 6 else 1.0)
                else:
                    ins = act.activation(dv[:, :, 256 * (i - 9):256 * (i - 8)], bank2(i % 2), ACT.Copy)
                ins.then_inc(drain_act, 1)
            for i in range(3):
                ahead(B, "uq", i, 2)
            for i in range(4):
                ahead(B, "ukv", i, 4)
                stepped(B, "ukv", i)
                act.activation(mkv[:, :, 2 * i:2 * i + 2, :].rearrange("p m h d -> p m (h d)"), bank2(i % 2), ACT.Copy).then_inc(drain_act, 1)
            act.wait_ge(half_set, 1)
            load_table(ACT.Exp)
            tb = B.plan.tb["mqk"]
            for b in range(8):
                plain_T(B, tb + b, (mqT if b < 4 else mkT)[0:DK1, 2 * (b % 4):2 * (b % 4) + 2, :], DK1)

            def group_weights(i):
                if i in (7, 10):
                    m = i // 10
                    act.wait_ge(wmx, m + 1)
                    w = wd[:, m].rearrange("p g s -> p (g s)")
                    act.activation(w, w, ACT.Exp).then_inc(wexp, 1)

            attention(B, "mla", mla_groups() + dil_groups(), AG_MLA, group_weights)
            square_T(B, B.plan.tb["ocat"], 3, oTh)
            out_steps(B, "wout")
            norm_T(B, "n1")
            ffn(B, "f0", 0)
            sumsq(2)
            norm_T(B, "n2")
            tb = B.plan.tb["gqk"]

            def turned_T(u):
                plain_T(B, tb + u, gqT[:, 2 * u - 2:2 * u, :] if u else gkT)

            load_table(ACT.Exp)
            for i in range(6):
                if i == 5:
                    for u in range(3):
                        turned_T(u)
                ahead(B, "gqkv", i)
                stepped(B, "gqkv", i)
                c = (1024, 0, 256, 512, 768, 1280)[i]
                if i < 5:
                    if i >= 2:
                        act.wait_ge(ms_ready, POWERS_GQA + i - 1)
                    act.activation(gsq[i % 2], bank2(i % 2), ACT.Square)
                act.activation(gqkv[:, :, c:c + 256], bank2(i % 2), ACT.Copy).then_inc(drain_act, 1)
            turned_T(3)
            turned_T(4)
            attention(B, "gqa", gqa_groups(), AG_GQA)
            square_T(B, B.plan.tb["go"], 4, yh)
            out_steps(B, "gwo")
            norm_T(B, "n3")
            ffn(B, "f1", 1)
            sumsq(4)
            sumsq(5, True)

            def layer(l):
                B = Numbers(l)
                plan = B.plan
                norm_T(B, "n4")
                ffn(B, "fa", 2 + 2 * l)
                sumsq(6 + 3 * l)
                norm_T(B, "n5")
                for i in range(17):
                    ahead(B, "win", i)
                    o = bank2(i % 2)
                    if WIN_DRAINS[i] == "A":
                        if i in (2, 10, 16):
                            load_table({2: ACT.Gelu_apprx_tanh, 10: ACT.Silu, 16: ACT.Exp}[i])
                        stepped(B, "win", i)
                        if i in (2, 3, 4, 5):
                            dst = (vA if i < 4 else uA)[:, :, 256 * (i % 2):256 * (i % 2) + 256]
                            ins = act.activation(dst, o, ACT.Gelu_apprx_tanh)
                        elif i in (8, 9):
                            ins = act.activation(rv[:, :, 256 * (i % 2):256 * (i % 2) + 256], o, ACT.Copy)
                        elif i in (10, 11):
                            ins = act.activation(rg[:, :, 256 * (i % 2):256 * (i % 2) + 256], o, ACT.Silu)
                        else:
                            ins = act.activation(ng.rearrange("p m g r b -> p m (g r b)"), o[:, :, 0:24], ACT.Exp, scale=-1.0)
                        ins.then_inc(drain_act, 1)
                    if i == 4:
                        act.wait_ge(hid_done, l + 1)
                        act.activation(hidT[0:30].rearrange("p i c -> p (i c)"), pb[2][0:30, 0:2 * P], ACT.Gelu_apprx_tanh).then_inc(hid_act, 1)
                for m in range(M):
                    act.wait_ge(cs_ready, M * l + m + 1)
                    act.activation(P2[0][:, m, 0:120], P2[0][:, m, 0:120], ACT.Exp).then_inc(ce_ready, 1)
                    if m == 0:
                        ahead(B, "gates", 0)

                def gate_drain(i):
                    stepped(B, "gates", i)
                    for c in range(2):
                        j = 2 * i + c
                        ins = act.activation(gates[:, j, :], bank2(0)[:, c, :], ACT.Tanh, bias=hmb[:, j:j + 1], scale=0.5)
                    ins.then_inc(drain_act, 1)

                gate_drain(0)
                ahead(B, "gates", 1)
                tb = plan.tb["cmp"]
                act.wait_ge(tb_done, B.tb0 + tb + 1)
                act.activation(PT2[0][0:120, 0, 0, :], pb[B.bank(tb)][0:120, 0:P], ACT.Copy).then_inc(tb_act, 1)
                gate_drain(1)
                square_T(B, plan.tb["ya"], 2, aTh)
                act.wait_ge(co_done, M * l + 2)
                attention(B, "nsa", nsa_groups(), AG_NSA + 8 * l,
                          lambda i: ahead(B, "gates", 2 + i), lambda i: gate_drain(2 + i))
                ahead(B, "gates", 11)
                gate_drain(11)
                def mix_high(j):
                    act.wait_ge(mix_sum, 4 * l + j + 1)
                    act.activation(yh[:, 2 * j:2 * j + 2, :], mix[:, 2 * j:2 * j + 2, :], ACT.Copy, scale=0.5).then_inc(mixh_made, 1)

                tb = plan.tb["y"]
                square_T(B, tb, 2, bTh)
                for i in range(12):
                    ahead(B, "branch", i, 2)
                    if i == 0:
                        square_T(B, tb + 2, 2, cTh)
                    if i >= 9:
                        mix_high(i - 9)
                mix_high(3)
                out_steps(B, "wo")
                norm_T(B, "n6")
                ffn(B, "fb", 3 + 2 * l)
                sumsq(8 + 3 * l)

            with nc.scalar.Fori(0, LAYERS) as l:
                layer(l)

        @block.vector
        def _(dve):
            links = [dve_link[0], 0]
            powers = [0]
            counted = [0]

            def link(ins):
                links[1] = links[1] + 1
                counted[0] += 1
                ins.then_inc(links[0], 1)
                dve.wait_ge(links[0], links[1])

            def pause():
                dve.tensor_copy(idle, half[:, 0:1])

            def split(B, tile):
                s = B.slot(tile)
                dve.wait_ge(hi_made, B.tile_no(tile) + 1)
                dve.tensor_tensor(wlo[s], raw[s], whi[s].bitcast(F32), ALU.subtract).then_inc(lo_made, 1)

            def ahead(B, stage, i, per_tile=1):
                if i % per_tile == 0:
                    split(B, B.plan.tile[stage] + i // per_tile + 2)

            def stepped(B, stage, i):
                dve.wait_ge(step_done, B.step0 + B.plan.step[stage] + i + 1)

            def lo_T(B, tb, dst, hi, n=512, bank=None):
                dve.wait_ge(tb_act, B.copied(tb + 1, "A"))
                src = pb[B.bank(tb) if bank is None else bank][:, 0:n]
                if len(dst.shape) == 3:
                    src = src.rearrange("p (a n) -> p a n", a=dst.shape[1])
                dve.tensor_tensor(dst, src, hi.bitcast(F32), ALU.subtract).then_inc(tb_dve, 1)

            def plain_T(B, tb, dst, rows_=P):
                if B.plan.copies[tb] == "D":
                    dve.wait_ge(tb_done, B.tb0 + tb + 1)
                    dve.tensor_copy(dst, pb[B.bank(tb)][0:rows_].rearrange("p (a n) -> p a n", a=dst.shape[1])).then_inc(tb_dve, 1)

            def power(mean):
                mean.then_inc(ms_ready, 1)
                powers[0] = powers[0] + 1
                dve.wait_ge(rstd_ready, powers[0])

            def half_power(n, m):
                dve.wait_ge(ss_act, 4 * n + 2 * m + 2)
                power(dve.tensor_scalar(ms[:, m:m + 1], ss[:, m, 0:1], ss[:, m, 1:2], EPS, ALU.add, ALU.add))

            def normed(m, q, dst=y, gain=gbc):
                c = slice(512 * q, 512 * q + 512)
                dve.scalar_tensor_tensor(out=dst[:, m, c], in0=x[:, m, c], scalar=rstd[:, m:m + 1], in1=gain[:, c],
                                         op0=ALU.mult, op1=ALU.mult).then_inc(y_ready, 1)

            def norm(n, gain_sem, value, gain, halves=range(M)):
                for m in halves:
                    half_power(n, m)
                    dve.wait_ge(gain_sem, value)
                    for q in range(2):
                        normed(m, q, gain=gain)

            def norm_T(B, stage, halves=range(M)):
                for tb, m, q, bank in B.quarters(stage):
                    if m not in halves:
                        continue
                    sl = (slice(None), slice(4 * q, 4 * q + 4), slice(m * P, m * P + P))
                    lo_T(B, tb, yl[sl], yh[sl], bank=bank)

            def after_ffn_T(B, stage, first):
                norm_T(B, stage)
                split(B, B.plan.tile[first] + 1)

            def square_T(B, tb, n, lo, hi):
                for b in range(n):
                    lo_T(B, tb + b, lo[:, 2 * b:2 * b + 2, :], hi[:, 2 * b:2 * b + 2, :])

            def add_x(B, stage, bank_i, i):
                c = slice(256 * i, 256 * i + 256)
                dve.tensor_tensor(x[:, :, c], x[:, :, c], bank2(bank_i), ALU.add).then_inc(drain_dve, 1)

            def out_steps(B, stage, n):
                for i in range(4):
                    ahead(B, stage, i)
                    stepped(B, stage, i)
                    add_x(B, stage, i % 2, i)
                    dve.wait_ge(drain_dve, B.drained(B.plan.step[stage] + i + 1, "D"))
                    c = slice(256 * i, 256 * i + 256)
                    ins = dve.tensor_tensor_reduce(out=y[:, 1, c], in0=x[:, 1, c], in1=x[:, 1, c], scale=1.0 / D, scalar=0.0,
                                                   op0=ALU.mult, op1=ALU.add, accum_out=ss[:, 1, i:i + 1])
                link(ins)
                dve.sem_inc(x_ready, 4)
                dve.wait_ge(ss_act, 4 * n + 4)
                link(dve.tensor_reduce(ms[:, 0:2], ss, AX_X, ALU.add))
                power(dve.tensor_scalar(ms[:, 0:2], ms[:, 0:2], EPS, None, ALU.add))
                dve.wait_ge(gain_in, 16 * gain_no(n))
                for q in range(2):
                    for m in range(M):
                        normed(m, q)

            def ffn(B, stage, f, weight, n, dst=y):
                def hidden(B, chunks, i, j, tile):
                    ahead(B, stage, tile)
                    dve.wait_ge(silu_done, chunks + j + 1)
                    dve.tensor_tensor(h32[j % 2], sg[j % 2], bank2(j % 2)[:, 1, :], ALU.mult).then_inc(drain_dve, 1)
                    if i >= 2:
                        dve.wait_ge(step_done, B.step0 + B.plan.step[stage] + 3 * (i - 2) + 4 + 1)
                    dve.wait_ge(drain_dve, B.drained(B.plan.step[stage] + tile + 1, "D"))
                    dve.tensor_copy(hh[i % 2][:, j % 2, :], h32[j % 2]).then_inc(hh_made, 1)
                    dve.wait_ge(hh_made, chunks + j + 1)
                    dve.tensor_tensor(hl[i % 2][:, j % 2, :], h32[j % 2], hh[i % 2][:, j % 2, :].bitcast(F32), ALU.subtract).then_inc(h_ready, 1)

                def pair(B, chunks, i):
                    hidden(B, chunks, i, 2 * i, 3 * i - 1)
                    hidden(B, chunks, i, 2 * i + 1, 3 * i)
                    ahead(B, stage, 3 * i + 1)

                hidden(B, NF * f, 0, 0, 0)
                hidden(B, NF * f, 0, 1, 1)
                pair(B, NF * f, 1)
                with nc.vector.Fori(0, FFN_ROUNDS) as r:
                    for i in (2, 3):
                        pair(B.later(r), NF * f + 4 * r, i)
                pair(B, NF * f, NF // 2 - 1)

                def add(j):
                    m, c = j // 2, slice(512 * (j % 2), 512 * (j % 2) + 512)
                    if j < 3:
                        dve.wait_ge(acc_done, 3 * f + j + 1)
                    else:
                        stepped(B, stage, FFN_TILES - 1)
                    dve.scalar_tensor_tensor(out=x[:, m, c], in0=pb[2 + j], scalar=weight, in1=x[:, m, c],
                                             op0=ALU.mult, op1=ALU.add).then_inc(x_ready, 1)

                for j in range(3):
                    add(j)
                half_power(n, 0)
                dve.wait_ge(gain_in, 16 * gain_no(n))
                normed(0, 0, dst)
                add(3)
                normed(0, 1, dst)
                half_power(n, 1)
                dve.wait_ge(x_ready, 4 * n)
                normed(1, 0, dst)
                normed(1, 1, dst)

            def bc(a, n):
                return a.unsqueeze(len(a.shape)).broadcast_to(list(a.shape) + [n])

            def attention(B, stage, groups, ag0, drain, extra=None, before=None):
                t, first_tb = B.plan.tb[stage], []
                for g in groups:
                    first_tb.append(t)
                    t += g["nk"] // P
                n = len(groups)
                for i in range(n + 2):
                    if i < n:
                        g, a = groups[i], ag0 + i
                        nk_ = g["nk"]
                        dve.wait_ge(sc_done, a + 1)
                        if type(a) is not int or a >= 2:
                            dve.wait_ge(p_ready, a - 1)
                        mxo = g["mx"] if "mx" in g else mx[:, i % 2, :]
                        if g["bias"] is not None:
                            if i >= 2:
                                dve.wait_ge(tb_done, B.tb0 + first_tb[i - 2] + groups[i - 2]["nk"] // P)
                            for h2 in range(2):
                                src = bank2(2 + 2 * (i % 2) + h2)[:, :, 0:nk_]
                                ins = dve.tensor_tensor(g["p"][:, 2 * h2:2 * h2 + 2, 0:nk_], src, g["bias"][:, 2 * h2:2 * h2 + 2, :], ALU.add)
                            link(ins)
                            link(dve.tensor_reduce(mxo, g["p"][:, :, 0:nk_], AX_X, ALU.max))
                        else:
                            for h2 in range(2):
                                ins = dve.tensor_reduce(mxo[:, 2 * h2:2 * h2 + 2], bank2(2 + 2 * (i % 2) + h2), AX_X, ALU.max)
                            link(ins)
                        dve.tensor_scalar(nmx[:, i % 2, :], mxo, -g["scale"], None, ALU.mult).then_inc(mx_ready, 1)
                    if extra:
                        extra(i)
                    if 1 <= i <= n:
                        g, a, tb = groups[i - 1], ag0 + i - 1, first_tb[i - 1]
                        nt = g["nk"] // P
                        if i - 1 >= 2:
                            dve.wait_ge(o_done, a - 1)
                        for b in range(nt):
                            plain_T(B, tb + b, pt_part(g, b))
                    if i >= 2:
                        g, a = groups[i - 2], ag0 + i - 2
                        if before:
                            before(i - 2)
                        dve.wait_ge(o_done, a + 1)
                        drain(g, i - 2, pb[1][:, 0:S].rearrange("p (h d) -> p h d", h=4))

            def normalize(g, i, o):
                link(dve.reciprocal(rec, den[:, i % 4, :]))
                dve.tensor_tensor(g["out"], o, bc(rec, 64), ALU.mult).then_inc(o_ready, 1)

            B = N1
            norm(0, gain0_in, 16, gbc, (0,))
            norm_T(B, "n0", (0,))
            split(B, 0)
            norm(0, gain0_in, 16, gbc, (1,))
            norm_T(B, "n0", (1,))
            split(B, 1)
            for i in range(4):
                ahead(B, "z", i)
            dve.wait_ge(tab_in, 16)
            dve.wait_ge(mlag_in, 16)
            dve.wait_ge(drain_act, 3)
            for j, (c0, n) in enumerate(((0, RQ), (RQ, RKV))):
                for m in range(M):
                    ins = dve.tensor_tensor_reduce(out=y[:, m, 0:n], in0=zA[:, m, c0:c0 + n], in1=zA[:, m, c0:c0 + n], scale=1.0,
                                                   scalar=0.0, op0=ALU.mult, op1=ALU.add, accum_out=ms[:, 4 + 2 * j + m:5 + 2 * j + m])
                    link(ins)
            link(dve.tensor_scalar(ms[:, 0:2], ms[:, 4:6], 1.0 / RQ, EPS, ALU.mult, ALU.add))
            power(dve.tensor_scalar(ms[:, 2:4], ms[:, 6:8], 1.0 / RKV, EPS, ALU.mult, ALU.add))
            for j, (c0, n) in enumerate(((0, RQ), (RQ, RKV))):
                for m in range(M):
                    ins = dve.scalar_tensor_tensor(out=zA[:, m, c0:c0 + n], in0=zA[:, m, c0:c0 + n], scalar=rstd[:, 2 * j + m:2 * j + m + 1],
                                                   in1=mlagain[:, c0:c0 + n], op0=ALU.mult, op1=ALU.mult)
            link(ins)
            dve.sem_inc(src_ready, 1)
            t1, t2 = (rt[:, i, 0:32].rearrange("p (m f) -> p m f", m=M) for i in range(2))
            ka, kb = zA[:, :, 640:656], zA[:, :, 656:672]
            dve.tensor_tensor(t1, ka, cos1, ALU.mult)
            link(dve.tensor_tensor(t2, kb, sin1, ALU.mult))
            link(dve.tensor_tensor(kr[:, :, 0:16], t1, t2, ALU.subtract))
            dve.tensor_tensor(t1, ka, sin1, ALU.mult)
            link(dve.tensor_tensor(t2, kb, cos1, ALU.mult))
            link(dve.tensor_tensor(kr[:, :, 16:32], t1, t2, ALU.add))
            for i in range(4, 12):
                if i == 11:
                    tb = B.plan.tb["cq"]
                    for m in range(M):
                        c = slice(m * P, m * P + P)
                        lo_T(B, tb + m, cqTl[:, :, c], cqTh[:, :, c], 384)
                    lo_T(B, tb + 2, kvTl, kvTh)
                ahead(B, "z", i)
            for i in range(3):
                if i == 1:
                    ahead(B, "uq", 0)
                stepped(B, "uq", i)
                dve.tensor_copy(mq.rearrange("p m h d -> p m (h d)")[:, :, 256 * i:256 * i + 256], bank2(i % 2)).then_inc(drain_dve, 1)
            split(B, B.plan.tile["uq"] + 3)
            split(B, B.plan.tile["ukv"] + 2)
            dve.wait_ge(drain_dve, 3)
            qa, qb = mq[:, :, :, 64:80], mq[:, :, :, 80:96]
            t = [rt[:, i, :].rearrange("p (m h f) -> p m h f", m=M, h=H1) for i in range(4)]
            cb = cos1.unsqueeze(2).broadcast_to([P, M, H1, 16])
            sb_ = sin1.unsqueeze(2).broadcast_to([P, M, H1, 16])
            dve.tensor_tensor(t[0], qa, cb, ALU.mult)
            dve.tensor_tensor(t[1], qb, sb_, ALU.mult)
            dve.tensor_tensor(t[2], qa, sb_, ALU.mult)
            link(dve.tensor_tensor(t[3], qb, cb, ALU.mult))
            dve.tensor_tensor(qa, t[0], t[1], ALU.subtract)
            dve.tensor_tensor(qb, t[2], t[3], ALU.add).then_inc(src_ready, 1)
            dve.wait_ge(drain_act, B.drained(B.plan.step["ukv"] + 4, "A"))
            for m in range(M):
                dve.tensor_copy(kasm[:, m, :, 0:64], mkv[:, m, :, 0:64])
                ins = dve.tensor_copy(kasm[:, m, :, 64:96], kr[:, m, :].unsqueeze(1).broadcast_to([P, H1, 32]))
            ins.then_inc(src_ready, 1)
            tb = B.plan.tb["mqk"]
            for b in range(8):
                plain_T(B, tb + b, (mqT if b < 4 else mkT)[0:DK1, 2 * (b % 4):2 * (b % 4) + 2, :], DK1)

            def weights_start(m):
                big = bigm[:, m, :]
                link(dve.tensor_tensor(big, mxd[:, m, 0, :], mxd[:, m, 1, :], ALU.max))
                link(dve.tensor_tensor(big, big, mxd[:, m, 2, :], ALU.max))
                dve.tensor_tensor(wd[:, m], mxd[:, m], big.unsqueeze(1).broadcast_to([P, DG, 4]), ALU.subtract).then_inc(wmx, 1)

            def weights(m):
                big = bigm[:, m, :]
                dve.wait_ge(wexp, m + 1)
                link(dve.tensor_tensor(dend[:, m], dend[:, m], wd[:, m], ALU.mult))
                link(dve.tensor_tensor(big, dend[:, m, 0, :], dend[:, m, 1, :], ALU.add))
                link(dve.tensor_tensor(big, big, dend[:, m, 2, :], ALU.add))
                link(dve.reciprocal(big, big))
                link(dve.tensor_tensor(wd[:, m], wd[:, m], big.unsqueeze(1).broadcast_to([P, DG, 4]), ALU.mult))

            def og4(m, g):
                return og[:, m, g, :, :].rearrange("p (b a) d -> p b a d", b=2)

            def drain(g, i, o):
                if i < AG_DIL:
                    return normalize(g, i, o)
                m, k = divmod(i - AG_DIL, DG)
                if k == 0:
                    dve.tensor_copy(g["out"], o).then_inc(o_ready, 1)
                    weights_start(m)
                    return
                dve.tensor_tensor(g["out"], o, bc(wd[:, m, k, :], 64), ALU.mult).then_inc(o_ready, 1)
                cat = ocat[:, m, 512:768].rearrange("p (a b d) -> p b a d", a=2, b=2)
                if k == 1:
                    first = og[:, m, 0, :, :]
                    link(dve.tensor_tensor(first, first, bc(wd[:, m, 0, :], 64), ALU.mult))
                    dve.wait_ge(o_ready, i + 1)
                    link(dve.tensor_tensor(cat, og4(m, 0), og4(m, 1), ALU.add))
                else:
                    dve.wait_ge(o_ready, i + 1)
                    ins = dve.tensor_tensor(cat, cat, og4(m, 2), ALU.add)
                    if m == M - 1:
                        ins.then_inc(src_ready, 1)

            dve.wait_ge(dilb_in, 16)
            attention(B, "mla", mla_groups() + dil_groups(), AG_MLA, drain,
                      before=lambda i: weights((i - AG_DIL) // DG) if i >= AG_DIL and (i - AG_DIL) % DG == 1 else None)
            square_T(B, B.plan.tb["ocat"], 3, oTl, oTh)
            out_steps(B, "wout", 1)
            norm_T(B, "n1")
            ffn(B, "f0", 0, 1.0, 2)
            after_ffn_T(B, "n2", "gqkv")
            assert powers[0] == POWERS_GQA
            dve.wait_ge(gtab_ready, 1)

            def mean_squares(u):
                dve.wait_ge(drain_act, B.drained(B.plan.step["gqkv"] + u + 1, "A"))
                c = slice(8 * u, 8 * u + 8)
                link(dve.tensor_reduce(gms[:, c], gsq[u % 2].rearrange("p m (h d) -> p (m h) d", d=64), AX_X, ALU.add))
                dve.tensor_scalar(gms[:, c], gms[:, c], 1.0 / 64, EPS, ALU.mult, ALU.add).then_inc(ms_ready, 1)
                powers[0] = powers[0] + 1

            def turn(u):
                dve.wait_ge(gn_ready, u + 1)
                if u:
                    dve.wait_ge(gr_dve, u)
                xab = gn[u % 2].rearrange("p m (g x f) -> p m g x f", g=8, x=2)
                for x_ in range(2):
                    ins = dve.tensor_tensor(gtv[:, x_], xab[:, :, :, x_, :], gtab[u == 0][:, x_], ALU.mult)
                link(ins)
                c = 1024 if u == 0 else 256 * (u - 1)
                dve.tensor_tensor(gr[:, :, c:c + 256].rearrange("p m (g x f) -> p m g x f", g=8, x=2)[:, :, :, 0, :],
                                  gtv[:, 0], gtv[:, 1], ALU.subtract).then_inc(gr_dve, 1)

            tb = B.plan.tb["gqk"]

            def turned_T(u):
                plain_T(B, tb + u, gqT[:, 2 * u - 2:2 * u, :] if u else gkT)

            for i in range(6):
                if i >= 1:
                    mean_squares(i - 1)
                if i >= 2:
                    turn(i - 2)
                if i == 5:
                    for u in range(3):
                        turned_T(u)
                    turn(4)
                ahead(B, "gqkv", i)
            turned_T(3)
            turned_T(4)
            attention(B, "gqa", gqa_groups(), AG_GQA, normalize)
            square_T(B, B.plan.tb["go"], 4, yl, yh)
            out_steps(B, "gwo", 3)
            norm_T(B, "n3")
            ffn(B, "f1", 1, 1.0, 4, x)
            dve.wait_ge(y_ready, 20)
            dve.sem_inc(x_ready, 4)
            norm(5, gain5_in, 16, gbc5)
            dve.wait_ge(y_ready, 24)
            dve.sem_inc(layer_done, 1)

            def layer(l):
                B = Numbers(l)
                plan = B.plan
                after_ffn_T(B, "n4", "fa")
                ffn(B, "fa", 2 + 2 * l, 0.5, 6 + 3 * l)
                after_ffn_T(B, "n5", "win")
                dve.wait_ge(lay_in, 64 * (l + 1))
                dve.wait_ge(tab2_in, 16)
                w0 = plan.step["win"]
                dve.tensor_scalar(hmb, mb, 0.5, None, ALU.mult)
                for i in range(17):
                    ahead(B, "win", i)
                    o = bank2(i % 2)
                    if WIN_DRAINS[i] == "D":
                        stepped(B, "win", i)
                        if i in (0, 1):
                            ins = dve.tensor_copy(kvd[:, i], o)
                        elif i == 6:
                            ins = dve.tensor_copy(rqk[:, 0:2, :], o)
                        elif i == 7:
                            ins = dve.tensor_scalar(rqk[:, 2:4, :], o, 0.125, None, ALU.mult)
                        elif i in (12, 13):
                            ins = dve.tensor_scalar(nq[:, 2 * i - 24:2 * i - 22, :], o, 0.125, None, ALU.mult)
                        elif i == 14:
                            ins = dve.tensor_copy(nk, o)
                        else:
                            ins = dve.tensor_copy(nv, o)
                        ins.then_inc(drain_dve, 1)
                    if i == 1:
                        dve.wait_ge(drain_dve, B.drained(w0 + 2, "D"))
                        for kv in range(2):
                            for g in range(2):
                                for par in range(2):
                                    r = slice(64 * par, 64 * par + 64)
                                    k3 = kvd[r, kv, g, :].rearrange("p (n l b) -> p l n b", l=8, b=2)[:, :, :, par]
                                    for hf in range(2):
                                        ins = dve.tensor_tensor(blk[r, kv, 8 * hf:8 * hf + 8, g, :], k3[:, :, hf:hf + NCMP],
                                                                bc(cpos[r, kv, 8 * hf:8 * hf + 8], NCMP), ALU.add)
                        ins.then_inc(blk_ready, 1)
                    if i == 5:
                        dve.wait_ge(drain_act, B.drained(w0 + 4, "A"))
                        for m in range(M):
                            ins = dve.bn_stats(st[:, m, :], vA[:, m, :])
                        link(ins)
                        pause()
                        for m in range(M):
                            ins = dve.bn_aggr(mv[:, m, :], st[:, m, :])
                        link(ins)
                        power(dve.tensor_scalar(ms[:, 0:2], mv[:, 0:2, 1], EPS, None, ALU.add))
                        for m in range(M):
                            ins = dve.tensor_scalar(vA[:, m, :], vA[:, m, :], mv[:, m, 0:1], rstd[:, m:m + 1], ALU.subtract, ALU.mult)
                        link(ins)
                        for c0, op in ((0, ALU.mult), (512, ALU.add)):
                            for m in range(M):
                                ins = dve.tensor_tensor(vA[:, m, :], vA[:, m, :], lng[:, c0:c0 + 512], op)
                            link(ins)
                        dve.tensor_tensor(gmws, gmws, trilT.unsqueeze(1).broadcast_to([P, 4, P]), ALU.mult).then_inc(gm_ready, 1)
                    if i == 6:
                        dve.wait_ge(hidt_done, l + 1)
                        dve.tensor_copy(hid[:, 0, :], pb[5][:, 0:30])
                        dve.tensor_copy(hidx, pb[5][:, 30:60].rearrange("p (g n) -> p g n", g=2).unsqueeze(2).broadcast_to([P, 2, 4, NCMP])).then_inc(hidx_ready, 1)
                    if i == 8:
                        dve.wait_ge(kc_done, l + 1)
                        dve.tensor_copy(kcs, pb[3][:, 0:NCMP])
                        dve.tensor_copy(bdrow, pb[4][0:120, 0:64]).then_inc(kc_ready, 1)
                dve.wait_ge(gm_done, l + 1)
                dve.wait_ge(drain_act, B.drained(w0 + 6, "A"))
                for m in range(M):
                    for g in range(4):
                        c = slice(g * P, g * P + P)
                        ins = dve.scalar_tensor_tensor(out=uA[:, m, c], in0=pb[4 + m][:, c], scalar=gmbs[:, g:g + 1], in1=uA[:, m, c],
                                                       op0=ALU.add, op1=ALU.mult)
                ins.then_inc(ya_ready, 1)
                for h in range(HR):
                    dve.wait_ge(rs_done, HR * l + h + 1)
                    if h >= 2:
                        dve.wait_ge(ro_done, HR * l + h - 1)
                    dve.tensor_tensor(rs[h % 2][:, 0:S], pb[2 + h % 2][:, 0:S], rdec[:, h, :], ALU.mult)
                    dve.tensor_tensor(rs[h % 2][:, S:S + P], pb[2 + h % 2][:, S:S + P], rdec[:, h, 0:P], ALU.mult).then_inc(rs_ready, 1)
                cden = st.rearrange("p a b -> p (a b)")[:, 0:16].rearrange("p (m h) -> p m h", m=M)
                cmx = st.rearrange("p a b -> p (a b)")[:, 16:32].rearrange("p (m h) -> p m h", m=M)
                cp = [P2[0][:, m, 0:120].rearrange("p (h n) -> p h n", h=HN) for m in range(M)]
                for m in range(M):
                    dve.wait_ge(cs_done, 4 * l + 2 * m + 2)
                    link(dve.tensor_tensor(cp[m], pb[2 + m][:, 0:120].rearrange("p (h n) -> p h n", h=HN), cbias[:, m], ALU.add))
                    link(dve.tensor_reduce(cmx[:, m, :], cp[m], AX_X, ALU.max))
                    link(dve.tensor_scalar(cmx[:, m, :], cmx[:, m, :], -1e29, None, ALU.max))
                    ins = dve.tensor_tensor(cp[m], cp[m], bc(cmx[:, m, :], NCMP), ALU.subtract)
                    ins.then_inc(cs_ready, 1)
                    if m == 0:
                        ahead(B, "gates", 0)
                dve.wait_ge(kc_ready, l + 1)
                dve.tensor_tensor(bd[0:120], bdrow.unsqueeze(1).broadcast_to([120, HN, 64]), bc(blockm[0:120, :], 64), ALU.mult)
                dve.wait_ge(cs_ready, M * (l + 1))
                for m in range(M):
                    for h in range(HR):
                        ins = dve.bn_stats(st[:, 4 * m + h, :], pb[4 + m][:, h * P:h * P + P])
                link(ins)
                pause()
                for j in range(8):
                    ins = dve.bn_aggr(mv[:, j, :], st[:, j, :])
                link(ins)
                power(dve.tensor_scalar(ms[:, 0:8], mv[:, :, 1], EPS, None, ALU.add))
                for m in range(M):
                    for h in range(HR):
                        j = 4 * m + h
                        ins = dve.tensor_scalar(rnorm[:, m, h * P:h * P + P], pb[4 + m][:, h * P:h * P + P], mv[:, j, 0:1], rstd[:, j:j + 1],
                                                ALU.subtract, ALU.mult)
                ins.then_inc(ro_used, 1)
                ahead(B, "gates", 1)
                dve.wait_ge(drain_act, B.drained(w0 + 17, "A"))
                ngf = ng.rearrange("p m g r b -> p (m g r b)")
                link(dve.tensor_scalar(ngf, ngf, 1.0, None, ALU.add))
                link(dve.reciprocal(ngf, ngf))
                tb = plan.tb["cmp"]
                dve.wait_ge(tb_done, B.tb0 + tb + 2)
                dve.tensor_copy(PT2[0][0:120, 1, 0, :], pb[B.bank(tb + 1)][0:120, 0:P]).then_inc(tb_dve, 1)
                for m in range(M):
                    dve.wait_ge(ce_ready, M * l + m + 1)
                    link(dve.tensor_reduce(cden[:, m, :], cp[m], AX_X, ALU.add))
                    link(dve.tensor_scalar(cden[:, m, :], cden[:, m, :], 1e-30, None, ALU.max))
                    link(dve.reciprocal(cden[:, m, :], cden[:, m, :]))
                    link(dve.tensor_tensor(cden[:, m, :].rearrange("p (g r) -> p g r", g=2), cden[:, m, :].rearrange("p (g r) -> p g r", g=2),
                                           ng[:, m, :, :, 0], ALU.mult))
                square_T(B, plan.tb["ya"], 2, aTl, aTh)
                for m in range(M):
                    dve.wait_ge(co_done, M * l + m + 1)
                    dve.tensor_tensor(vA[:, m, :].rearrange("p (h d) -> p h d", h=HN), pb[4 + m].rearrange("p (h d) -> p h d", h=HN),
                                      bc(cden[:, m, :], 64), ALU.mult).then_inc(yc_ready, 1)
                dve.wait_ge(yc_ready, 3 * l + 2)

                def gated(g, i, o):
                    link(dve.reciprocal(rec, den[:, i % 4, :]))
                    link(dve.tensor_tensor(rec, rec, g["gate"], ALU.mult))
                    link(dve.tensor_tensor(og2, o, bc(rec, 64), ALU.mult))
                    link(dve.tensor_tensor(g["out"], g["out"], og2, ALU.add))
                    dve.sem_inc(o_ready, 1)

                attention(B, "nsa", nsa_groups(), AG_NSA + 8 * l, gated,
                          lambda i: ahead(B, "gates", 2 + i))
                dve.sem_inc(yc_ready, 1)
                tb = plan.tb["y"]
                square_T(B, tb, 2, bTl, bTh)
                b0 = plan.step["branch"]

                def mix_low(j):
                    dve.wait_ge(mixh_made, 4 * l + j + 1)
                    c = slice(2 * j, 2 * j + 2)
                    dve.scalar_tensor_tensor(out=yl[:, c, :], in0=mix[:, c, :], scalar=0.5, in1=yh[:, c, :].bitcast(F32),
                                             op0=ALU.mult, op1=ALU.subtract).then_inc(mix_ready, 1)

                for i in range(12):
                    if i < 10:
                        ahead(B, "branch", i, 2)
                    if i == 0:
                        square_T(B, tb + 2, 2, cTl, cTh)
                    if i == 11:
                        mix_low(2)
                    stepped(B, "branch", i)
                    if i == 0:
                        dve.wait_ge(drain_act, B.drained(plan.step["gates"] + 12, "A"))
                    j = i % 4
                    c, gs = slice(2 * j, 2 * j + 2), gates[:, 2 * i:2 * i + 2, :]
                    if i < 4:
                        dve.scalar_tensor_tensor(out=mix[:, c, :], in0=gs, scalar=1.0, in1=bank2(i % 2), op0=ALU.add, op1=ALU.mult).then_inc(drain_dve, 1)
                    else:
                        dve.scalar_tensor_tensor(out=gs, in0=gs, scalar=1.0, in1=bank2(i % 2), op0=ALU.add, op1=ALU.mult).then_inc(drain_dve, 1)
                        if i >= 8:
                            if i in (9, 10):
                                mix_low(i - 9)
                            dve.wait_ge(drain_dve, B.drained(b0 + i + 1, "D"))
                            dve.wait_ge(mix_pool, 4 * l + j + 1)
                            dve.tensor_tensor(mix[:, c, :], mix[:, c, :], gs, ALU.add).then_inc(mix_sum, 1)
                mix_low(3)
                ahead(B, "branch", 10, 2)
                dve.sem_inc(layer_done, 1)
                out_steps(B, "wo", 7 + 3 * l)
                norm_T(B, "n6")
                ffn(B, "fb", 3 + 2 * l, 0.5, 8 + 3 * l)

            before = powers[0]
            with nc.vector.Fori(0, LAYERS) as l:
                links[:] = dve_link[1], LINKS * l
                powers[0] = before + POWERS * l
                counted[0] = 0
                layer(l)
                assert counted[0] == LINKS, counted
            links[:] = dve_link[1], LINKS * LAYERS
            powers[0] = before + POWERS * LAYERS
            dve.wait_ge(y_ready, 48)
            dve.sem_inc(out_ready, 1)
    return nc


def weight_tile(parts, k_rows):
    w = np.concatenate(parts, 1)
    kc = k_rows // P
    t = w.reshape(kc, P, -1).transpose(1, 0, 2).reshape(P, -1)
    out = np.zeros((P, TILE), w.dtype)
    out[:, :t.shape[1]] = t
    return out


def weight_stream(a):
    tiles = []

    def cols(w, starts, n=256):
        for c in starts:
            tiles.append(weight_tile([w[:, c:c + n]], w.shape[0]))

    def ffn(w1, w2):
        def up(j):
            tiles.append(weight_tile([w1[:, P * j:P * j + P], w1[:, FF + P * j:FF + P * j + P]], D))

        def down(i):
            tiles.append(weight_tile([w2[2 * P * i:2 * P * i + 2 * P]], 2 * P))
        up(0)
        up(1)
        for i in range(1, NF // 2):
            up(2 * i)
            up(2 * i + 1)
            down(i - 1)
        down(NF // 2 - 1)

    w = a["w_in_ab"][0]
    cols(w, (0, 256))
    cols(w, (512,))
    cols(w, range(672, 2976, 256))
    w = a["mla_w_uq"][0].reshape(RQ, -1)
    cols(w, (0, 512), 512)
    cols(a["mla_w_ukv"][0].reshape(RKV, -1), (0,), 1024)
    cols(a["w_out_ab"][0], range(0, D, 256))
    ffn(a["ffn_w_in"][0], a["ffn_w_out"][0])
    order = [4 * (2 * (c // 4) + b) + c % 4 for c in range(8) for b in range(2)]
    wq = a["gqa_w_q"][0].reshape(D, H2, 64)[:, order].reshape(D, D)
    cols(a["gqa_w_kv"][0], (0,))
    cols(wq, range(0, D, 256))
    cols(a["gqa_w_kv"][0], (256,))
    cols(a["gqa_w_o"][0].reshape(H2, 64, D)[order].reshape(D, D), range(0, D, 256))
    ffn(a["ffn_w_in"][1], a["ffn_w_out"][1])
    for l in range(LAYERS):
        ffn(a["ffn1_w1_2"][l], a["ffn1_w2_2"][l])
        w = a["w_in_2"][l]

        def part(c, n=64):
            return w[:, c:c + n]
        for c in (3072, 3200):
            tiles.append(weight_tile([part(c), part(c), part(c + 64), part(c + 64)], D))
        cols(w, (512, 768, 0, 256, 1024, 1280, 1536, 1792, 2048, 2304))
        for j in (0, 2):
            tiles.append(weight_tile([part(2560 + 64 * h) for h in (j, j + 4, j + 1, j + 5)], D))
        tiles.append(weight_tile([part(3328, P), part(3584, P)], D))
        tiles.append(weight_tile([part(3456, P), part(3712, P)], D))
        gl = np.zeros((D, 256), w.dtype)
        gl[:, :24] = w[:, 3840:3864]
        tiles.append(weight_tile([gl], D))
        cols(a["w_merge_gate_2"][l], range(0, 3 * D, 256))
        for i in range(3):
            cols(a["w_branch_out_2"][l, i], (0, 512), 512)
        cols(a["w_o_2"][l], range(0, D, 256))
        ffn(a["ffn2_w1_2"][l], a["ffn2_w2_2"][l])
    tiles += [np.zeros((P, TILE), np.float32)] * 2
    assert len(tiles) == TILES
    return np.stack(tiles)


def everywhere(v):
    return np.ascontiguousarray(np.broadcast_to(v.reshape(1, -1), (P, v.size)))


def layer_small(a, l):
    ws = a["gm_ws_2"][l].transpose(2, 0, 1).reshape(P, -1)
    bs = a["gm_bs_2"][l].T
    w2 = a["cmp_w2_2"][l].transpose(1, 0, 2).reshape(P, -1)
    pos = a["cmp_pos_2"][l].reshape(2, 16, P).transpose(2, 0, 1).reshape(P, -1)
    w1 = a["cmp_w1_2"][l].reshape(2, 16, P, P).transpose(2, 0, 1, 3).reshape(P, -1)
    mb = a["b_merge_gate_2"][l].reshape(24, P).T
    return np.concatenate([ws, bs, w2, pos, mb, w1], 1)


def kernel(**inputs):
    import concourse.bacc as _bacc
    from concourse.bass_utils import run_bass_kernel_spmd as _run

    a = {k: np.asarray(v) for k, v in inputs.items()}
    misc, dil, second = tables()
    norms = [a["mix_norm_ab"][0], a["ffn_norm"][0], a["mix_norm_c"][0], a["ffn_norm"][1], a["final_norm"]]
    for l in range(LAYERS):
        norms += [a["ffn1_norm_2"][l], a["mix_norm_2"][l], a["ffn2_norm_2"][l]]
    norms.append(a["final_norm_2"])
    arrays = {
        "stream": weight_stream(a),
        "xin": np.ascontiguousarray(a["x"].reshape(M, P, D).transpose(1, 0, 2)),
        "misc": misc, "dilb": dil, "second": second,
        "gains": np.stack([everywhere(g) for g in norms]),
        "mlag": everywhere(np.concatenate([a["mla_q_norm"][0], a["mla_kv_norm"][0], a["gqa_q_norm"][0], a["gqa_k_norm"][0]])),
        "small": np.stack([layer_small(a, l) for l in range(LAYERS)]),
        "rows": np.stack([everywhere(np.concatenate([a[k][l] for k in ("gm_ln_g_2", "gm_ln_b_2", "ret_gn_g_2", "ret_gn_b_2")]))
                          for l in range(LAYERS)]),
    }
    nc = _bacc.Bacc("TRN2", target_bir_lowering=False, num_devices=1)
    d = {k: nc.dram_tensor(k, v.shape, F32, kind="ExternalInput").ap() for k, v in arrays.items()}
    out = nc.dram_tensor("out", (P, M, D), F32, kind="ExternalOutput").ap()
    build(nc, d["stream"], d["xin"], d["misc"], d["dilb"], d["second"], d["gains"], d["mlag"], d["small"], d["rows"], out)
    r = _run(nc, [arrays], core_ids=[0])
    return np.ascontiguousarray(r.results[0]["out"].transpose(1, 0, 2).reshape(1, S, D))
```
